# Optimizing a Trainium2 kernel written in Bass

```python
import math
import jax, jax.numpy as jnp
from jax import lax
import numpy as np

D_MODEL = 1024
BATCH = 1
SEQ = 256
DEPTH = 2

N_META = 16
CHUNK = 64
Q_BLOCK = 128
FRONT_PAD = Q_BLOCK - N_META
EPS = 1e-6
NEG = -1e30
ROPE_THETA = 10000.0

GROUP_W = D_MODEL // 4
GLA_HEADS = 4
GLA_DK = GROUP_W // GLA_HEADS // 2
GLA_DV = GROUP_W // GLA_HEADS
GLA_GATE_RANK = 16
GLA_TAU = 16.0
RET_HEADS = 4
RET_DK = GROUP_W // RET_HEADS
RET_DV = GROUP_W // RET_HEADS
MLA_HEADS = 4
MLA_Q_RANK = 192
MLA_KV_RANK = 64
MLA_NOPE = 64
MLA_ROPE = 32
MLA_DV = GROUP_W // MLA_HEADS
DIFF_HEADS = 4
DIFF_DK = 32
DIFF_DV = GROUP_W // DIFF_HEADS
D_FF = 2816
N_EXPERTS = 8
TOP_K = 2
D_FF_EXPERT = 3584
N_DENSE = (DEPTH + 1) // 2
N_MOE = DEPTH // 2

SPLIT_SIZES = (
    GLA_HEADS * GLA_DK, GLA_HEADS * GLA_DK, GLA_HEADS * GLA_DV, GLA_GATE_RANK, GLA_HEADS * GLA_DV,
    RET_HEADS * RET_DK, RET_HEADS * RET_DK, RET_HEADS * RET_DV, RET_HEADS * RET_DV,
    MLA_Q_RANK, MLA_KV_RANK, MLA_ROPE,
    DIFF_HEADS * 2 * DIFF_DK, DIFF_HEADS * 2 * DIFF_DK, DIFF_HEADS * DIFF_DV,
)
D_IN = sum(SPLIT_SIZES)

kernel_name = "hybrid_parallel_heads_gla_ret_mla_diff_moe"

def rmsnorm(x, g):
    xf = x.astype(jnp.float32)
    y = xf * lax.rsqrt(jnp.mean(xf * xf, axis=-1, keepdims=True) + EPS)
    return (y * g.astype(jnp.float32)).astype(x.dtype)

def head_groupnorm(x, g):
    xf = x.astype(jnp.float32)
    mu = jnp.mean(xf, axis=-1, keepdims=True)
    xc = xf - mu
    y = xc * lax.rsqrt(jnp.mean(xc * xc, axis=-1, keepdims=True) + EPS)
    return (y * g.astype(jnp.float32)).astype(x.dtype)

def rope(x, pos):
    half = x.shape[-1] // 2
    inv = ROPE_THETA ** (-jnp.arange(half, dtype=jnp.float32) / half)
    ang = pos.astype(jnp.float32)[:, None] * inv[None, :]
    cos, sin = jnp.cos(ang), jnp.sin(ang)
    xf = x.astype(jnp.float32)
    x1, x2 = xf[..., :half], xf[..., half:]
    return jnp.concatenate([x1 * cos - x2 * sin, x1 * sin + x2 * cos], axis=-1).astype(x.dtype)

def to_heads(t, n_heads):
    b, t_len, _ = t.shape
    return t.reshape(b, t_len, n_heads, -1).transpose(0, 2, 1, 3)

def from_heads(t):
    b, h, t_len, d = t.shape
    return t.transpose(0, 2, 1, 3).reshape(b, t_len, h * d)

def chunk_state_scan(decay, update):
    def step(s, inp):
        d, u = inp
        return d[..., None] * s + u, s
    s0 = jnp.zeros(update.shape[1:], jnp.float32)
    _, s_prev = lax.scan(step, s0, (decay, update))
    return s_prev

def gla_chunked(q, k, v, g):
    b, h, t_len, dk = q.shape
    dv = v.shape[-1]
    n = t_len // CHUNK
    q = q.astype(jnp.float32).reshape(b, h, n, CHUNK, dk)
    k = k.astype(jnp.float32).reshape(b, h, n, CHUNK, dk)
    vf = v.astype(jnp.float32).reshape(b, h, n, CHUNK, dv)
    cum = jnp.cumsum(g.astype(jnp.float32).reshape(b, h, n, CHUNK, dk), axis=-2)
    cum_last = cum[..., -1:, :]
    q_t = q * jnp.exp(cum)
    k_t = k * jnp.exp(-cum)
    tri = jnp.tril(jnp.ones((CHUNK, CHUNK), bool))
    a = jnp.where(tri, jnp.einsum('bhncd,bhnsd->bhncs', q_t, k_t), 0.0)
    o_intra = jnp.einsum('bhncs,bhnse->bhnce', a, vf)
    upd = jnp.einsum('bhncd,bhnce->nbhde', k * jnp.exp(cum_last - cum), vf)
    dec = jnp.exp(cum_last[..., 0, :]).transpose(2, 0, 1, 3)
    s_prev = chunk_state_scan(dec, upd)
    o_inter = jnp.einsum('bhncd,nbhde->bhnce', q_t, s_prev)
    return (o_intra + o_inter).reshape(b, h, t_len, dv).astype(v.dtype)

def retention_chunked(q, k, v):
    b, h, t_len, dk = q.shape
    dv = v.shape[-1]
    n = t_len // CHUNK
    lg = jnp.log(1.0 - jnp.exp2(-5.0 - jnp.arange(h, dtype=jnp.float32)))
    idx = jnp.arange(CHUNK, dtype=jnp.float32)
    rel = idx[:, None] - idx[None, :]
    dmask = jnp.where(rel[None] >= 0, jnp.exp(rel[None] * lg[:, None, None]), 0.0)
    qfac = jnp.exp((idx[None, :] + 1.0) * lg[:, None])
    kfac = jnp.exp((CHUNK - 1.0 - idx[None, :]) * lg[:, None])
    q = q.astype(jnp.float32).reshape(b, h, n, CHUNK, dk)
    k = k.astype(jnp.float32).reshape(b, h, n, CHUNK, dk)
    vf = v.astype(jnp.float32).reshape(b, h, n, CHUNK, dv)
    a = jnp.einsum('bhncd,bhnsd->bhncs', q, k) * dmask[None, :, None]
    o_intra = jnp.einsum('bhncs,bhnse->bhnce', a, vf)
    upd = jnp.einsum('bhncd,hc,bhnce->nbhde', k, kfac, vf)
    dec = jnp.broadcast_to(jnp.exp(CHUNK * lg)[None, None, :, None], (n, b, h, dk))
    s_prev = chunk_state_scan(dec, upd)
    o_inter = jnp.einsum('bhncd,hc,nbhde->bhnce', q, qfac, s_prev)
    return (o_intra + o_inter).reshape(b, h, t_len, dv).astype(v.dtype)

def signed_softmax_attention(q, k, v, valid, scale, coef):
    b, h, m, t_len, dk = q.shape
    dv = v.shape[-1]
    nb = t_len // Q_BLOCK
    qb = q.reshape(b, h, m, nb, Q_BLOCK, dk).transpose(3, 0, 1, 2, 4, 5)
    kpos = jnp.arange(t_len)
    coef = coef.astype(jnp.float32)

    def block(args):
        qi, i = args
        qpos = i * Q_BLOCK + jnp.arange(Q_BLOCK)
        mask = (kpos[None, :] <= qpos[:, None]) & valid[None, :]
        s = jnp.einsum('bhmqd,bhmkd->bhmqk', qi, k).astype(jnp.float32) * scale
        p = jax.nn.softmax(jnp.where(mask, s, NEG), axis=-1)
        w = jnp.einsum('bhmqk,m->bhqk', p, coef)
        return jnp.einsum('bhqk,bhkd->bhqd', w.astype(v.dtype), v)

    out = lax.map(block, (qb, jnp.arange(nb)))
    return out.transpose(1, 2, 0, 3, 4).reshape(b, h, t_len, dv)

def hybrid_mixer(hn, li, w_in, gla_w_gate, gla_b_gate, gla_norm, ret_norm,
                 mla_q_norm, mla_w_uq, mla_kv_norm, mla_w_ukv, diff_lambda, diff_norm, w_out):
    b, t_len, _ = hn.shape
    tp = t_len + FRONT_PAD
    proj = jnp.pad(hn @ w_in, ((0, 0), (FRONT_PAD, 0), (0, 0)))
    offs = [int(o) for o in np.cumsum(SPLIT_SIZES)[:-1]]
    (a_q, a_k, a_v, a_lr, a_og, r_q, r_k, r_v, r_og,
     c_cq, c_ckv, c_kpe, d_q, d_k, d_v) = jnp.split(proj, offs, axis=-1)
    tpos = jnp.arange(tp)
    valid = tpos >= FRONT_PAD
    pos = tpos - FRONT_PAD
    kmask = valid[None, None, :, None].astype(proj.dtype)

    g = jax.nn.log_sigmoid((a_lr @ gla_w_gate + gla_b_gate).astype(jnp.float32)) / GLA_TAU
    g = jnp.where(valid[None, :, None], g, 0.0)
    o_a = gla_chunked(to_heads(a_q, GLA_HEADS) * (GLA_DK ** -0.5), to_heads(a_k, GLA_HEADS) * kmask,
                      to_heads(a_v, GLA_HEADS), to_heads(g, GLA_HEADS))
    o_a = from_heads(rmsnorm(o_a, gla_norm)) * jax.nn.silu(a_og)

    rq = rope(to_heads(r_q, RET_HEADS), pos)
    rk = rope(to_heads(r_k, RET_HEADS), pos) * (RET_DK ** -0.5) * kmask
    o_b = retention_chunked(rq, rk, to_heads(r_v, RET_HEADS))
    o_b = from_heads(head_groupnorm(o_b, ret_norm)) * jax.nn.silu(r_og)

    cq = (rmsnorm(c_cq, mla_q_norm) @ mla_w_uq).reshape(b, tp, MLA_HEADS, MLA_NOPE + MLA_ROPE).transpose(0, 2, 1, 3)
    q_c = jnp.concatenate([cq[..., :MLA_NOPE], rope(cq[..., MLA_NOPE:], pos)], axis=-1)
    kv = (rmsnorm(c_ckv, mla_kv_norm) @ mla_w_ukv).reshape(b, tp, MLA_HEADS, MLA_NOPE + MLA_DV).transpose(0, 2, 1, 3)
    k_pe = jnp.broadcast_to(rope(c_kpe[:, None], pos), (b, MLA_HEADS, tp, MLA_ROPE))
    k_c = jnp.concatenate([kv[..., :MLA_NOPE], k_pe], axis=-1)
    o_c = signed_softmax_attention(q_c[:, :, None], k_c[:, :, None], kv[..., MLA_NOPE:], valid,
                                   (MLA_NOPE + MLA_ROPE) ** -0.5, jnp.ones((1,), jnp.float32))
    o_c = from_heads(o_c)

    lam_init = 0.8 - 0.6 * math.exp(-0.3 * li)
    lv = diff_lambda.astype(jnp.float32)
    lam = jnp.exp(jnp.sum(lv[0] * lv[1])) - jnp.exp(jnp.sum(lv[2] * lv[3])) + lam_init
    qd = d_q.reshape(b, tp, DIFF_HEADS, 2, DIFF_DK).transpose(0, 2, 3, 1, 4)
    kd = d_k.reshape(b, tp, DIFF_HEADS, 2, DIFF_DK).transpose(0, 2, 3, 1, 4)
    o_d = signed_softmax_attention(qd, kd, to_heads(d_v, DIFF_HEADS), valid, DIFF_DK ** -0.5,
                                   jnp.stack([jnp.ones((), jnp.float32), -lam]))
    o_d = from_heads(rmsnorm(o_d, diff_norm)) * (1.0 - lam_init)

    o = jnp.concatenate([o_a, o_b, o_c, o_d], axis=-1)[:, FRONT_PAD:]
    return o @ w_out

def swiglu(h, wg, wu, wd):
    return (jax.nn.silu(h @ wg) * (h @ wu)) @ wd

def moe_swiglu(h, router, wg, wu, wd):
    logits = (h @ router).astype(jnp.float32)
    top_v, top_i = lax.top_k(logits, TOP_K)
    top_w = jax.nn.softmax(top_v, axis=-1)
    gates = jnp.sum(jax.nn.one_hot(top_i, N_EXPERTS, dtype=jnp.float32) * top_w[..., None], axis=-2)
    out = jnp.zeros_like(h)
    for e in range(N_EXPERTS):
        out = out + gates[..., e:e + 1].astype(h.dtype) * swiglu(h, wg[e], wu[e], wd[e])
    return out

def setup_inputs(seed: int = 0) -> dict:
    key = jax.random.key(seed)
    ks = jax.random.split(key, 32)
    f32 = jnp.float32

    def nrm(k, shape, fan_in):
        return jax.random.normal(k, shape, f32) * (fan_in ** -0.5)

    def gain(k, shape):
        return 1.0 + 0.01 * jax.random.normal(k, shape, f32)

    return {
        "x": jax.random.normal(ks[0], (BATCH, SEQ, D_MODEL), f32),
        "meta_tokens": jax.random.normal(ks[1], (N_META, D_MODEL), f32),
        "attn_norm": gain(ks[2], (DEPTH, D_MODEL)),
        "w_in": nrm(ks[3], (DEPTH, D_MODEL, D_IN), D_MODEL),
        "gla_w_gate": nrm(ks[4], (DEPTH, GLA_GATE_RANK, GLA_HEADS * GLA_DK), GLA_GATE_RANK),
        "gla_b_gate": 0.01 * jax.random.normal(ks[5], (DEPTH, GLA_HEADS * GLA_DK), f32),
        "gla_norm": gain(ks[6], (DEPTH, GLA_DV)),
        "ret_norm": gain(ks[7], (DEPTH, RET_DV)),
        "mla_q_norm": gain(ks[8], (DEPTH, MLA_Q_RANK)),
        "mla_w_uq": nrm(ks[9], (DEPTH, MLA_Q_RANK, MLA_HEADS * (MLA_NOPE + MLA_ROPE)), MLA_Q_RANK),
        "mla_kv_norm": gain(ks[10], (DEPTH, MLA_KV_RANK)),
        "mla_w_ukv": nrm(ks[11], (DEPTH, MLA_KV_RANK, MLA_HEADS * (MLA_NOPE + MLA_DV)), MLA_KV_RANK),
        "diff_lambda": 0.1 * jax.random.normal(ks[12], (DEPTH, 4, DIFF_DK), f32),
        "diff_norm": gain(ks[13], (DEPTH, DIFF_DV)),
        "w_out": nrm(ks[14], (DEPTH, D_MODEL, D_MODEL), D_MODEL),
        "ffn_norm": gain(ks[15], (DEPTH, D_MODEL)),
        "ffn_w_gate": nrm(ks[16], (N_DENSE, D_MODEL, D_FF), D_MODEL),
        "ffn_w_up": nrm(ks[17], (N_DENSE, D_MODEL, D_FF), D_MODEL),
        "ffn_w_down": nrm(ks[18], (N_DENSE, D_FF, D_MODEL), D_FF),
        "moe_router": nrm(ks[19], (N_MOE, D_MODEL, N_EXPERTS), D_MODEL),
        "moe_w_gate": nrm(ks[20], (N_MOE, N_EXPERTS, D_MODEL, D_FF_EXPERT), D_MODEL),
        "moe_w_up": nrm(ks[21], (N_MOE, N_EXPERTS, D_MODEL, D_FF_EXPERT), D_MODEL),
        "moe_w_down": nrm(ks[22], (N_MOE, N_EXPERTS, D_FF_EXPERT, D_MODEL), D_FF_EXPERT),
        "final_norm": gain(ks[23], (D_MODEL,)),
    }

def reference(x, meta_tokens, attn_norm, w_in, gla_w_gate, gla_b_gate, gla_norm, ret_norm,
              mla_q_norm, mla_w_uq, mla_kv_norm, mla_w_ukv, diff_lambda, diff_norm, w_out,
              ffn_norm, ffn_w_gate, ffn_w_up, ffn_w_down, moe_router, moe_w_gate, moe_w_up,
              moe_w_down, final_norm):
    b = x.shape[0]
    meta = jnp.broadcast_to(meta_tokens[None].astype(x.dtype), (b, N_META, x.shape[-1]))
    h = jnp.concatenate([meta, x], axis=1)
    for li in range(DEPTH):
        h = h + hybrid_mixer(rmsnorm(h, attn_norm[li]), li, w_in[li], gla_w_gate[li], gla_b_gate[li],
                             gla_norm[li], ret_norm[li], mla_q_norm[li], mla_w_uq[li], mla_kv_norm[li],
                             mla_w_ukv[li], diff_lambda[li], diff_norm[li], w_out[li])
        hn = rmsnorm(h, ffn_norm[li])
        j = li // 2
        if li % 2 == 0:
            h = h + swiglu(hn, ffn_w_gate[j], ffn_w_up[j], ffn_w_down[j])
        else:
            h = h + moe_swiglu(hn, moe_router[j], moe_w_gate[j], moe_w_up[j], moe_w_down[j])
    h = rmsnorm(h, final_norm)
    return h[:, N_META:]


_drawn_inputs = setup_inputs


def setup_inputs(seed=0):
    import zlib

    import numpy as np

    out = dict(_drawn_inputs(seed))
    spreads = {}
    factors = {'gla_b_gate': 8.0,
     'gla_norm': 21.474,
     'ret_norm': 17.973,
     'mla_q_norm': 5.386,
     'mla_kv_norm': 8.0,
     'diff_norm': 15.238,
     'final_norm': 34.108,
     'ffn_norm': 6.013}
    for name, (base, spread) in spreads.items():
        noise = np.random.default_rng([zlib.crc32(name.encode()), seed]).standard_normal(out[name].shape)
        drawn = base * np.exp(spread * noise) if base else spread * noise
        out[name] = __import__('jax').numpy.asarray(drawn.astype(out[name].dtype))
    for name, factor in factors.items():
        out[name] = (out[name] * factor).astype(out[name].dtype)
    return out
```

```python
from contextlib import ExitStack

import numpy as np
import concourse.bass as bass
from concourse import mybir

F32 = mybir.dt.float32
I32 = mybir.dt.int32
ALU = mybir.AluOpType
ACT = mybir.ActivationFunctionType
AX = mybir.AxisListType

P = 128
D = 1024
KD = D // P
META = 16
SEQ = 256
T = META + SEQ
LAYERS = 2
EPS = 1e-6
NEG = -1e30
H = 4
DV = 64
GLA_DK = 32
GLA_TAU = 16.0
RET_DK = 64
NOPE, ROPE = 64, 32
MLA_DK = NOPE + ROPE
Q_RANK = 192
DIFF_DK = 32
CHUNK = 64
D_FF = 2816
F_EXP = 3584
EXPERTS = 8
FC = 512
RING = 7
SLOT = KD * FC
OVER = (2 * SEQ) // (P + 1)
ITEMS = EXPERTS + OVER

WIDE = [slice(0, 128), slice(16, 144), slice(144, 272)]
ROWS = [META, P, P]

IN_LOADS = [
    (0, 512, [(0, 0, 128, 0), (1, 128, 128, 0), (2, 256, 128, 0), (3, 384, 128, 0)]),
    (512, 272, [(4, 0, 16, 0), (5, 16, 128, 0), (6, 144, 128, 0)]),
    (784, 512, [(7, 0, 128, 0), (8, 128, 128, 0), (9, 256, 128, 0), (10, 384, 128, 0)]),
    (1296, 512, [(11, 0, 128, 0), (12, 128, 128, 0), (13, 256, 128, 0), (14, 384, 128, 0)]),
    (1808, 288, [(15, 0, 128, 0), (16, 128, 128, 0), (17, 256, 32, 64)]),
    (2096, 512, [(18, 0, 128, 0), (19, 128, 128, 0), (20, 256, 128, 0), (21, 384, 128, 0)]),
    (2608, 256, [(22, 0, 128, 0), (23, 128, 128, 0)]),
]
AQ, AK, AV, ALR, AOG, RQ, RK, RV, ROG, CQ, CKV, KPE, DQ, DK, DVT = 0, 1, 2, 4, 5, 7, 9, 11, 13, 15, 16, 17, 18, 20, 22
TILES = 24
FF_GROUPS = [(c * FC, min(FC, D_FF - c * FC)) for c in range(-(-D_FF // FC))]
FT = D_FF // P
DOWN_TILES = [min(4, FT - 4 * j) for j in range(-(-FT // 4))]
N_MAPS = 12
DIFF_MAPS = 8


def constants():
    parts, at = [], {}

    def put(name, a):
        full = np.zeros((P, a.shape[1]), np.float32)
        full[: a.shape[0]] = a
        at[name] = (sum(x.shape[1] for x in parts), a.shape[1])
        parts.append(full)

    p = np.arange(P)
    put("ident", np.eye(P))
    put("ones", np.ones((P, P)))
    half = RET_DK // 2
    swap = np.zeros((P, P))
    for m in range(P):
        if m % RET_DK < half:
            swap[m + half, m] = -1.0
        else:
            swap[m - half, m] = 1.0
    put("swap_ret", swap)
    half = ROPE // 2
    swap = np.zeros((P, ROPE))
    for m in range(ROPE):
        if m < half:
            swap[NOPE + m + half, m] = -1.0
        else:
            swap[NOPE + m - half, m] = 1.0
    put("swap_mla", swap)
    same = (p[:, None] // CHUNK == p[None, :] // CHUNK) & (p[:, None] <= p[None, :])
    put("cum", same / GLA_TAU)
    put("intra", same * 1.0)
    put("block", (p[:, None] // GLA_DK == np.arange(H * DV)[None, :] // DV) * 1.0)
    lg = np.log(1.0 - 2.0 ** (-5.0 - np.arange(H)))
    rel = np.arange(T)[None, :] - p[:, None]
    decay = [np.where(rel >= 0, np.exp(np.maximum(rel, 0) * lg[h]), 0.0) * RET_DK**-0.5 for h in range(H)]
    put("decay", np.concatenate(decay, axis=1))
    put("mask", np.where(np.arange(T)[None, :] <= META + P + p[:, None], 0.0, NEG))
    inv = 10000.0 ** (-(p % (RET_DK // 2)) / (RET_DK // 2))
    ang = np.arange(T)[None, :] * inv[:, None]
    put("cos_ret", np.cos(ang))
    put("sin_ret", np.sin(ang))
    inv = 10000.0 ** (-(p % (ROPE // 2)) / (ROPE // 2))
    ang = np.arange(T)[None, :] * inv[:, None]
    put("cos_mla", np.cos(ang))
    put("sin_mla", np.sin(ang))
    put("iota", np.broadcast_to(p[None, :], (P, P)))
    put("upper", (p[:, None] <= p[None, :]) * 1.0)
    e = np.arange(EXPERTS)
    put("index", np.broadcast_to(np.tile(e, 2)[None, :], (P, 2 * EXPERTS)))
    put("before", np.broadcast_to((e[None, :] < e[:, None]).reshape(1, -1), (P, EXPERTS**2)))
    return np.ascontiguousarray(np.concatenate(parts, axis=1).astype(np.float32)), at


class Results:

    def __init__(self):
        self.at, self.n = {}, [0] * 8

    def add(self, bank, *name):
        assert name not in self.at
        self.at[name] = (bank, self.n[bank])
        self.n[bank] += 1


TURNS = {3: (0, 1), 9: (2, 3)}


def plan_results():
    r = Results()
    turn = [0]

    def spread(*name):
        r.add(3 + turn[0] % 4, *name)
        turn[0] += 1

    r.add(0, "cols")
    for k in range(KD):
        r.add((k + 1) % 8, "x", k)
    for li in range(LAYERS):
        r.add(7, "ms", 2 * li)
        for n, (_, _, tiles) in enumerate(IN_LOADS):
            for t, *_ in tiles:
                r.add(t % 3, "proj", li, t)
            if n == 1:
                spread("gate", li)
                spread("vA", li, 0)
                spread("vB", li, 0)
            if n == 3:
                for j in range(4):
                    spread("swap", li, j)
                spread("vA", li, 1)
                spread("vB", li, 1)
            if n == 4:
                spread("cum", li)
            if n == 5:
                spread("cq", li)
                spread("ckv", li)
                spread("kswap", li)
        spread("vA", li, 2)
        spread("vB", li, 2)
        for h in range(H):
            spread("mq", li, h)
        for h in range(H):
            spread("mk", li, h)
        spread("mvA", li)
        spread("mvB", li)
        spread("kd", li)
        for h in range(H):
            spread("qswap", li, h)
        spread("upA", li)
        spread("upB", li)
        spread("upC", li)
        for h in range(H):
            r.add(h % 3, "gs", li, h)
        r.add(6, "goA", li)
        r.add(7, "goB", li)
        for h in range(H):
            r.add(h % 2, "rsM", li, h)
            r.add(2 + h % 2, "rsX", li, h)
        r.add(6, "roA", li)
        r.add(7, "roB", li)
        for m in range(N_MAPS + 3):
            if m < N_MAPS:
                r.add(m % 3, "sc", li, m)
            if 2 <= m < N_MAPS + 2:
                r.add(3 + m % 2, "ptX", li, m - 2)
                r.add(5, "ptM", li, m - 2)
            if 3 <= m:
                r.add(6 + m % 2, "o", li, m - 3)
            for k in TURNS.get(m, ()):
                r.add(3 + k % 2, "turn", li, k)
        for k in (4, 5, 6, 7):
            r.add(k - 4, "turn", li, k)
        for k in range(KD):
            r.add(k, "wo", li, k)
        r.add(7, "ms", 2 * li + 1)
        if li == 0:
            for f in range(FT):
                r.add(2 * (f % 3), "fg", f)
                r.add(2 * (f % 3) + 1, "fu", f)
            for k in range(KD):
                r.add(6 + k % 2, "fd", k)
    for j in range(4):
        r.add(j, "h_tok", j)
        r.add(4 + j, "hn_tok", j)
    r.add(0, "logits")
    r.add(1, "pos")
    r.add(2, "count")
    base = list(r.n)
    for j in range(2):
        r.add(4 + j, "xg", j)
    r.add(6, "selT")
    for c in range(F_EXP // FC):
        r.add(c % 2, "g", c)
        r.add(2 + c % 2, "u", c)
        r.add(4 + c % 2, "aT", c)
    r.add(6, "y", 0)
    r.add(7, "y", 1)
    for j in range(4):
        r.add(j, "back", j)
    return r, [n - b for n, b in zip(r.n, base)]


def hybrid_trunk(nc, x, meta_tokens, attn_norm, w_in, gla_w_gate, gla_b_gate, gla_norm, ret_norm, mla_q_norm,
                 mla_w_uq, mla_kv_norm, mla_w_ukv, diff_lambda, diff_norm, w_out, ffn_norm, ffn_w_gate,
                 ffn_w_up, ffn_w_down, moe_router, moe_w_gate, moe_w_up, moe_w_down, final_norm, consts,
                 out, const_at):
    plan, PER_ITEM = plan_results()
    NFC = F_EXP // FC

    with ExitStack() as ctx:
        def sb(name, shape, dt=F32):
            return ctx.enter_context(nc.sbuf_tensor(name, shape, dt))

        def sem(name):
            return ctx.enter_context(nc.semaphore(name))

        ring = sb("ring", [P, RING, SLOT])
        hT = sb("hT", [P, KD, T])
        hnT = sb("hnT", [P, KD, T])
        pr = sb("pr", [P, TILES, T])
        oT = sb("oT", [P, KD, T])
        va = sb("va", [P, 3, H * DV])
        vr = sb("vr", [P, 3, H * DV])
        vd = sb("vd", [P, 3, H * DV])
        vm = sb("vm", [P, 3, H * DV])
        pt = sb("pt", [P, 2, 768])
        probs = sb("probs", [P, 3, 432])
        ob = sb("ob", [P, 3, H * DV])
        sq = sb("sq", [P, 3, H * DV])
        cst = sb("cst", [P, consts.shape[1]])
        rows = sb("rows", [48, P])
        cols = sb("cols", [P, 48])
        wuq = sb("wuq", [P, LAYERS, 2, H * MLA_DK])
        wukv = sb("wukv", [P, LAYERS, H * (NOPE + DV)])
        wgate = sb("wgate", [META, LAYERS, P])
        bgate = sb("bgate", [P, LAYERS, P])
        small = sb("small", [P, 160])
        lam = sb("lam", [P, 8])
        half_neg = sb("half_neg", [P, 12])
        rms = sb("rms", [P, 2, T])
        wrout = sb("wrout", [P, KD, EXPERTS])
        ctl = sb("ctl", [1, 4], I32)
        banks = [ctx.enter_context(nc.psum_tensor(f"bank{b}", [P, FC], F32))[:, :] for b in range(8)]

        def const(name):
            a, n = const_at[name]
            return cst[:, a:a + n]

        ident, ones = const("ident"), const("ones")
        decay = const("decay").rearrange("p (h t) -> p h t", h=H)
        mask = const("mask")

        def gain(kind, li, k=0):
            j = {"attn": KD * li + k, "ffn": 16 + KD * li + k, "q": 32 + li, "q_kv": 34 + li,
                 "gla": 36 + li, "ret": 38 + li, "diff": 40 + li}[kind]
            return cols[:, j:j + 1]

        def flat(a): return a.rearrange("p a b -> p (a b)")
        prf, ptf, oTf, hTf = flat(pr[:, :, :]), flat(pt[:, :, :]), flat(oT[:, :, :]), flat(hT[:, :, :])
        x_in = prf[:, 0:2048].rearrange("p (c d) -> p c d", c=2)
        meta_in = prf[0:META, 2048:3072]
        dlam = flat(sq[:, :, :])[:, 0:LAYERS * 4 * DIFF_DK].rearrange("p (l a d) -> p l a d", l=LAYERS, a=4)
        cumT, eq, ek, ekd, kdT, t1, t2 = (oT[:, j, :] for j in range(7))
        gx, gabs = pt[:, 0, 0:384], pt[:, 1, 0:384]
        kd_tok = probs[:, 0, 0:384]
        s01, s23 = flat(pr[:, 2:4, :]), flat(pr[:, 11:13, :])
        state = [s01[:, 0:256], s01[:, 256:512], s23[:, 0:256], s23[:, 256:512]]
        qc, kc = hnT[:, 0:4, :], hnT[:, 4:8, :]
        ob_r = flat(pr[:, 9:12, :])[:, 0:768].rearrange("p (c v) -> p c v", c=3)
        o1, o2, om = va, vr, ob
        neg_max, den, rden = (small[:, 36 * j:36 * j + 36].rearrange("p (m c) -> p m c", c=3) for j in range(3))
        st1, st2, st3, st4 = (small[:, 108 + 12 * j:120 + 12 * j] for j in range(4))
        ffa, ffs = pr[:, 0:FT, :], pt[:, :, 0:T]
        h_tok = prf[:, 0:2048].rearrange("p (c d) -> p c d", c=2)
        hn_tok = prf[:, 2048:4096].rearrange("p (c d) -> p c d", c=2)
        xg = prf[:, 4096:5120]
        ysb = prf[:, 5120:6144]
        act_sb = oTf[:, 0:1024].rearrange("p (b f) -> p b f", b=2)
        actT = oTf[:, 1024:2048].rearrange("p (b f) -> p b f", b=2)
        sg = ptf[:, 0:1024].rearrange("p (b f) -> p b f", b=2)
        sel = vd[:, 0, :].rearrange("p (c s) -> p c s", c=2)
        selT = vm[:, 0, :].rearrange("p (c s) -> p c s", c=2)
        fgain = flat(probs[:, :, :])[:, 0:D]
        route = flat(ob[:, :, :])
        out_sb = hTf[:, 0:2048].rearrange("p (c d) -> p c d", c=2)

        made = [sem(f"made{b}") for b in range(8)]
        taken = [sem(f"taken{b}") for b in range(8)]
        landed = [sem(f"landed{s}") for s in range(RING)]
        consts_in, x_landed, rows_in, params_in, gain_in = (
            sem(n) for n in ("consts_in", "x_landed", "rows_in", "params_in", "gain_in"))
        filled = sem("filled")
        sq_a = sem("sq_a")
        rms_a = sem("rms_a")
        rstd_v = sem("rstd_v")
        hn_v = sem("hn_v")
        lam_v, lam_a = sem("lam_v"), sem("lam_a")
        gate_a = sem("gate_a")
        gla_v = sem("gla_v")
        cum_a = sem("cum_a")
        rot_v = sem("rot_v")
        c_a, c_v = sem("c_a"), sem("c_v")
        rk_v, rq_v = sem("rk_v"), sem("rq_v")
        st_v = sem("st_v")
        map_used = sem("map_used")
        exp_a = sem("exp_a")
        rd_v = sem("rd_v")
        n_v, n_a, n_p = sem("n_v"), sem("n_a"), sem("n_p")
        r_v, r_a = sem("r_v"), sem("r_a")
        sel_v = sem("sel_v")
        down_used = sem("down_used")
        fin_v, fin_a, fin_p = sem("fin_v"), sem("fin_a"), sem("fin_p")
        stored = sem("stored")

        def bank(*name):
            return banks[plan.at[name][0]]

        def room(*name):
            b, n = plan.at[name]
            return taken[b], n

        def done(*name):
            b, n = plan.at[name]
            return made[b], n + 1

        def gone(*name):
            b, n = plan.at[name]
            return taken[b], n + 1

        def made_of(*name):
            return made[plan.at[name][0]]

        def taken_of(*name):
            return taken[plan.at[name][0]]

        def room_i(i, *name):
            b, n = plan.at[name]
            return taken[b], i * PER_ITEM[b] + n

        def done_i(i, *name):
            b, n = plan.at[name]
            return made[b], i * PER_ITEM[b] + (n + 1)

        def gone_i(i, *name):
            b, n = plan.at[name]
            return taken[b], i * PER_ITEM[b] + (n + 1)

        def stream(v, k):
            return [("x", k), ("wo", 0, k), ("fd", k), ("wo", 1, k)][v]

        N_FF = 2 * len(FF_GROUPS) + len(DOWN_TILES)
        PER_LAYER = len(IN_LOADS) + 2
        MOE0 = 2 * PER_LAYER + N_FF
        PER_EXPERT = 3 * NFC
        assert PER_EXPERT % RING == 0
        LAP = 16 * PER_EXPERT // RING

        def load_in(li, n): return li * (PER_LAYER + N_FF) + n
        def load_out(li, n): return load_in(li, len(IN_LOADS) + n)
        def load_ff(n): return PER_LAYER + n

        def at_gate(c): return 3 * c - (1 if c else 0)
        def at_up(c): return at_gate(c) + 1
        def at_down(c): return 3 * c + 4 if c < NFC - 1 else PER_EXPERT - 1

        def slot(n): return n % RING

        def in_slot(n):
            return landed[slot(n)], 16 * (n // RING + 1)

        def in_slot_i(i, n):
            return landed[slot(MOE0 + n)], i * LAP + 16 * ((MOE0 + n) // RING + 1)

        def used_up(n):
            for li in range(LAYERS):
                if load_in(li, 0) <= n < load_out(li, 0):
                    return ("proj", li, IN_LOADS[n - load_in(li, 0)][2][-1][0])
                if load_out(li, 0) <= n < load_out(li, 2):
                    return ("wo", li, KD - 1)
            n -= PER_LAYER
            if n < 2 * len(FF_GROUPS):
                f0, w = FF_GROUPS[n // 2]
                return ("fu" if n % 2 else "fg", (f0 + w) // P - 1)
            return ("fd", KD - 1)

        def used_up_i(i, n):
            c = next(c for c in range(NFC) if n in (at_gate(c), at_up(c), at_down(c)))
            if n == at_down(c):
                return (down_used, i * (NFC - 1) + (c + 1)) if c < NFC - 1 else done_i(i, "y", 1)
            return done_i(i, "g" if n == at_gate(c) else "u", c)

        block = ctx.enter_context(nc.Block())

        @block.sync
        def _(sp):
            sp.dma_start(x_in, x[0].rearrange("(c p) d -> p c d", p=P)).then_inc(x_landed, 16)
            sp.dma_start(meta_in, meta_tokens).then_inc(x_landed, 16)
            sp.dma_start(cst[:, :], consts).then_inc(consts_in, 16)

            def start(n, src, **split):
                if n >= RING:
                    sp.wait_ge(*done(*used_up(n - RING)))
                k, f = split["k"], split["f"]
                sp.dma_start(ring[:, slot(n), 0:k * f].rearrange("p (k f) -> p k f", k=k),
                             src.rearrange("(k p) f -> p k f", p=P)).then_inc(landed[slot(n)], 16)

            for li in range(LAYERS):
                for n, (c0, w, _) in enumerate(IN_LOADS):
                    start(load_in(li, n), w_in[li, :, c0:c0 + w], k=KD, f=w)
                for n in range(2):
                    start(load_out(li, n), w_out[li, 512 * n:512 * n + 512, :], k=4, f=D)
                if li == 0:
                    for c, (f0, w) in enumerate(FF_GROUPS):
                        start(load_ff(2 * c), ffn_w_gate[0, :, f0:f0 + w], k=KD, f=w)
                        start(load_ff(2 * c + 1), ffn_w_up[0, :, f0:f0 + w], k=KD, f=w)
                    for j, nt in enumerate(DOWN_TILES):
                        start(load_ff(2 * len(FF_GROUPS) + j), ffn_w_down[0, FC * j:FC * j + P * nt, :], k=nt, f=D)

            gate_v = moe_w_gate[0].rearrange("e (k p) f -> e p k f", p=P)
            up_v = moe_w_up[0].rearrange("e (k p) f -> e p k f", p=P)
            down_v = moe_w_down[0].rearrange("e (c p j) d -> e p c (j d)", p=P, j=4)

            def item(i, e, first):
                for n in range(PER_EXPERT):
                    c = next(c for c in range(NFC) if n in (at_gate(c), at_up(c), at_down(c)))
                    s = slot(MOE0 + n)
                    if n >= RING:
                        sp.wait_ge(*used_up_i(i, n - RING))
                    elif first:
                        sp.wait_ge(*done(*used_up(MOE0 + n - RING)))
                    else:
                        sp.wait_ge(*used_up_i(i - 1, n - RING + PER_EXPERT))
                    if n == at_down(c):
                        src = down_v[bass.ds(e, 1), :, c, :].rearrange("e p x -> (e p) x")
                        dst = ring[:, s, :]
                    else:
                        view = gate_v if n == at_gate(c) else up_v
                        src = view[bass.ds(e, 1), :, :, FC * c:FC * c + FC].rearrange("e p k f -> (e p) k f")
                        dst = ring[:, s, :].rearrange("p (k f) -> p k f", k=KD)
                    sp.dma_start(dst, src).then_inc(landed[s], 16)

            item(0, 0, True)
            with sp.Fori(1, EXPERTS) as e:
                item(e, e, False)
            sp.dma_start(fgain, final_norm.partition_broadcast(P)).then_inc(gain_in, 16)
            sp.wait_ge(r_v, N_ROUTE)
            n_items = sp.value_load(ctl[0:1, 0:1], min_val=EXPERTS, max_val=ITEMS)
            with sp.Fori(EXPERTS, ITEMS) as i:
                with sp.If(i < n_items):
                    e = sp.value_load(ctl[0:1, bass.ds(i - (EXPERTS - 1), 1)], min_val=0, max_val=EXPERTS - 1)
                    item(i, e, False)
            sp.wait_ge(fin_v, 3)
            sp.dma_start(out[0].rearrange("(c p) d -> p c d", p=P), out_sb).then_inc(stored, 16)
            sp.wait_ge(stored, 16)

        @block.tensor
        def _(pe):
            def mm(o, lhsT, rhs, first, end, **kw):
                return pe.matmul(o, lhsT, rhs, start=first, stop=end, **kw)

            pe.wait_ge(consts_in, 16)
            pe.wait_ge(rows_in, 16 * N_ROWS)
            pe.transpose(bank("cols")[:, 0:48], rows[:, :], ident[0:48, 0:48]).then_inc(made_of("cols"), 1)
            pe.wait_ge(x_landed, 32)
            for k in range(KD):
                b = bank("x", k)
                pe.wait_ge(*room("x", k))
                pe.transpose(b[:, 0:META], meta_in[:, P * k:P * k + P], ident[0:META, 0:META])
                pe.transpose(b[:, WIDE[1]], x_in[:, 0, P * k:P * k + P], ident)
                pe.transpose(b[:, WIDE[2]], x_in[:, 1, P * k:P * k + P], ident).then_inc(made_of("x", k), 1)

            def mean_squares(r):
                pe.wait_ge(*room("ms", r))
                for k in range(KD):
                    pe.wait_ge(sq_a, KD * r + k + 1)
                    i = mm(bank("ms", r)[:, 0:T], ones, hnT[:, k, :], k == 0, k == KD - 1)
                i.then_inc(made_of("ms", r), 1)

            def turn_values(li, tile, n):
                pe.wait_ge(*gone("proj", li, tile))
                pe.wait_ge(*gone("proj", li, tile + 1))
                pe.wait_ge(*room("vA", li, n))
                for c in range(2):
                    for j in range(2):
                        i = pe.transpose(bank("vA", li, n)[:, 256 * c + 128 * j:256 * c + 128 * j + 128],
                                         pr[:, tile + j, WIDE[c]], ident)
                i.then_inc(made_of("vA", li, n), 1)
                pe.wait_ge(*room("vB", li, n))
                for j in range(2):
                    i = pe.transpose(bank("vB", li, n)[:, 128 * j:128 * j + 128], pr[:, tile + j, WIDE[2]], ident)
                i.then_inc(made_of("vB", li, n), 1)

            def turn_output(li, k, src):
                b = bank("turn", li, k)
                f = slice(P * (k % 2), P * (k % 2) + P)
                pe.wait_ge(*room("turn", li, k))
                pe.transpose(b[:, 0:META], src[0:META, 0, f], ident[0:META, 0:META])
                pe.transpose(b[:, WIDE[1]], src[:, 1, f], ident)
                pe.transpose(b[:, WIDE[2]], src[:, 2, f], ident).then_inc(made_of("turn", li, k), 1)

            for li in range(LAYERS):
                mean_squares(2 * li)
                for n, (_, w, tiles) in enumerate(IN_LOADS):
                    m = load_in(li, n)
                    wt = ring[:, slot(m), 0:KD * w].rearrange("p (k f) -> p k f", k=KD)
                    pe.wait_ge(*in_slot(m))
                    for t, c0, wd, p0 in tiles:
                        pe.wait_ge(*room("proj", li, t))
                        for k in range(KD):
                            if t == 0:
                                pe.wait_ge(hn_v, KD * 2 * li + k + 1)
                            i = mm(bank("proj", li, t)[p0:p0 + wd, 0:T], wt[:, k, c0:c0 + wd], hnT[:, k, :],
                                   k == 0, k == KD - 1)
                        i.then_inc(made_of("proj", li, t), 1)
                    if n == 1:
                        pe.wait_ge(*gone("proj", li, ALR))
                        pe.wait_ge(*room("gate", li))
                        for c in range(3):
                            i = mm(bank("gate", li)[:, P * c:P * c + P], pr[0:META, ALR, WIDE[c]], wgate[:, li, :], True, True)
                        i.then_inc(made_of("gate", li), 1)
                        turn_values(li, AV, 0)
                    if n == 3:
                        for j in range(4):
                            pe.wait_ge(*gone("proj", li, RQ + j))
                            pe.wait_ge(*room("swap", li, j))
                            mm(bank("swap", li, j)[:, 0:T], const("swap_ret"), pr[:, RQ + j, :], True, True)\
                                .then_inc(made_of("swap", li, j), 1)
                        turn_values(li, RV, 1)
                    if n == 4:
                        pe.wait_ge(gla_v, 5 * li + 2)
                        pe.wait_ge(*room("cum", li))
                        for c in range(3):
                            a = (0, META, META + P)[c]
                            i = mm(bank("cum", li)[:, a:a + ROWS[c]], gx[0:ROWS[c], P * c:P * c + P],
                                   const("cum")[0:ROWS[c], 0:ROWS[c]], True, True)
                        i.then_inc(made_of("cum", li), 1)
                    if n == 5:
                        pe.wait_ge(c_a, 4 * li + 2)
                        pe.wait_ge(*room("cq", li))
                        mm(bank("cq", li)[:, 0:T], ones, rms[:, 0, :], True, False)
                        mm(bank("cq", li)[:, 0:T], ones[0:64, :], rms[0:64, 1, :], False, True).then_inc(made_of("cq", li), 1)
                        pe.wait_ge(*room("ckv", li))
                        mm(bank("ckv", li)[:, 0:T], ones[64:128, :], rms[64:128, 1, :], True, True).then_inc(made_of("ckv", li), 1)
                        pe.wait_ge(*gone("proj", li, KPE))
                        pe.wait_ge(*room("kswap", li))
                        mm(bank("kswap", li)[64:96, 0:T], const("swap_mla")[64:96, :], pr[64:96, KPE, :], True, True)\
                            .then_inc(made_of("kswap", li), 1)
                turn_values(li, DVT, 2)

                pe.wait_ge(params_in, 16 * N_PARAMS)
                pe.wait_ge(c_v, 5 * li + 4)
                for h in range(H):
                    hs = slice(MLA_DK * h, MLA_DK * h + MLA_DK)
                    pe.wait_ge(*room("mq", li, h))
                    mm(bank("mq", li, h)[0:MLA_DK, 0:T], wuq[:, li, 0, hs], pr[:, CQ, :], True, False)
                    mm(bank("mq", li, h)[0:MLA_DK, 0:T], wuq[0:64, li, 1, hs], pr[0:64, CKV, :], False, True)\
                        .then_inc(made_of("mq", li, h), 1)
                pe.wait_ge(c_v, 5 * li + 5)
                for h in range(H):
                    pe.wait_ge(*room("mk", li, h))
                    mm(bank("mk", li, h)[0:NOPE, 0:T], wukv[64:128, li, P * h:P * h + NOPE], pr[64:128, CKV, :], True, True)\
                        .then_inc(made_of("mk", li, h), 1)
                wv = wukv[64:128, li, :].rearrange("p (h c) -> p h c", h=H)[:, :, NOPE:NOPE + DV]
                pe.wait_ge(*room("mvA", li))
                for c in range(2):
                    i = mm(bank("mvA", li)[:, 256 * c:256 * c + 256], pr[64:128, CKV, WIDE[c]], wv, True, True)
                i.then_inc(made_of("mvA", li), 1)
                pe.wait_ge(*room("mvB", li))
                mm(bank("mvB", li)[:, 0:256], pr[64:128, CKV, WIDE[2]], wv, True, True).then_inc(made_of("mvB", li), 1)

                pe.wait_ge(gla_v, 5 * li + 4)
                pe.wait_ge(*room("kd", li))
                for c, (a, q) in enumerate(((0, META), (META, P), (META + P, CHUNK))):
                    i = pe.transpose(bank("kd", li)[0:q, P * c:P * c + P], kdT[:, a:a + q], ident)
                i.then_inc(made_of("kd", li), 1)
                for h in range(H):
                    pe.wait_ge(*gone("mq", li, h))
                    pe.wait_ge(*room("qswap", li, h))
                    mm(bank("qswap", li, h)[64:96, 0:T], const("swap_mla")[64:96, :], qc[64:96, h, :], True, True)\
                        .then_inc(made_of("qswap", li, h), 1)
                pe.wait_ge(*gone("kd", li))
                pe.wait_ge(*gone("vA", li, 0))
                pe.wait_ge(*gone("vB", li, 0))
                for name, parts in (("upA", ((0, 0, META), (1, 0, CHUNK))), ("upB", ((1, CHUNK, CHUNK),)), ("upC", ((2, 0, CHUNK),))):
                    pe.wait_ge(*room(name, li))
                    for j, (c, p0, q) in enumerate(parts):
                        i = mm(bank(name, li)[:, 256 * j:256 * j + 256], kd_tok[p0:p0 + q, P * c:P * c + P],
                               va[p0:p0 + q, c, :], True, True)
                    i.then_inc(made_of(name, li), 1)
                pe.wait_ge(gla_v, 5 * li + 5)
                for h in range(H):
                    d = slice(GLA_DK * h, GLA_DK * h + GLA_DK)
                    pe.wait_ge(*room("gs", li, h))
                    for j, c in enumerate((1, 2, 0)):
                        i = mm(bank("gs", li, h)[:, P * j:P * j + P], pr[d, AK, WIDE[c]], pr[d, AQ, WIDE[c]], True, True,
                               tile_position=(GLA_DK * h, 0))
                    i.then_inc(made_of("gs", li, h), 1)
                oa, ol = bank("goA", li), bank("goB", li)
                pe.wait_ge(*room("goA", li))
                pe.wait_ge(*room("goB", li))
                for h in range(H):
                    hs, ho = slice(DV * h, DV * h + DV), slice(256 + DV * h, 256 + DV * h + DV)
                    mp = pt[:, h % 2, :]
                    pe.wait_ge(*gone("gs", li, h))
                    mm(oa[:, hs], mp[0:META, 256:384], va[0:META, 0, hs], h == 0, False, skip_group_check=True)
                    mm(oa[:, ho], mp[:, 0:128], va[:, 1, hs], False, False, skip_group_check=True)
                    mm(ol[:, hs], mp[:, 128:256], va[:, 2, hs], h == 0, False, skip_group_check=True).then_inc(map_used, 1)
                pe.wait_ge(st_v, 4 * li + 4)
                mm(oa[0:64, 256:512], pr[:, AQ, 16:80], state[0], False, False, skip_group_check=True)
                mm(oa[64:128, 256:512], pr[:, AQ, 80:144], state[1], False, True, skip_group_check=True)\
                    .then_inc(made_of("goA", li), 1)
                mm(ol[0:64, 0:256], pr[:, AQ, 144:208], state[2], False, False, skip_group_check=True)
                mm(ol[64:128, 0:256], pr[:, AQ, 208:272], state[3], False, True, skip_group_check=True)\
                    .then_inc(made_of("goB", li), 1)

                pe.wait_ge(rot_v, 8 * li + 8)
                for h in range(H):
                    d = slice(RET_DK * (h % 2), RET_DK * (h % 2) + RET_DK)
                    qt, kt = pr[d, RQ + h // 2, :], pr[d, RK + h // 2, :]
                    pe.wait_ge(*room("rsM", li, h))
                    mm(bank("rsM", li, h)[0:META, 0:T], kt[:, 0:META], qt, True, True).then_inc(made_of("rsM", li, h), 1)
                    pe.wait_ge(*room("rsX", li, h))
                    b = bank("rsX", li, h)
                    mm(b[:, 0:256], kt[:, WIDE[1]], qt[:, META:T], True, True)
                    mm(b[:, 256:384], kt[:, WIDE[2]], qt[:, WIDE[2]], True, True).then_inc(made_of("rsX", li, h), 1)
                oa, ol = bank("roA", li), bank("roB", li)
                pe.wait_ge(*gone("vA", li, 1))
                pe.wait_ge(*gone("vB", li, 1))
                pe.wait_ge(*room("roA", li))
                pe.wait_ge(*room("roB", li))
                for h in range(H):
                    hs, ho = slice(DV * h, DV * h + DV), slice(256 + DV * h, 256 + DV * h + DV)
                    mp = pt[:, h % 2, :]
                    mk = mp[0:META, 384:384 + T]
                    vmeta = vr[0:META, 0, hs]
                    pe.wait_ge(*gone("rsM", li, h))
                    pe.wait_ge(*gone("rsX", li, h))
                    mm(oa[:, hs], mk[:, WIDE[0]], vmeta, True, True, skip_group_check=True)
                    mm(oa[:, ho], mk[:, WIDE[1]], vmeta, True, False, skip_group_check=True)
                    i = mm(oa[:, ho], mp[:, 0:128], vr[:, 1, hs], False, True, skip_group_check=True)
                    if h == H - 1:
                        i.then_inc(made_of("roA", li), 1)
                    mm(ol[:, hs], mk[:, WIDE[2]], vmeta, True, False, skip_group_check=True)
                    mm(ol[:, hs], mp[:, 128:256], vr[:, 1, hs], False, False, skip_group_check=True)
                    i = mm(ol[:, hs], mp[:, 256:384], vr[:, 2, hs], False, True, skip_group_check=True)
                    i.then_inc(made_of("roB", li) if h == H - 1 else map_used, 1)

                def scores(m):
                    b = bank("sc", li, m)
                    if m < DIFF_MAPS:
                        d = slice(DIFF_DK * (m % 4), DIFF_DK * (m % 4) + DIFF_DK)
                        q, k = pr[d, DQ + m // 4, :], pr[d, DK + m // 4, :]
                        kw = {"tile_position": (DIFF_DK * (m % 4), 0)}
                    else:
                        q, k, kw = qc[0:MLA_DK, m - DIFF_MAPS, :], kc[0:MLA_DK, m - DIFF_MAPS, :], {}
                    if m == 0:
                        pe.wait_ge(*gone("proj", li, DK + 1))
                    if m == DIFF_MAPS:
                        pe.wait_ge(*gone("mk", li, H - 1))
                        pe.wait_ge(rk_v, 2 * li + 2)
                        pe.wait_ge(rq_v, 8 * li + 8)
                    pe.wait_ge(*room("sc", li, m))
                    mm(b[:, 0:T], q[:, WIDE[2]], k, True, True, **kw)
                    mm(b[:, T:T + 144], q[:, WIDE[1]], k[:, 0:144], True, True, **kw)
                    mm(b[:, T + 144:T + 160], q[:, WIDE[0]], k[:, 0:META], True, True, **kw).then_inc(made_of("sc", li, m), 1)

                def turn_map(m):
                    pb = probs[:, m % 3, :]
                    pe.wait_ge(exp_a, N_MAPS * li + m + 1)
                    pe.wait_ge(*room("ptX", li, m))
                    b = bank("ptX", li, m)
                    pe.transpose(b[:, 0:128], pb[:, T + META:T + 144], ident)
                    pe.transpose(b[:, 128:256], pb[:, WIDE[1]], ident)
                    pe.transpose(b[:, 256:384], pb[:, WIDE[2]], ident).then_inc(made_of("ptX", li, m), 1)
                    pe.wait_ge(*room("ptM", li, m))
                    b = bank("ptM", li, m)
                    pe.transpose(b[0:META, 0:128], pb[:, T:T + META], ident)
                    pe.transpose(b[0:META, 128:256], pb[:, 0:META], ident)
                    pe.transpose(b[0:META, 256:384], pb[:, T + 144:T + 160], ident).then_inc(made_of("ptM", li, m), 1)

                def output(m):
                    v, h = (vd, m // 2) if m < DIFF_MAPS else (vm, m - DIFF_MAPS)
                    hs = slice(DV * h, DV * h + DV)
                    mp, b = pt[:, m % 2, :], bank("o", li, m)
                    if m == 0:
                        pe.wait_ge(*gone("vA", li, 2))
                        pe.wait_ge(*gone("vB", li, 2))
                    if m == DIFF_MAPS:
                        pe.wait_ge(*gone("mvA", li))
                        pe.wait_ge(*gone("mvB", li))
                    pe.wait_ge(*gone("ptX", li, m))
                    pe.wait_ge(*gone("ptM", li, m))
                    pe.wait_ge(*room("o", li, m))
                    mm(b[:, 0:64], mp[0:META, 640:768], v[0:META, 0, hs], True, True)
                    mm(b[:, 64:128], mp[0:META, 384:512], v[0:META, 0, hs], True, False)
                    mm(b[:, 64:128], mp[:, 0:128], v[:, 1, hs], False, True)
                    mm(b[:, 128:192], mp[0:META, 512:640], v[0:META, 0, hs], True, False)
                    mm(b[:, 128:192], mp[:, 128:256], v[:, 1, hs], False, False)
                    mm(b[:, 128:192], mp[:, 256:384], v[:, 2, hs], False, True).then_inc(made_of("o", li, m), 1)

                for m in range(N_MAPS + 3):
                    if m < N_MAPS:
                        scores(m)
                    if 2 <= m < N_MAPS + 2:
                        turn_map(m - 2)
                    if m >= 3:
                        output(m - 3)
                    if m in TURNS:
                        pe.wait_ge(n_v, N_NORM * li + (3 if m == 3 else 9))
                        for k in TURNS[m]:
                            turn_output(li, k, ob if m == 3 else ob_r)
                pe.wait_ge(*gone("o", li, N_MAPS - 1))
                for k in (4, 5):
                    turn_output(li, k, om)
                pe.wait_ge(n_v, N_NORM * li + N_NORM)
                for k in (6, 7):
                    turn_output(li, k, o1)

                for n in range(2):
                    pe.wait_ge(*in_slot(load_out(li, n)))
                for k in range(KD):
                    pe.wait_ge(*room("wo", li, k))
                    for j in range(KD):
                        if k == 0:
                            pe.wait_ge(*gone("turn", li, j))
                        m = slot(load_out(li, j // 4))
                        at = D * (j % 4) + P * k
                        i = mm(bank("wo", li, k)[:, 0:T], ring[:, m, at:at + P], oT[:, j, :], j == 0, j == KD - 1)
                    i.then_inc(made_of("wo", li, k), 1)
                mean_squares(2 * li + 1)

                if li == 0:
                    for c, (f0, w) in enumerate(FF_GROUPS):
                        for f in range(f0 // P, (f0 + w) // P):
                            for u, name in enumerate(("fg", "fu")):
                                m = load_ff(2 * c + u)
                                wt = ring[:, slot(m), 0:KD * w].rearrange("p (k f) -> p k f", k=KD)
                                pe.wait_ge(*in_slot(m))
                                pe.wait_ge(*room(name, f))
                                for k in range(KD):
                                    if f == 0 and u == 0:
                                        pe.wait_ge(hn_v, KD * 1 + k + 1)
                                    i = mm(bank(name, f)[:, 0:T], wt[:, k, P * f - f0:P * f - f0 + P], hnT[:, k, :],
                                           k == 0, k == KD - 1)
                                i.then_inc(made_of(name, f), 1)
                    for j in range(len(DOWN_TILES)):
                        pe.wait_ge(*in_slot(load_ff(2 * len(FF_GROUPS) + j)))
                    for k in range(KD):
                        pe.wait_ge(*room("fd", k))
                        for f in range(FT):
                            if k == 0:
                                pe.wait_ge(*gone("fu", f))
                            m = slot(load_ff(2 * len(FF_GROUPS) + f // 4))
                            at = D * (f % 4) + P * k
                            i = mm(bank("fd", k)[:, 0:T], ring[:, m, at:at + P], ffa[:, f, :], f == 0, f == FT - 1)
                        i.then_inc(made_of("fd", k), 1)

            for j in range(4):
                c, k0 = 1 + j // 2, 4 * (j % 2)
                pe.wait_ge(*room("h_tok", j))
                for k in range(4):
                    i = pe.transpose(bank("h_tok", j)[:, P * k:P * k + P], hT[:, k0 + k, WIDE[c]], ident)
                i.then_inc(made_of("h_tok", j), 1)
            pe.wait_ge(hn_v, KD * 4)
            for j in range(4):
                c, k0 = 1 + j // 2, 4 * (j % 2)
                pe.wait_ge(*room("hn_tok", j))
                for k in range(4):
                    i = pe.transpose(bank("hn_tok", j)[:, P * k:P * k + P], hnT[:, k0 + k, WIDE[c]], ident)
                i.then_inc(made_of("hn_tok", j), 1)
            pe.wait_ge(*room("logits"))
            for c in range(2):
                for k in range(KD):
                    i = mm(bank("logits")[:, EXPERTS * c:EXPERTS * c + EXPERTS], hnT[:, k, WIDE[c + 1]], wrout[:, k, :],
                           k == 0, k == KD - 1)
            i.then_inc(made_of("logits"), 1)
            pe.wait_ge(r_v, R_MASK)
            m0, m1 = route[:, R["mask"]:R["mask"] + 8], route[:, R["mask"] + 8:R["mask"] + 16]
            b = bank("pos")
            pe.wait_ge(*room("pos"))
            mm(b[:, 0:8], const("upper"), m0, True, True)
            mm(b[:, 8:16], ones, m0, True, False)
            mm(b[:, 8:16], const("upper"), m1, False, True).then_inc(made_of("pos"), 1)
            pe.wait_ge(*room("count"))
            mm(bank("count")[:, 0:8], ones, m0, True, False)
            mm(bank("count")[:, 0:8], ones, m1, False, True).then_inc(made_of("count"), 1)
            for j in range(4):
                pe.wait_ge(*gone("hn_tok", j))
                pe.wait_ge(*gone("h_tok", j))

            def item(i):
                pe.wait_ge(sel_v, 2 * i + 2)
                for j in range(2):
                    pe.wait_ge(*room_i(i, "xg", j))
                    for k in range(4):
                        for c in range(2):
                            f = P * (4 * j + k)
                            m = mm(bank("xg", j)[:, P * k:P * k + P], hn_tok[:, c, f:f + P], sel[:, c, :], c == 0, c == 1)
                    m.then_inc(made_of("xg", j), 1)
                pe.wait_ge(*room_i(i, "selT"))
                for c in range(2):
                    m = pe.transpose(bank("selT")[:, P * c:P * c + P], sel[:, c, :], ident)
                m.then_inc(made_of("selT"), 1)

                def product(name, n, c):
                    pe.wait_ge(*in_slot_i(i, n))
                    pe.wait_ge(*room_i(i, name, c))
                    s = slot(MOE0 + n)
                    for k in range(KD):
                        if n == 0 and k % 4 == 0:
                            pe.wait_ge(*gone_i(i, "xg", k // 4))
                        m = mm(bank(name, c), xg[:, P * k:P * k + P], ring[:, s, FC * k:FC * k + FC], k == 0, k == KD - 1)
                    m.then_inc(made_of(name, c), 1)

                def turn(c):
                    pe.wait_ge(*gone_i(i, "u", c))
                    pe.wait_ge(*room_i(i, "aT", c))
                    for j in range(4):
                        m = pe.transpose(bank("aT", c)[:, P * j:P * j + P],
                                         act_sb[:, c % 2, :].rearrange("p (f j) -> p j f", j=4)[:, j, :], ident)
                    m.then_inc(made_of("aT", c), 1)

                def down(c):
                    pe.wait_ge(*gone_i(i, "aT", c))
                    pe.wait_ge(*in_slot_i(i, at_down(c)))
                    if c == 0:
                        pe.wait_ge(*room_i(i, "y", 0))
                        pe.wait_ge(*room_i(i, "y", 1))
                    s = slot(MOE0 + at_down(c))
                    for j in range(4):
                        for half in range(2):
                            m = mm(bank("y", half), actT[:, c % 2, P * j:P * j + P],
                                   ring[:, s, D * j + FC * half:D * j + FC * half + FC],
                                   c == 0 and j == 0, c == NFC - 1 and j == 3)
                            if c == NFC - 1 and j == 3:
                                m.then_inc(made_of("y", half), 1)
                            elif j == 3 and half == 1:
                                m.then_inc(down_used, 1)

                for c in range(NFC):
                    product("g", at_gate(c), c)
                    if c:
                        turn(c - 1)
                    product("u", at_up(c), c)
                    if c:
                        down(c - 1)
                turn(NFC - 1)
                down(NFC - 1)
                pe.wait_ge(*gone_i(i, "selT"))
                for j in range(4):
                    c, half = j // 2, j % 2
                    pe.wait_ge(*gone_i(i, "y", half))
                    pe.wait_ge(*room_i(i, "back", j))
                    mm(bank("back", j), selT[:, c, :], ysb[:, FC * half:FC * half + FC], True, True)\
                        .then_inc(made_of("back", j), 1)

            pe.wait_ge(r_v, N_ROUTE)
            n_items = pe.value_load(ctl[0:1, 0:1], min_val=EXPERTS, max_val=ITEMS)
            with pe.Fori(0, ITEMS) as i:
                with pe.If(i < n_items):
                    item(i)

        @block.scalar
        def _(act):
            r = 0
            for a, n in ((attn_norm, KD), (ffn_norm, KD)):
                act.dma_start(rows[r:r + LAYERS * n, :], a.rearrange("l (k p) -> (l k) p", p=P)).then_inc(rows_in, 16)
                r += LAYERS * n
            act.dma_start(rows[32:34, :], mla_q_norm[:, 0:P]).then_inc(rows_in, 16)
            act.dma_start(rows[34:36, 0:64], mla_q_norm[:, P:Q_RANK]).then_inc(rows_in, 16)
            act.dma_start(rows[34:36, 64:128], mla_kv_norm).then_inc(rows_in, 16)
            for a, r in ((gla_norm, 36), (ret_norm, 38), (diff_norm, 40), (gla_norm, 42), (ret_norm, 44), (diff_norm, 46)):
                for half in range(2):
                    act.dma_start(rows[r:r + 2, 64 * half:64 * half + 64], a).then_inc(rows_in, 16)
            act.dma_start(wgate[:, :, :], gla_w_gate.rearrange("l r f -> r l f")).then_inc(params_in, 16)
            act.dma_start(bgate[:, :, :], gla_b_gate.partition_broadcast(P)).then_inc(params_in, 16)
            act.dma_start(dlam, diff_lambda.partition_broadcast(P)).then_inc(params_in, 16)
            act.dma_start(wuq[:, :, 0, :], mla_w_uq[:, 0:P, :].rearrange("l p f -> p l f")).then_inc(params_in, 16)
            act.dma_start(wuq[0:64, :, 1, :], mla_w_uq[:, P:Q_RANK, :].rearrange("l p f -> p l f")).then_inc(params_in, 16)
            act.dma_start(wukv[64:128, :, :], mla_w_ukv.rearrange("l p f -> p l f")).then_inc(params_in, 16)
            act.dma_start(wrout[:, :, :], moe_router[0].rearrange("(k p) e -> p k e", p=P)).then_inc(params_in, 16)

            def squares(r):
                for k in range(KD):
                    act.wait_ge(*gone(*stream(r, k)))
                    if k == 0 and r in (1, 3):
                        act.wait_ge(*done("wo", r // 2, KD - 1))
                    act.activation(hnT[:, k, :], hT[:, k, :], ACT.Square).then_inc(sq_a, 1)
                act.wait_ge(*gone("ms", r))
                act.activation(rms[:, 1, :], rms[:, 0, :], ACT.Sqrt).then_inc(rms_a, 1)

            act.wait_ge(lam_v, 4)
            act.activation(lam[:, 0:4], lam[:, 0:4], ACT.Exp).then_inc(lam_a, 1)
            squares(0)
            for li in range(LAYERS):
                if li:
                    squares(2 * li)

                def values(n, v):
                    act.wait_ge(*done("vA", li, n))
                    act.activation(v[:, 0:2, :], bank("vA", li, n)[:, :].rearrange("p (c v) -> p c v", c=2), ACT.Copy)\
                        .then_inc(taken_of("vA", li, n), 1)
                    act.wait_ge(*done("vB", li, n))
                    act.activation(v[:, 2, :], bank("vB", li, n)[:, 0:256], ACT.Copy).then_inc(taken_of("vB", li, n), 1)

                for n, (_, _, tiles) in enumerate(IN_LOADS):
                    for t, _, wd, p0 in tiles:
                        f = ACT.Silu if t in (AOG, AOG + 1, ROG, ROG + 1) else ACT.Copy
                        act.wait_ge(*done("proj", li, t))
                        act.activation(pr[p0:p0 + wd, t, :], bank("proj", li, t)[p0:p0 + wd, 0:T], f)\
                            .then_inc(taken_of("proj", li, t), 1)
                    if n == 2:
                        values(0, va)
                    if n == 3:
                        act.wait_ge(gla_v, 5 * li + 1)
                        act.activation(gabs, gabs, ACT.Exp, scale=-1.0).then_inc(gate_a, 1)
                        act.wait_ge(gate_a, 2 * li + 1)
                        act.activation(gabs, gabs, ACT.Ln, bias=1.0).then_inc(gate_a, 1)
                    if n == 4:
                        values(1, vr)
                        act.wait_ge(*gone("proj", li, CQ))
                        act.wait_ge(*gone("proj", li, CKV))
                        act.activation(rms[:, 0, :], pr[:, CQ, :], ACT.Square).then_inc(c_a, 1)
                        act.activation(rms[:, 1, :], pr[:, CKV, :], ACT.Square).then_inc(c_a, 1)
                    if n == 5:
                        act.wait_ge(*gone("cum", li))
                        act.activation(eq, cumT, ACT.Exp).then_inc(cum_a, 1)
                        act.activation(ek, cumT, ACT.Exp, scale=-1.0).then_inc(cum_a, 1)
                        for a, e in ((0, 16), (16, 80), (80, 144), (144, 208)):
                            act.activation(ekd[:, a:e], cumT[:, a:e], ACT.Exp, bias=cumT[:, e - 1:e], scale=-1.0)\
                                .then_inc(cum_a, 1)
                        act.wait_ge(*gone("cq", li))
                        act.activation(rms[:, 0, :], rms[:, 0, :], ACT.Sqrt).then_inc(c_a, 1)
                        act.wait_ge(*gone("ckv", li))
                        act.activation(rms[64:128, 1, :], rms[64:128, 1, :], ACT.Sqrt).then_inc(c_a, 1)
                values(2, vd)
                for h in range(H):
                    act.wait_ge(*done("mq", li, h))
                    act.activation(qc[0:MLA_DK, h, :], bank("mq", li, h)[0:MLA_DK, 0:T], ACT.Copy).then_inc(taken_of("mq", li, h), 1)
                for h in range(H):
                    act.wait_ge(*done("mk", li, h))
                    act.activation(kc[0:NOPE, h, :], bank("mk", li, h)[0:NOPE, 0:T], ACT.Copy).then_inc(taken_of("mk", li, h), 1)
                act.wait_ge(*done("mvA", li))
                act.activation(vm[:, 0:2, :], bank("mvA", li)[:, :].rearrange("p (c v) -> p c v", c=2), ACT.Copy)\
                    .then_inc(taken_of("mvA", li), 1)
                act.wait_ge(*done("mvB", li))
                act.activation(vm[:, 2, :], bank("mvB", li)[:, 0:256], ACT.Copy).then_inc(taken_of("mvB", li), 1)
                for name, o in (("go", ob), ("ro", ob_r)):
                    act.wait_ge(*done(name + "A", li))
                    act.activation(o[:, 0:2, :], bank(name + "A", li)[:, :].rearrange("p (c v) -> p c v", c=2), ACT.Copy)\
                        .then_inc(taken_of(name + "A", li), 1)
                    act.wait_ge(*done(name + "B", li))
                    act.activation(o[:, 2, :], bank(name + "B", li)[:, 0:256], ACT.Copy).then_inc(taken_of(name + "B", li), 1)
                    if name == "go":
                        act.wait_ge(*gone("goB", li))
                        act.wait_ge(*gone("goA", li))
                        act.activation(sq[:, :, :], ob[:, :, :], ACT.Square).then_inc(n_a, 1)
                for m in range(N_MAPS + 2):
                    if m < N_MAPS:
                        act.wait_ge(*gone("sc", li, m))
                        pb = probs[:, m % 3, :]
                        for c, a, e in ((2, 0, T), (1, T, T + 144), (0, T + 144, T + 160)):
                            i = act.activation(pb[:, a:e], pb[:, a:e], ACT.Exp, bias=neg_max[:, m, c:c + 1], scale=-1.0,
                                               accum_out=den[:, m, c:c + 1])
                        i.then_inc(exp_a, 1)
                    if m >= 2:
                        act.wait_ge(*done("ptM", li, m - 2))
                        if m >= 4:
                            act.wait_ge(*done("o", li, m - 4))
                        act.activation(pt[0:META, m % 2, 384:768], bank("ptM", li, m - 2)[0:META, 0:384], ACT.Copy)\
                            .then_inc(taken_of("ptM", li, m - 2), 1)
                    if m == 5:
                        act.wait_ge(n_v, N_NORM * li + 6)
                        act.activation(sq[:, :, :], ob_r, ACT.Square).then_inc(n_a, 1)
                    if m == 11:
                        act.wait_ge(n_v, N_NORM * li + 10)
                        act.activation(sq[:, :, :], o1[:, :, :], ACT.Square).then_inc(n_a, 1)
                for k in (4, 5):
                    act.wait_ge(*done("turn", li, k))
                    act.activation(oT[:, k, :], bank("turn", li, k)[:, 0:T], ACT.Copy).then_inc(taken_of("turn", li, k), 1)
                squares(2 * li + 1)
                if li == 0:
                    for f in range(FT):
                        act.wait_ge(*done("fg", f))
                        if f >= 2:
                            act.wait_ge(*gone("fu", f - 2))
                        act.activation(ffs[:, f % 2, :], bank("fg", f)[:, 0:T], ACT.Silu).then_inc(taken_of("fg", f), 1)
            for j in range(4):
                act.wait_ge(*done("hn_tok", j))
                act.activation(hn_tok[:, j // 2, FC * (j % 2):FC * (j % 2) + FC], bank("hn_tok", j), ACT.Copy)\
                    .then_inc(taken_of("hn_tok", j), 1)
            act.wait_ge(r_v, R_EXP)
            act.activation(route[:, R["e"]:R["e"] + 2], route[:, R["d"]:R["d"] + 2], ACT.Exp).then_inc(r_a, 1)

            def item(i):
                for j in range(2):
                    act.wait_ge(*done_i(i, "xg", j))
                    act.activation(xg[:, FC * j:FC * j + FC], bank("xg", j), ACT.Copy).then_inc(taken_of("xg", j), 1)

                def turned(c):
                    act.wait_ge(*done_i(i, "aT", c))
                    if c >= 2:
                        act.wait_ge(down_used, (NFC - 1) * i + c - 1)
                    act.activation(actT[:, c % 2, :], bank("aT", c), ACT.Copy).then_inc(taken_of("aT", c), 1)

                for c in range(NFC):
                    act.wait_ge(*done_i(i, "g", c))
                    if c >= 2:
                        act.wait_ge(*gone_i(i, "u", c - 2))
                    act.activation(sg[:, c % 2, :], bank("g", c), ACT.Silu).then_inc(taken_of("g", c), 1)
                    if c:
                        turned(c - 1)
                turned(NFC - 1)
                act.wait_ge(*done_i(i, "y", 0))
                act.activation(ysb[:, 0:FC], bank("y", 0), ACT.Copy).then_inc(taken_of("y", 0), 1)

            act.wait_ge(r_v, N_ROUTE)
            n_items = act.value_load(ctl[0:1, 0:1], min_val=EXPERTS, max_val=ITEMS)
            with act.Fori(0, ITEMS) as i:
                with act.If(i < n_items):
                    item(i)
            act.wait_ge(*gone_i(n_items - 1, "back", 3))
            for c in range(2):
                act.activation(out_sb[:, c, :], h_tok[:, c, :], ACT.Square, accum_out=st1[:, c:c + 1]).then_inc(fin_a, 1)

        @block.vector
        def _(dve):
            dve.wait_ge(params_in, 16 * N_PARAMS)
            for li in range(LAYERS):
                for j in range(2):
                    dve.tensor_tensor_reduce(t1[:, 64 * li + 32 * j:64 * li + 32 * j + 32], dlam[:, li, 2 * j, :], dlam[:, li, 2 * j + 1, :],
                                             1.0, 0.0, ALU.mult, ALU.add, lam[:, 2 * li + j:2 * li + j + 1]).then_inc(lam_v, 1)
            dve.wait_ge(lam_a, 1)
            for li in range(LAYERS):
                dve.scalar_tensor_tensor(out=lam[:, 4 + li:5 + li], in0=lam[:, 2 * li + 1:2 * li + 2], scalar=-LAM_INIT[li],
                                         in1=lam[:, 2 * li:2 * li + 1], op0=ALU.add, op1=ALU.subtract).then_inc(lam_v, 1)
            dve.wait_ge(*done("cols"))
            dve.tensor_copy(cols[:, :], bank("cols")[:, 0:48]).then_inc(taken_of("cols"), 1)
            for k in range(KD):
                dve.wait_ge(*done("x", k))
                dve.tensor_copy(hT[:, k, :], bank("x", k)[:, 0:T]).then_inc(taken_of("x", k), 1)
            dve.wait_ge(*gone("cols"))

            def normalize(r):
                dve.wait_ge(*done("ms", r))
                dve.tensor_scalar(rms[:, 0, :], bank("ms", r)[:, 0:T], 1.0 / D, EPS, ALU.mult, ALU.add)\
                    .then_inc(taken_of("ms", r), 1)
                dve.wait_ge(rms_a, r + 1)
                dve.reciprocal(rms[:, 0, :], rms[:, 1, :]).then_inc(rstd_v, 1)
                dve.wait_ge(rstd_v, r + 1)
                for k in range(KD):
                    dve.scalar_tensor_tensor(out=hnT[:, k, :], in0=hT[:, k, :], scalar=gain("ffn" if r % 2 else "attn", r // 2, k),
                                             in1=rms[:, 0, :], op0=ALU.mult, op1=ALU.mult).then_inc(hn_v, 1)

            def head_sums(o, n):
                dve.tensor_reduce(st1, o[:, :, :].rearrange("p c (h v) -> p (c h) v", h=H), AX.X, ALU.add).then_inc(n_v, 1)

            def head_mean_squares(li, step, n):
                dve.wait_ge(n_v, N_NORM * li + step)
                dve.tensor_scalar(st2, st1, 1.0 / DV, EPS, ALU.mult, ALU.add).then_inc(n_v, 1)

            def head_scale(li, o, n):
                dve.wait_ge(n_p, 3 * li + n)
                v = o[:, :, :].rearrange("p c (h v) -> p (c h) v", h=H)
                dve.tensor_tensor(v, v, st3.unsqueeze(2).to_broadcast([P, 12, DV]), ALU.mult).then_inc(n_v, 1)

            for li in range(LAYERS):
                normalize(2 * li)
                dve.wait_ge(*done("gate", li))
                dve.tensor_tensor(gx.rearrange("p (c f) -> p c f", c=3), bank("gate", li)[:, 0:384].rearrange("p (c f) -> p c f", c=3),
                                  bgate[:, li, :].unsqueeze(1).to_broadcast([P, 3, P]), ALU.add).then_inc(taken_of("gate", li), 1)
                dve.wait_ge(*gone("gate", li))
                dve.scalar_tensor_tensor(out=gabs, in0=gx, scalar=-1.0, in1=gx, op0=ALU.mult, op1=ALU.max).then_inc(gla_v, 1)
                for j in range(4):
                    dve.wait_ge(*gone("proj", li, RQ + j))
                    if j:
                        dve.wait_ge(rot_v, 8 * li + 2 * j)
                    dve.tensor_tensor(t1, pr[:, RQ + j, :], const("cos_ret"), ALU.mult).then_inc(rot_v, 1)
                    dve.wait_ge(*done("swap", li, j))
                    dve.tensor_tensor(t2, bank("swap", li, j)[:, 0:T], const("sin_ret"), ALU.mult).then_inc(taken_of("swap", li, j), 1)
                    dve.wait_ge(rot_v, 8 * li + 2 * j + 1)
                    dve.wait_ge(*gone("swap", li, j))
                    dve.tensor_tensor(pr[:, RQ + j, :], t1, t2, ALU.add).then_inc(rot_v, 1)
                dve.wait_ge(gate_a, 2 * li + 2)
                dve.scalar_tensor_tensor(out=gx, in0=gx, scalar=0.0, in1=gabs, op0=ALU.min, op1=ALU.subtract).then_inc(gla_v, 1)
                dve.wait_ge(*done("cum", li))
                dve.tensor_copy(cumT, bank("cum", li)[:, 0:T]).then_inc(taken_of("cum", li), 1)
                dve.wait_ge(*done("cq", li))
                dve.wait_ge(*done("ckv", li))
                dve.tensor_scalar(rms[:, 0, :], bank("cq", li)[:, 0:T], 1.0 / Q_RANK, EPS, ALU.mult, ALU.add)\
                    .then_inc(taken_of("cq", li), 1)
                dve.tensor_scalar(rms[64:128, 1, :], bank("ckv", li)[64:128, 0:T], 1.0 / 64, EPS, ALU.mult, ALU.add)\
                    .then_inc(taken_of("ckv", li), 1)
                r4 = slice(64, 96)
                dve.wait_ge(rot_v, 8 * li + 8)
                dve.tensor_tensor(t1[r4, :], pr[r4, KPE, :], const("cos_mla")[r4, :], ALU.mult).then_inc(rk_v, 1)
                dve.wait_ge(*done("kswap", li))
                dve.tensor_tensor(t2[r4, :], bank("kswap", li)[r4, 0:T], const("sin_mla")[r4, :], ALU.mult)\
                    .then_inc(taken_of("kswap", li), 1)
                dve.wait_ge(cum_a, 6 * li + 6)
                dve.scalar_tensor_tensor(out=pr[:, AQ, :], in0=pr[:, AQ, :], scalar=GLA_DK**-0.5, in1=eq, op0=ALU.mult, op1=ALU.mult)\
                    .then_inc(gla_v, 1)
                dve.tensor_tensor(kdT[:, 0:208], pr[:, AK, 0:208], ekd[:, 0:208], ALU.mult).then_inc(gla_v, 1)
                dve.wait_ge(gla_v, 5 * li + 4)
                dve.tensor_tensor(pr[:, AK, :], pr[:, AK, :], ek, ALU.mult).then_inc(gla_v, 1)
                dve.wait_ge(c_a, 4 * li + 4)
                dve.reciprocal(rms[:, 0, :], rms[:, 0, :]).then_inc(c_v, 1)
                dve.reciprocal(rms[64:128, 1, :], rms[64:128, 1, :]).then_inc(c_v, 1)
                dve.wait_ge(c_v, 5 * li + 2)
                dve.scalar_tensor_tensor(out=pr[:, CQ, :], in0=pr[:, CQ, :], scalar=gain("q", li), in1=rms[:, 0, :],
                                         op0=ALU.mult, op1=ALU.mult).then_inc(c_v, 1)
                dve.scalar_tensor_tensor(out=pr[0:64, CKV, :], in0=pr[0:64, CKV, :], scalar=gain("q_kv", li)[0:64, :],
                                         in1=rms[0:64, 0, :], op0=ALU.mult, op1=ALU.mult).then_inc(c_v, 1)
                dve.scalar_tensor_tensor(out=pr[64:128, CKV, :], in0=pr[64:128, CKV, :], scalar=gain("q_kv", li)[64:128, :],
                                         in1=rms[64:128, 1, :], op0=ALU.mult, op1=ALU.mult).then_inc(c_v, 1)
                dve.wait_ge(rk_v, 2 * li + 1)
                dve.wait_ge(*gone("kswap", li))
                dve.wait_ge(*done("proj", li, TILES - 1))
                dve.tensor_tensor(kc[r4, :, :], t1[r4, :].unsqueeze(1).to_broadcast([32, H, T]),
                                  t2[r4, :].unsqueeze(1).to_broadcast([32, H, T]), ALU.add).then_inc(rk_v, 1)
                dve.wait_ge(*done("kd", li))
                dve.tensor_copy(kd_tok[0:META, 0:128], bank("kd", li)[0:META, 0:128])
                dve.tensor_copy(kd_tok[:, 128:256], bank("kd", li)[:, 128:256])
                dve.tensor_copy(kd_tok[0:64, 256:384], bank("kd", li)[0:64, 256:384]).then_inc(taken_of("kd", li), 1)
                for h in range(H):
                    dve.wait_ge(*gone("mq", li, h))
                    if h:
                        dve.wait_ge(rq_v, 8 * li + 2 * h)
                    else:
                        dve.wait_ge(rk_v, 2 * li + 2)
                    dve.tensor_tensor(t1[r4, :], qc[r4, h, :], const("cos_mla")[r4, :], ALU.mult).then_inc(rq_v, 1)
                    dve.wait_ge(*done("qswap", li, h))
                    dve.tensor_tensor(t2[r4, :], bank("qswap", li, h)[r4, 0:T], const("sin_mla")[r4, :], ALU.mult)\
                        .then_inc(taken_of("qswap", li, h), 1)
                    dve.wait_ge(rq_v, 8 * li + 2 * h + 1)
                    dve.wait_ge(*gone("qswap", li, h))
                    dve.tensor_tensor(qc[r4, h, :], t1[r4, :], t2[r4, :], ALU.add).then_inc(rq_v, 1)
                dve.wait_ge(*done("upA", li))
                dve.tensor_tensor(state[0], bank("upA", li)[:, 0:256], const("block"), ALU.mult).then_inc(st_v, 1)
                dve.tensor_tensor(state[1], bank("upA", li)[:, 256:512], const("block"), ALU.mult).then_inc(taken_of("upA", li), 1)
                dve.wait_ge(*done("upB", li))
                dve.tensor_tensor(state[2], bank("upB", li)[:, 0:256], const("block"), ALU.mult).then_inc(taken_of("upB", li), 1)
                dve.wait_ge(*done("upC", li))
                dve.tensor_tensor(state[3], bank("upC", li)[:, 0:256], const("block"), ALU.mult).then_inc(taken_of("upC", li), 1)
                for name in ("upA", "upB", "upC"):
                    dve.wait_ge(*gone(name, li))
                for j in range(3):
                    dve.wait_ge(st_v, 4 * li + 1 + j)
                    e = (80, 144, 208)[j]
                    dve.scalar_tensor_tensor(out=state[j + 1], in0=state[j], scalar=eq[:, e - 1:e], in1=state[j + 1],
                                             op0=ALU.mult, op1=ALU.add).then_inc(st_v, 1)
                for h in range(H):
                    dve.wait_ge(*done("gs", li, h))
                    if h >= 2:
                        dve.wait_ge(map_used, 7 * li + h - 1)
                    dve.tensor_tensor(pt[:, h % 2, 0:384].rearrange("p (c q) -> p c q", c=3),
                                      bank("gs", li, h)[:, 0:384].rearrange("p (c q) -> p c q", c=3),
                                      const("intra").unsqueeze(1).to_broadcast([P, 3, P]), ALU.mult).then_inc(taken_of("gs", li, h), 1)
                for h in range(H):
                    dve.wait_ge(map_used, 7 * li + 3 + h)
                    mp = pt[:, h % 2, :]
                    dve.wait_ge(*done("rsM", li, h))
                    dve.tensor_tensor(mp[0:META, 384:384 + T], bank("rsM", li, h)[0:META, 0:T], decay[0:META, h, :], ALU.mult)\
                        .then_inc(taken_of("rsM", li, h), 1)
                    dve.wait_ge(*done("rsX", li, h))
                    dve.tensor_tensor(mp[:, 0:256], bank("rsX", li, h)[:, 0:256], decay[:, h, 0:256], ALU.mult)
                    dve.tensor_tensor(mp[:, 256:384], bank("rsX", li, h)[:, 256:384], decay[:, h, 0:128], ALU.mult)\
                        .then_inc(taken_of("rsX", li, h), 1)
                sc = DIFF_DK**-0.5
                for m in range(N_MAPS + 3):
                    if m - 1 in TURNS:
                        kind = "gla" if m == 4 else "ret"
                        og = AOG if m == 4 else ROG
                        for j, k in enumerate(TURNS[m - 1]):
                            dve.wait_ge(*done("turn", li, k))
                            dve.scalar_tensor_tensor(out=oT[:, k, :], in0=bank("turn", li, k)[:, 0:T], scalar=gain(kind, li),
                                                     in1=pr[:, og + j, :], op0=ALU.mult, op1=ALU.mult).then_inc(taken_of("turn", li, k), 1)
                    if m < N_MAPS:
                        sc = DIFF_DK**-0.5 if m < DIFF_MAPS else MLA_DK**-0.5
                        dve.wait_ge(*done("sc", li, m))
                        b, pb = bank("sc", li, m), probs[:, m % 3, :]
                        if m >= 3:
                            dve.wait_ge(*done("ptM", li, m - 3))
                        for c, a, e, q in ((2, 0, T, 0), (1, T, T + 144, 128), (0, T + 144, T + 160, 144)):
                            i = dve.tensor_tensor_reduce(pb[:, a:e], b[:, a:e], mask[:, q:q + e - a], -sc, 3e38,
                                                         ALU.add, ALU.min, neg_max[:, m, c:c + 1])
                        i.then_inc(taken_of("sc", li, m), 1)
                        if m:
                            dve.wait_ge(exp_a, N_MAPS * li + m)
                            dve.reciprocal(rden[:, m - 1, :], den[:, m - 1, :]).then_inc(rd_v, 1)
                    if m == N_MAPS:
                        dve.wait_ge(exp_a, N_MAPS * li + m)
                        dve.reciprocal(rden[:, m - 1, :], den[:, m - 1, :]).then_inc(rd_v, 1)
                    if 2 <= m < N_MAPS + 2:
                        dve.wait_ge(*done("ptX", li, m - 2))
                        if m >= 4:
                            dve.wait_ge(*done("o", li, m - 4))
                        dve.tensor_copy(pt[:, m % 2, 0:384], bank("ptX", li, m - 2)[:, 0:384]).then_inc(taken_of("ptX", li, m - 2), 1)
                    if m >= 3:
                        n = m - 3
                        o, h = (((o1, o2)[n % 2], n // 2) if n < DIFF_MAPS else (om, n - DIFF_MAPS))
                        dve.wait_ge(*done("o", li, n))
                        dve.wait_ge(rd_v, N_MAPS * li + n + 1)
                        dve.tensor_tensor(o[:, :, DV * h:DV * h + DV], bank("o", li, n)[:, 0:192].rearrange("p (c v) -> p c v", c=3),
                                          rden[:, n, :].unsqueeze(2).to_broadcast([P, 3, DV]), ALU.mult).then_inc(taken_of("o", li, n), 1)
                    if m == 0:
                        dve.wait_ge(n_a, 3 * li + 1)
                        head_sums(sq, 0)
                    if m == 1:
                        head_mean_squares(li, 1, 0)
                    if m == 2:
                        head_scale(li, ob, 1)
                    if m == 3:
                        dve.wait_ge(*gone("roA", li))
                        dve.wait_ge(*gone("roB", li))
                        dve.wait_ge(n_v, N_NORM * li + 3)
                        head_sums(ob_r, 0)
                    if m == 4:
                        dve.wait_ge(n_v, N_NORM * li + 4)
                        dve.tensor_scalar(st4, st1, -1.0 / DV, None, ALU.mult).then_inc(n_v, 1)
                    if m == 5:
                        dve.wait_ge(n_v, N_NORM * li + 5)
                        v = ob_r.rearrange("p c (h v) -> p c h v", h=H)
                        dve.tensor_tensor(v, v, st4.rearrange("p (c h) -> p c h", c=3).unsqueeze(3).to_broadcast([P, 3, H, DV]),
                                          ALU.add).then_inc(n_v, 1)
                    if m == 6:
                        dve.wait_ge(n_a, 3 * li + 2)
                        head_sums(sq, 0)
                    if m == 7:
                        head_mean_squares(li, 7, 0)
                    if m == 8:
                        head_scale(li, ob_r, 2)
                    if m == 10:
                        dve.wait_ge(lam_v, 6)
                        for n in (6, 7):
                            dve.wait_ge(*gone("o", li, n))
                        dve.scalar_tensor_tensor(out=flat(o1[:, :, :]), in0=flat(o2[:, :, :]), scalar=lam[:, 4 + li:5 + li],
                                                 in1=flat(o1[:, :, :]), op0=ALU.mult, op1=ALU.add).then_inc(n_v, 1)
                    if m == 12:
                        dve.wait_ge(n_a, 3 * li + 3)
                        head_sums(sq, 0)
                    if m == 13:
                        head_mean_squares(li, 11, 0)
                    if m == 14:
                        head_scale(li, o1, 3)
                for k in (6, 7):
                    dve.wait_ge(*done("turn", li, k))
                    dve.tensor_scalar(oT[:, k, :], bank("turn", li, k)[:, 0:T], gain("diff", li), 1.0 - LAM_INIT[li],
                                      ALU.mult, ALU.mult).then_inc(taken_of("turn", li, k), 1)
                for k in range(KD):
                    dve.wait_ge(*done("wo", li, k))
                    dve.tensor_tensor(hT[:, k, :], hT[:, k, :], bank("wo", li, k)[:, 0:T], ALU.add).then_inc(taken_of("wo", li, k), 1)
                normalize(2 * li + 1)
                if li == 0:
                    for f in range(FT):
                        dve.wait_ge(*done("fu", f))
                        dve.wait_ge(*gone("fg", f))
                        dve.tensor_tensor(ffa[:, f, :], ffs[:, f % 2, :], bank("fu", f)[:, 0:T], ALU.mult).then_inc(taken_of("fu", f), 1)
                    for k in range(KD):
                        dve.wait_ge(*done("fd", k))
                        dve.tensor_tensor(hT[:, k, :], hT[:, k, :], bank("fd", k)[:, 0:T], ALU.add).then_inc(taken_of("fd", k), 1)

            for j in range(4):
                dve.wait_ge(*done("h_tok", j))
                dve.tensor_copy(h_tok[:, j // 2, FC * (j % 2):FC * (j % 2) + FC], bank("h_tok", j)).then_inc(taken_of("h_tok", j), 1)

            step = [0]

            def next_step(ins):
                step[0] += 1
                ins.then_inc(r_v, 1)
                dve.wait_ge(r_v, step[0])

            def rt(name, n): return route[:, R[name]:R[name] + n]
            def by(name, n=EXPERTS): return rt(name, 2 * n).rearrange("p (c e) -> p c e", c=2)
            def wide(a): return a.unsqueeze(2).to_broadcast([P, 2, EXPERTS])

            index = const("index").rearrange("p (c e) -> p c e", c=2)
            dve.wait_ge(*done("logits"))
            dve.tensor_copy(rt("logits", 16), bank("logits")[:, 0:16]).then_inc(taken_of("logits"), 1)
            dve.wait_ge(*gone("logits"))
            for n, src in enumerate(("logits", "rest")):
                next_step(dve.tensor_reduce(rt(f"max{n}", 2), by(src), AX.X, ALU.max))
                next_step(dve.tensor_tensor(by("tmp"), by(src), wide(rt(f"max{n}", 2)), ALU.is_equal))
                next_step(dve.scalar_tensor_tensor(out=rt("tmp", 16), in0=rt("tmp", 16), scalar=-float(EXPERTS), in1=const("index"),
                                                   op0=ALU.mult, op1=ALU.add))
                next_step(dve.tensor_reduce(rt("first", 2), by("tmp"), AX.X, ALU.min))
                next_step(dve.tensor_scalar(rt("first", 2), rt("first", 2), float(EXPERTS), None, ALU.add))
                next_step(dve.tensor_tensor(by(f"hot{n}"), index, wide(rt("first", 2)), ALU.is_equal))
                if n == 0:
                    next_step(dve.scalar_tensor_tensor(out=rt("rest", 16), in0=rt("hot0", 16), scalar=-3e38, in1=rt("logits", 16),
                                                       op0=ALU.mult, op1=ALU.add))
            next_step(dve.tensor_tensor(rt("d", 2), rt("max1", 2), rt("max0", 2), ALU.subtract))
            assert step[0] == R_EXP
            next_step(dve.tensor_tensor(rt("mask", 16), rt("hot0", 16), rt("hot1", 16), ALU.add))
            assert step[0] == R_MASK
            dve.wait_ge(r_a, 1)
            next_step(dve.tensor_scalar(rt("w0", 2), rt("e", 2), 1.0, None, ALU.add))
            next_step(dve.reciprocal(rt("w0", 2), rt("w0", 2)))
            next_step(dve.tensor_tensor(rt("w1", 2), rt("e", 2), rt("w0", 2), ALU.mult))
            next_step(dve.tensor_tensor(by("hot0"), by("hot0"), wide(rt("w0", 2)), ALU.mult))
            next_step(dve.tensor_tensor(by("hot1"), by("hot1"), wide(rt("w1", 2)), ALU.mult))
            gates, places = by("gates", ITEMS), by("places", ITEMS)
            next_step(dve.tensor_tensor(gates[:, :, 0:EXPERTS], by("hot0"), by("hot1"), ALU.add))
            dve.wait_ge(*done("pos"))
            dve.tensor_tensor(rt("tmp", 16), bank("pos")[:, 0:16], rt("mask", 16), ALU.mult).then_inc(taken_of("pos"), 1)
            dve.wait_ge(*gone("pos"))
            next_step(dve.tensor_scalar(places[:, :, 0:EXPERTS], by("tmp"), -1.0, None, ALU.add))
            dve.wait_ge(*done("count"))
            dve.tensor_scalar(rt("over", 8), bank("count")[:, 0:8], P + 0.5, None, ALU.is_gt).then_inc(taken_of("count"), 1)
            dve.wait_ge(*gone("count"))
            next_step(dve.tensor_tensor(rt("tmp64", 64).rearrange("p (a b) -> p a b", a=8), const("before").rearrange("p (a b) -> p a b", a=8),
                                        rt("over", 8).unsqueeze(1).to_broadcast([P, 8, 8]), ALU.mult))
            next_step(dve.tensor_reduce(rt("rank", 8), rt("tmp64", 64).rearrange("p (a b) -> p a b", a=8), AX.X, ALU.add))
            for n in range(OVER):
                pick = rt("pick", 8)
                next_step(dve.scalar_tensor_tensor(out=pick, in0=rt("rank", 8), scalar=float(n), in1=rt("over", 8),
                                                   op0=ALU.is_equal, op1=ALU.mult))
                for c in range(2):
                    next_step(dve.tensor_tensor_reduce(rt("tmp64", 8), gates[:, c, 0:EXPERTS], pick, 1.0, 0.0, ALU.mult, ALU.add,
                                                       gates[:, c, EXPERTS + n:EXPERTS + n + 1]))
                    next_step(dve.tensor_tensor_reduce(rt("tmp64", 8), places[:, c, 0:EXPERTS], pick, 1.0, 0.0, ALU.mult, ALU.add,
                                                       places[:, c, EXPERTS + n:EXPERTS + n + 1]))
                next_step(dve.tensor_tensor_reduce(rt("tmp64", 8), const("index")[:, 0:8], pick, 1.0, 0.0, ALU.mult, ALU.add,
                                                   rt("ctl", 4)[:, 1 + n:2 + n]))
            next_step(dve.tensor_scalar(places[:, :, EXPERTS:ITEMS], places[:, :, EXPERTS:ITEMS], -float(P), None, ALU.add))
            next_step(dve.tensor_reduce(rt("ctl", 1), rt("over", 8), AX.X, ALU.add))
            next_step(dve.tensor_scalar(rt("ctl", 1), rt("ctl", 1), float(EXPERTS), None, ALU.add))
            next_step(dve.tensor_copy(ctl[:, :], rt("ctl", 4)[0:1, :]))
            assert step[0] == N_ROUTE, step[0]

            def item(i):
                for c in range(2):
                    dve.wait_ge(*room_i(i, "selT"))
                    dve.tensor_scalar(sel[:, c, :], const("iota"), places[:, c, bass.ds(i, 1)], None, ALU.is_equal).then_inc(sel_v, 1)
                dve.wait_ge(*done_i(i, "selT"))
                dve.tensor_copy(flat(selT), bank("selT")[:, 0:256]).then_inc(taken_of("selT"), 1)
                for c in range(NFC):
                    dve.wait_ge(*done_i(i, "u", c))
                    dve.wait_ge(*gone_i(i, "g", c))
                    if c >= 2:
                        dve.wait_ge(*done_i(i, "aT", c - 2))
                    dve.tensor_tensor(act_sb[:, c % 2, :], sg[:, c % 2, :], bank("u", c), ALU.mult)\
                        .then_inc(taken_of("u", c), 1)
                dve.wait_ge(*done_i(i, "y", 1))
                dve.tensor_copy(ysb[:, FC:2 * FC], bank("y", 1)).then_inc(taken_of("y", 1), 1)
                for j in range(4):
                    c, half = j // 2, j % 2
                    hs = h_tok[:, c, FC * half:FC * half + FC]
                    dve.wait_ge(*done_i(i, "back", j))
                    dve.scalar_tensor_tensor(out=hs, in0=bank("back", j), scalar=gates[:, c, bass.ds(i, 1)], in1=hs,
                                             op0=ALU.mult, op1=ALU.add).then_inc(taken_of("back", j), 1)

            n_items = dve.value_load(ctl[0:1, 0:1], min_val=EXPERTS, max_val=ITEMS)
            with dve.Fori(0, ITEMS) as i:
                with dve.If(i < n_items):
                    item(i)
            dve.wait_ge(fin_a, 2)
            dve.tensor_scalar(st2[:, 0:2], st1[:, 0:2], 1.0 / D, EPS, ALU.mult, ALU.add).then_inc(fin_v, 1)
            dve.wait_ge(fin_p, 1)
            dve.wait_ge(gain_in, 16)
            for c in range(2):
                dve.scalar_tensor_tensor(out=out_sb[:, c, :], in0=h_tok[:, c, :], scalar=st3[:, c:c + 1], in1=fgain,
                                         op0=ALU.mult, op1=ALU.mult).then_inc(fin_v, 1)

        @block.gpsimd
        def _(pool):
            pool.memset(half_neg[:, :], -0.5).then_inc(filled, 1)
            pool.wait_ge(filled, 1)
            for li in range(LAYERS):
                for n, s in enumerate((2, 8, 12)):
                    pool.wait_ge(n_v, N_NORM * li + s)
                    pool.tensor_tensor(st3, st2, half_neg[:, :], ALU.pow).then_inc(n_p, 1)
            pool.wait_ge(fin_v, 1)
            pool.tensor_tensor(st3[:, 0:2], st2[:, 0:2], half_neg[:, 0:2], ALU.pow).then_inc(fin_p, 1)


N_NORM = 13
N_ROWS, N_PARAMS = 17, 7
LAM_INIT = [0.8 - 0.6 * float(np.exp(-0.3 * li)) for li in range(LAYERS)]
R_EXP, R_MASK, N_ROUTE = 14, 15, 46
R, _at = {}, 0
for _name, _n in (("logits", 16), ("rest", 16), ("tmp", 16), ("max0", 2), ("max1", 2), ("first", 2), ("hot0", 16), ("hot1", 16),
                  ("d", 2), ("e", 2), ("w0", 2), ("w1", 2), ("mask", 16), ("gates", 2 * ITEMS), ("places", 2 * ITEMS),
                  ("over", 8), ("rank", 8), ("pick", 8), ("tmp64", 64), ("ctl", 4)):
    R[_name] = _at
    _at += _n


_INS = ["x", "meta_tokens", "attn_norm", "w_in", "gla_w_gate", "gla_b_gate", "gla_norm", "ret_norm", "mla_q_norm",
        "mla_w_uq", "mla_kv_norm", "mla_w_ukv", "diff_lambda", "diff_norm", "w_out", "ffn_norm", "ffn_w_gate",
        "ffn_w_up", "ffn_w_down", "moe_router", "moe_w_gate", "moe_w_up", "moe_w_down", "final_norm"]


def kernel(**inputs):
    import numpy as _np
    import concourse.bacc as _bacc
    from concourse import mybir as _mybir
    from concourse.bass_utils import run_bass_kernel_spmd as _run

    nc = _bacc.Bacc("TRN2", target_bir_lowering=False, num_devices=1, dynamic_dma_scratch_size=1024)
    table, const_at = constants()
    arrays, args = {}, []
    for name in _INS:
        arrays[f"in_{name}_dram"] = _np.ascontiguousarray(inputs[name])
    arrays["in_consts_dram"] = table
    for name in _INS + ["consts"]:
        a = arrays[f"in_{name}_dram"]
        args.append(nc.dram_tensor(f"in_{name}_dram", a.shape, _mybir.dt.from_np(a.dtype), kind="ExternalInput").ap())
    args.append(nc.dram_tensor("out_0_dram", (1, SEQ, D), F32, kind="ExternalOutput").ap())
    hybrid_trunk(nc, *args, const_at)
    r = _run(nc, [arrays], core_ids=[0])
    return r.results[0]["out_0_dram"]
```

```python
from contextlib import ExitStack

import numpy as np
import concourse.bass as bass
from concourse import mybir

F32 = mybir.dt.float32
F32R = mybir.dt.float32r
I32 = mybir.dt.int32
ALU = mybir.AluOpType
ACT = mybir.ActivationFunctionType
AX = mybir.AxisListType

P = 128
D = 1024
KD = D // P
META = 16
SEQ = 256
T = META + SEQ
LAYERS = 2
EPS = 1e-6
NEG = -1e30
H = 4
DV = 64
GLA_DK = 32
GLA_TAU = 16.0
RET_DK = 64
NOPE, ROPE = 64, 32
MLA_DK = NOPE + ROPE
Q_RANK = 192
DIFF_DK = 32
CHUNK = 64
D_FF = 2816
F_EXP = 3584
EXPERTS = 8
FC = 512
LOAD = 2048
RING = 6
SPLIT = 3
OVER = (2 * SEQ) // (P + 1)
ITEMS = EXPERTS + OVER

WIDE = [slice(0, 128), slice(16, 144), slice(144, 272)]
ROWS = [META, P, P]

IN_LOADS = [
    (0, 256, [(0, 0), (1, 128)]),
    (256, 256, [(2, 0), (3, 128)]),
    (512, 144, [(4, 0), (5, 16)]),
    (656, 128, [(6, 0)]),
    (784, 256, [(7, 0), (8, 128)]),
    (1040, 256, [(9, 0), (10, 128)]),
    (1296, 256, [(11, 0), (12, 128)]),
    (1552, 256, [(13, 0), (14, 128)]),
    (1808, 128, [(15, 0)]),
    (1936, 192, [(16, 0), (17, 64)]),
    (2096, 256, [(18, 0), (19, 128)]),
    (2352, 256, [(20, 0), (21, 128)]),
    (2608, 256, [(22, 0), (23, 128)]),
]
PART = {4: slice(0, 16), 17: slice(64, 96)}
AQ, AK, AV, ALR, AOG, RQ, RK, RV, ROG, CQ, CKV, KPE, DQ, DK, DVT = 0, 1, 2, 4, 5, 7, 9, 11, 13, 15, 16, 17, 18, 20, 22
TILES = 24
FW = 256
FF_GROUPS = D_FF // FW
FT = D_FF // P
FF_ROWS = [8, 8, 6]
N_MAPS = 12
DIFF_MAPS = 8


def constants():
    parts, at = [], {}

    def put(name, a):
        full = np.zeros((P, a.shape[1]), np.float32)
        full[: a.shape[0]] = a
        at[name] = (sum(x.shape[1] for x in parts), a.shape[1])
        parts.append(full)

    p = np.arange(P)
    put("ident", np.eye(P))
    put("ones", np.ones((P, P)))
    half = RET_DK // 2
    swap = np.zeros((P, P))
    for m in range(P):
        if m % RET_DK < half:
            swap[m + half, m] = -1.0
        else:
            swap[m - half, m] = 1.0
    put("swap_ret", swap)
    half = ROPE // 2
    swap = np.zeros((P, ROPE))
    for m in range(ROPE):
        if m < half:
            swap[NOPE + m + half, m] = -1.0
        else:
            swap[NOPE + m - half, m] = 1.0
    put("swap_mla", swap)
    same = (p[:, None] // CHUNK == p[None, :] // CHUNK) & (p[:, None] <= p[None, :])
    put("cum", same / GLA_TAU)
    put("intra", same * 1.0)
    put("block", (p[:, None] // GLA_DK == np.arange(H * DV)[None, :] // DV) * 1.0)
    lg = np.log(1.0 - 2.0 ** (-5.0 - np.arange(H)))
    rel = np.arange(T)[None, :] - p[:, None]
    decay = [np.where(rel >= 0, np.exp(np.maximum(rel, 0) * lg[h]), 0.0) * RET_DK**-0.5 for h in range(H)]
    put("decay", np.concatenate(decay, axis=1))
    put("mask", np.where(np.arange(T)[None, :] <= META + P + p[:, None], 0.0, NEG))
    inv = 10000.0 ** (-(p % (RET_DK // 2)) / (RET_DK // 2))
    ang = np.arange(T)[None, :] * inv[:, None]
    put("cos_ret", np.cos(ang))
    put("sin_ret", np.sin(ang))
    inv = 10000.0 ** (-(p % (ROPE // 2)) / (ROPE // 2))
    ang = np.arange(T)[None, :] * inv[:, None]
    put("cos_mla", np.cos(ang))
    put("sin_mla", np.sin(ang))
    put("iota", np.broadcast_to(p[None, :], (P, P)))
    put("upper", (p[:, None] <= p[None, :]) * 1.0)
    e = np.arange(EXPERTS)
    put("index", np.broadcast_to(np.tile(e, 2)[None, :], (P, 2 * EXPERTS)))
    put("before", np.broadcast_to((e[None, :] < e[:, None]).reshape(1, -1), (P, EXPERTS**2)))
    return np.concatenate(parts, axis=1).astype(np.float32), at


class Results:

    def __init__(self):
        self.at, self.n = {}, [0] * 8

    def add(self, bank, *name):
        assert name not in self.at
        self.at[name] = (bank, self.n[bank])
        self.n[bank] += 1


TURNS = {3: (0, 1), 9: (2, 3)}


def plan_results():
    r = Results()
    turn = [0]

    def spread(*name):
        r.add(3 + turn[0] % 4, *name)
        turn[0] += 1

    for li in range(LAYERS):
        r.add(7, "ms", 2 * li)
        for n, (_, _, tiles) in enumerate(IN_LOADS):
            for t, _ in tiles:
                r.add(t % 3, "proj", li, t)
            if n == 3:
                spread("gate", li)
                spread("vA", li, 0)
                spread("vB", li, 0)
            if n in (6, 7):
                for j in (2 * n - 12, 2 * n - 11):
                    spread("swap", li, j)
            if n == 7:
                spread("vA", li, 1)
                spread("vB", li, 1)
            if n == 9:
                spread("cum", li)
            if n == 10:
                spread("cq", li)
                spread("ckv", li)
                spread("kswap", li)
        spread("vA", li, 2)
        spread("vB", li, 2)
        for h in range(H):
            spread("mq", li, h)
        for h in range(H):
            spread("mk", li, h)
        spread("mvA", li)
        spread("mvB", li)
        spread("kd", li)
        for h in range(H):
            spread("qswap", li, h)
        spread("upA", li)
        spread("upB", li)
        spread("upC", li)
        for h in range(H):
            r.add(h % 3, "gs", li, h)
        r.add(6, "goA", li)
        r.add(7, "goB", li)
        for h in range(H):
            r.add(h % 2, "rsM", li, h)
            r.add(2 + h % 2, "rsX", li, h)
        r.add(6, "roA", li)
        r.add(7, "roB", li)
        for m in range(N_MAPS + 3):
            if m < N_MAPS:
                r.add(m % 3, "sc", li, m)
            if 2 <= m < N_MAPS + 2:
                r.add(3 + m % 2, "ptX", li, m - 2)
                r.add(5, "ptM", li, m - 2)
            if 3 <= m:
                r.add(6 + m % 2, "o", li, m - 3)
            for k in TURNS.get(m, ()):
                r.add(3 + k % 2, "turn", li, k)
        for k in (4, 5, 6, 7):
            r.add(k - 4, "turn", li, k)
        for k in range(KD):
            r.add(k, "wo", li, k)
        r.add(7, "ms", 2 * li + 1)
        if li == 0:
            for f in range(FT):
                r.add(2 * (f % 3), "fg", f)
                r.add(2 * (f % 3) + 1, "fu", f)
            for k in range(KD):
                r.add((6, 7, 4, 5)[k % 4], "fd", k)
    for j in range(4):
        r.add(j, "h_tok", j)
        r.add(4 + j, "hn_tok", j)
    r.add(0, "logits")
    r.add(1, "pos")
    r.add(2, "count")
    base = list(r.n)
    for j in range(4):
        r.add(j, "xg", j)
    r.add(5, "selT")
    for c in range(F_EXP // FC):
        r.add(c % 2, "g", c)
        r.add(2 + c % 2, "u", c)
        r.add(4 + c % 2, "aT", c)
    r.add(6, "y", 0)
    r.add(7, "y", 1)
    for j in range(4):
        r.add(6 + j % 2, "back", j)
    return r, [n - b for n, b in zip(r.n, base)]


def hybrid_trunk(nc, w_in, w_out, ffn_w_gate, ffn_w_up, ffn_w_down, moe_w_gate, moe_w_up, moe_w_down, final_norm,
                 x_t, cols_t, params_t, router_t, consts, out, const_at):
    plan, PER_ITEM = plan_results()
    NFC = F_EXP // FC

    with ExitStack() as ctx:
        def sem(name):
            return ctx.enter_context(nc.semaphore(name))

        top = [nc.sbuf_base + (-nc.sbuf_base) % 32]

        def at(offset, name, *shape, dt=F32):
            return nc.alloc_sbuf_tensor_at(name, list(shape), dt, offset=offset)

        def new(name, *shape, dt=F32):
            offset = top[0]
            size = 4 * int(np.prod(shape[1:]))
            top[0] += size + (-size) % 32
            return at(offset, name, *shape, dt=dt)

        ring = new("ring", P, RING, LOAD)
        w_hi, w_lo = new("w_hi", P, SPLIT, LOAD, dt=F32R), new("w_lo", P, SPLIT, LOAD, dt=F32R)
        hT = new("hT", P, KD, T)
        hnT = new("hnT", P, KD, T)
        a_hi, a_lo = new("a_hi", P, KD, T, dt=F32R), new("a_lo", P, KD, T, dt=F32R)
        work = top[0]
        pr = new("pr", P, TILES, T)
        oT = new("oT", P, KD, T)
        va, vr, vd, vm = (new(n, P, 3, H * DV) for n in ("va", "vr", "vd", "vm"))
        pt = new("pt", P, 2, 768)
        probs = new("probs", P, 3, 432)
        ob = new("ob", P, 3, H * DV)
        sq = new("sq", P, 3, H * DV)
        work_end = top[0]
        cst = new("cst", P, consts.shape[1])
        cols = new("cols", P, 48)
        params = new("params", P, params_t.shape[2])
        small = new("small", P, 160)
        lam = new("lam", P, 8)
        half_neg = new("half_neg", P, 12)
        rms = new("rms", P, 2, T)
        wrout = new("wrout", P, KD, EXPERTS)
        ctl = new("ctl", 1, 4, dt=I32)
        assert top[0] <= nc.sbuf_usable_end, (top[0], nc.sbuf_usable_end)

        def over(name, *shape, dt=F32):
            offset = place[0]
            size = 4 * int(np.prod(shape[1:]))
            place[0] += size + (-size) % 32
            assert place[0] <= work_end
            return at(offset, name, *shape, dt=dt)

        place = [work]
        f_hi, f_lo = over("f_hi", P, FT, T, dt=F32R), over("f_lo", P, FT, T, dt=F32R)
        ffs, ffa = over("ffs", P, 2, T), over("ffa", P, 3, T)
        place = [work]
        hn_hi, hn_lo = over("hn_hi", P, 2, D, dt=F32R), over("hn_lo", P, 2, D, dt=F32R)
        h_tok = over("h_tok", P, 2, D)
        x_hi, x_lo = over("x_hi", P, D, dt=F32R), over("x_lo", P, D, dt=F32R)
        act_sb = over("act_sb", P, 2, FC)
        act_hi, act_lo = over("act_hi", P, 2, FC, dt=F32R), over("act_lo", P, 2, FC, dt=F32R)
        y_hi, y_lo = over("y_hi", P, D, dt=F32R), over("y_lo", P, D, dt=F32R)
        sg = over("sg", P, 2, FC)
        sel, selT = over("sel", P, 2, P, dt=F32R), over("selT", P, 2, P, dt=F32R)
        banks = [ctx.enter_context(nc.psum_tensor(f"bank{b}", [P, FC], F32))[:, :] for b in range(8)]

        def const(name):
            a, n = const_at[name]
            return cst[:, a:a + n]

        ident, ones = const("ident"), const("ones")
        decay = const("decay").rearrange("p (h t) -> p h t", h=H)
        mask = const("mask")

        def gain(kind, li, k=0):
            j = {"attn": KD * li + k, "ffn": 16 + KD * li + k, "q": 32 + li, "q_kv": 34 + li,
                 "gla": 36 + li, "ret": 38 + li, "diff": 40 + li}[kind]
            return cols[:, j:j + 1]

        def param(name):
            a, n = PARAMS[name]
            return params[:, a:a + n]

        def flat(a): return a.rearrange("p a b -> p (a b)")
        cumT, eq, ek, ekd, kdT, t1, t2 = (oT[:, j, :] for j in range(7))
        gx, gabs = pt[:, 0, 0:384], pt[:, 1, 0:384]
        kd_tok = probs[:, 0, 0:384]
        s01, s23 = flat(pr[:, 2:4, :]), flat(pr[:, 11:13, :])
        state = [s01[:, 0:256], s01[:, 256:512], s23[:, 0:256], s23[:, 256:512]]
        qc, kc = hnT[:, 0:4, :], hnT[:, 4:8, :]
        ob_r = flat(pr[:, 9:12, :])[:, 0:768].rearrange("p (c v) -> p c v", c=3)
        o1, o2, om = va, vr, ob
        neg_max, den, rden = (small[:, 36 * j:36 * j + 36].rearrange("p (m c) -> p m c", c=3) for j in range(3))
        st1, st2, st3, st4 = (small[:, 108 + 12 * j:120 + 12 * j] for j in range(4))
        hnf = flat(hnT[:, :, :])
        route, fgain = hnf[:, 0:512], hnf[:, 1024:2048]
        out_sb = flat(hT[:, :, :])[:, 0:2048].rearrange("p (c d) -> p c d", c=2)

        made = [sem(f"made{b}") for b in range(8)]
        taken = [sem(f"taken{b}") for b in range(8)]
        landed = [sem(f"landed{s}") for s in range(RING)]
        x_in = sem("x_in")
        tables_in = sem("tables_in")
        params_in = sem("params_in")
        gain_in = sem("gain_in")
        filled = sem("filled")
        hi_a = sem("hi_a")
        lo_v = sem("lo_v")
        part_used = sem("part_used")
        sq_a = sem("sq_a")
        rms_a = sem("rms_a")
        rstd_v = sem("rstd_v")
        hn_v = sem("hn_v")
        ahi_a = sem("ahi_a")
        alo_v = sem("alo_v")
        ff_a, ff_v = sem("ff_a"), sem("ff_v")
        lam_v, lam_a = sem("lam_v"), sem("lam_a")
        gate_a = sem("gate_a")
        gla_v = sem("gla_v")
        cum_a = sem("cum_a")
        rot_v = sem("rot_v")
        c_a, c_v = sem("c_a"), sem("c_v")
        rk_v, rq_v = sem("rk_v"), sem("rq_v")
        st_v = sem("st_v")
        map_used = sem("map_used")
        exp_a = sem("exp_a")
        rd_v = sem("rd_v")
        n_v, n_a, n_p = sem("n_v"), sem("n_a"), sem("n_p")
        r_v, r_a = sem("r_v"), sem("r_a")
        tok_a = sem("tok_a")
        sel_v = sem("sel_v")
        part_a = sem("part_a")
        fin_v, fin_a, fin_p = sem("fin_v"), sem("fin_a"), sem("fin_p")
        stored = sem("stored")

        def bank(*name):
            return banks[plan.at[name][0]]

        def room(*name):
            b, n = plan.at[name]
            return taken[b], n

        def done(*name):
            b, n = plan.at[name]
            return made[b], n + 1

        def gone(*name):
            b, n = plan.at[name]
            return taken[b], n + 1

        def made_of(*name):
            return made[plan.at[name][0]]

        def taken_of(*name):
            return taken[plan.at[name][0]]

        def room_i(i, *name, before=0):
            b, n = plan.at[name]
            return taken[b], i * PER_ITEM[b] + (n - before * PER_ITEM[b])

        def done_i(i, *name, before=0):
            b, n = plan.at[name]
            return made[b], i * PER_ITEM[b] + (n + 1 - before * PER_ITEM[b])

        def gone_i(i, *name, before=0):
            b, n = plan.at[name]
            return taken[b], i * PER_ITEM[b] + (n + 1 - before * PER_ITEM[b])

        LO_LAYER = 3 * KD - 2

        def stream(v, k):
            return [None, ("wo", 0, k), ("fd", k), ("wo", 1, k)][v]

        PER_LAYER = len(IN_LOADS) + 4
        N_FF = 2 * FF_GROUPS + 4 * len(FF_ROWS)
        MOE0 = 2 * PER_LAYER + N_FF
        PER_EXPERT = 6 * NFC
        assert PER_EXPERT % RING == 0 and PER_EXPERT % SPLIT == 0

        def load_in(li, n): return li * (PER_LAYER + N_FF) + n
        def load_out(li, n): return load_in(li, len(IN_LOADS) + n)
        def load_gate(c): return PER_LAYER + 2 * c
        def load_up(c): return PER_LAYER + 2 * c + 1
        def load_down(pair, j): return PER_LAYER + 2 * FF_GROUPS + len(FF_ROWS) * pair + j

        ITEM = []
        for c in range(NFC):
            ITEM += [(w, c, j) for w in ("g", "u") for j in range(2)]
            ITEM += [("d", c - 1, j) for j in range(2)] if c else []
        ITEM += [("d", NFC - 1, j) for j in range(2)]

        def ends_i(n):
            w, c, j = ITEM[n]
            if w == "d":
                return ("y", 1) if (c, j) == (NFC - 1, 1) else None
            return (w, c) if j else None

        PA_Y, PA = NFC, NFC + 2

        def turned_after(w, c, j):
            if w == "u" and j == 0 and c:
                return c - 1
            return NFC - 1 if (w, c, j) == ("d", NFC - 2, 1) else None

        BACK, SEL_TURN = {2: (0, 1), 4: (2, 3)}, 5

        PARTS_I = sum(ends_i(n) is None for n in range(PER_EXPERT))

        def ends(n):
            for li in range(LAYERS):
                if load_in(li, 0) <= n < load_out(li, 0):
                    return ("proj", li, IN_LOADS[n - load_in(li, 0)][2][-1][0])
                if load_out(li, 0) <= n < load_out(li, 4):
                    return ("wo", li, 2 * (n - load_out(li, 0)) + 1)
            if n < load_down(0, 0):
                return ("fu" if (n - PER_LAYER) % 2 else "fg", 2 * ((n - PER_LAYER) // 2) + 1)
            pair, j = divmod(n - load_down(0, 0), len(FF_ROWS))
            return ("fd", 2 * pair + 1) if j == len(FF_ROWS) - 1 else None

        PARTS = sum(ends(n) is None for n in range(MOE0))

        def ready(n):
            return (hi_a, n + 1), (lo_v, n + 1)

        def ready_i(i, n):
            return (hi_a, i * PER_EXPERT + (MOE0 + n + 1)), (lo_v, i * PER_EXPERT + (MOE0 + n + 1))

        def used(n):
            if ends(n) is None:
                return part_used, sum(ends(m) is None for m in range(n + 1))
            return done(*ends(n))

        def used_i(i, n, before=0):
            if ends_i(n) is None:
                return part_used, i * PARTS_I + (PARTS + sum(ends_i(m) is None for m in range(n + 1)) - before * PARTS_I)
            return done_i(i, *ends_i(n), before=before)

        def width(n):
            for li in range(LAYERS):
                if load_in(li, 0) <= n < load_out(li, 0):
                    return KD * IN_LOADS[n - load_in(li, 0)][1]
            if load_down(0, 0) <= n < load_down(4, 0):
                return FW * FF_ROWS[(n - load_down(0, 0)) % len(FF_ROWS)]
            return LOAD

        def split_hi(act, n):
            a = slice(0, width(n))
            act.wait_ge(landed[n % RING], 16 * (n // RING + 1))
            if n >= SPLIT:
                act.wait_ge(*used(n - SPLIT))
            act.activation(w_hi[:, n % SPLIT, a], ring[:, n % RING, a], ACT.Copy).then_inc(hi_a, 1)

        def split_lo(dve, n):
            a = slice(0, width(n))
            dve.wait_ge(hi_a, n + 1)
            dve.tensor_tensor(w_lo[:, n % SPLIT, a], ring[:, n % RING, a], w_hi[:, n % SPLIT, a].bitcast(F32), ALU.subtract)\
                .then_inc(lo_v, 1)

        def split_hi_i(act, i, n):
            m = MOE0 + n
            act.wait_ge(landed[m % RING], i * (16 * PER_EXPERT // RING) + 16 * (m // RING + 1))
            act.wait_ge(*(used_i(i, n - SPLIT) if n >= SPLIT else used_i(i, n - SPLIT + PER_EXPERT, before=1)))
            act.activation(w_hi[:, m % SPLIT, :], ring[:, m % RING, :], ACT.Copy).then_inc(hi_a, 1)

        def split_lo_i(dve, i, n):
            m = MOE0 + n
            dve.wait_ge(hi_a, i * PER_EXPERT + (m + 1))
            dve.tensor_tensor(w_lo[:, m % SPLIT, :], ring[:, m % RING, :], w_hi[:, m % SPLIT, :].bitcast(F32), ALU.subtract)\
                .then_inc(lo_v, 1)

        block = ctx.enter_context(nc.Block())

        @block.sync
        def _(sp):
            sp.dma_start(hT[:, :, :], x_t).then_inc(x_in, 16)
            sp.dma_start(cols[:, :], cols_t).then_inc(tables_in, 16)
            sp.dma_start(cst[:, :], consts).then_inc(tables_in, 16)

            def load(n, k, f, src):
                if n >= RING:
                    sp.wait_ge(lo_v, n - RING + 1)
                sp.dma_start(ring[:, n % RING, 0:k * f].rearrange("p (k f) -> p k f", k=k),
                             src.rearrange("(k p) f -> p k f", p=P)).then_inc(landed[n % RING], 16)

            for li in range(LAYERS):
                for n, (c0, w, _) in enumerate(IN_LOADS):
                    load(load_in(li, n), KD, w, w_in[li, :, c0:c0 + w])
                    if li == 0 and n == 1:
                        sp.dma_start(wrout[:, :, :], router_t).then_inc(tables_in, 16)
                        sp.dma_start(params[:, :], params_t[0]).then_inc(params_in, 16)
                for n in range(4):
                    load(load_out(li, n), KD, FW, w_out[li, :, FW * n:FW * n + FW])
                if li == 0:
                    sp.wait_ge(*done("mvB", 0))
                    sp.dma_start(params[:, :], params_t[1]).then_inc(params_in, 16)
                    for c in range(FF_GROUPS):
                        load(load_gate(c), KD, FW, ffn_w_gate[0, :, FW * c:FW * c + FW])
                        load(load_up(c), KD, FW, ffn_w_up[0, :, FW * c:FW * c + FW])
                    for pair in range(4):
                        for j, nt in enumerate(FF_ROWS):
                            load(load_down(pair, j), nt, FW,
                                 ffn_w_down[0, 8 * P * j:8 * P * j + P * nt, FW * pair:FW * pair + FW])

            views = {
                "g": moe_w_gate[0].rearrange("e (j k p) f -> e j p k f", j=2, p=P),
                "u": moe_w_up[0].rearrange("e (j k p) f -> e j p k f", j=2, p=P),
                "d": moe_w_down[0].rearrange("e (c j p r) d -> e (c j) p (r d)", j=2, p=P, r=2),
            }

            def item(i, e, first):
                for n, (w, c, j) in enumerate(ITEM):
                    m = MOE0 + n
                    if first:
                        sp.wait_ge(lo_v, m - RING + 1)
                    else:
                        sp.wait_ge(lo_v, i * PER_EXPERT + (m - RING + 1))
                    if w == "d":
                        src = views[w][bass.ds(e, 1), 2 * c + j, :, :].rearrange("e p x -> (e p) x")
                        dst = ring[:, m % RING, :]
                    else:
                        src = views[w][bass.ds(e, 1), j, :, :, FC * c:FC * c + FC].rearrange("e p k f -> (e p) k f")
                        dst = ring[:, m % RING, :].rearrange("p (k f) -> p k f", k=4)
                    sp.dma_start(dst, src).then_inc(landed[m % RING], 16)

            item(0, 0, True)
            sp.wait_ge(*done("logits"))
            sp.dma_start(fgain, final_norm.partition_broadcast(P)).then_inc(gain_in, 16)
            with sp.Fori(1, EXPERTS) as e:
                item(e, e, False)
            sp.wait_ge(r_v, N_ROUTE)
            n_items = sp.value_load(ctl[0:1, 0:1], min_val=EXPERTS, max_val=ITEMS)
            with sp.Fori(EXPERTS, ITEMS) as i:
                with sp.If(i < n_items):
                    e = sp.value_load(ctl[0:1, bass.ds(i - (EXPERTS - 1), 1)], min_val=0, max_val=EXPERTS - 1)
                    item(i, e, False)
            sp.wait_ge(fin_v, 3)
            sp.dma_start(out[0].rearrange("(c p) d -> p c d", p=P), out_sb).then_inc(stored, 16)
            sp.wait_ge(stored, 16)

        @block.tensor
        def _(pe):
            def mm(o, lhsT, rhs, first, end, **kw):
                return pe.matmul(o, lhsT, rhs, start=first, stop=end, **kw)

            def exact(o, a, b, first, end, **kw):
                (a_h, a_l), (b_h, b_l) = a, b
                pe.matmul(o, a_h, b_h, start=first, stop=False, **kw)
                pe.matmul(o, a_h, b_l, start=False, stop=False, **kw)
                return pe.matmul(o, a_l, b_h, start=False, stop=end, **kw)

            def parts_of_load(n, at):
                return w_hi[:, n % SPLIT, at], w_lo[:, n % SPLIT, at]

            pe.wait_ge(tables_in, 16 * 3)

            def mean_squares(r):
                pe.wait_ge(*room("ms", r))
                for k in range(KD):
                    pe.wait_ge(sq_a, KD * r + k + 1)
                    i = mm(bank("ms", r)[:, 0:T], ones, hnT[:, k, :], k == 0, k == KD - 1)
                i.then_inc(made_of("ms", r), 1)

            def turn_values(li, tile, n):
                pe.wait_ge(*gone("proj", li, tile))
                pe.wait_ge(*gone("proj", li, tile + 1))
                pe.wait_ge(*room("vA", li, n))
                for c in range(2):
                    for j in range(2):
                        i = pe.transpose(bank("vA", li, n)[:, 256 * c + 128 * j:256 * c + 128 * j + 128],
                                         pr[:, tile + j, WIDE[c]], ident)
                i.then_inc(made_of("vA", li, n), 1)
                pe.wait_ge(*room("vB", li, n))
                for j in range(2):
                    i = pe.transpose(bank("vB", li, n)[:, 128 * j:128 * j + 128], pr[:, tile + j, WIDE[2]], ident)
                i.then_inc(made_of("vB", li, n), 1)

            def turn_output(li, k, src):
                b = bank("turn", li, k)
                f = slice(P * (k % 2), P * (k % 2) + P)
                pe.wait_ge(*room("turn", li, k))
                pe.transpose(b[:, 0:META], src[0:META, 0, f], ident[0:META, 0:META])
                pe.transpose(b[:, WIDE[1]], src[:, 1, f], ident)
                pe.transpose(b[:, WIDE[2]], src[:, 2, f], ident).then_inc(made_of("turn", li, k), 1)

            for li in range(LAYERS):
                mean_squares(2 * li)
                for n, (_, w, tiles) in enumerate(IN_LOADS):
                    m = load_in(li, n)
                    for wait in ready(m):
                        pe.wait_ge(*wait)
                    for t, c0 in tiles:
                        pe.wait_ge(*room("proj", li, t))
                        for k in range(KD):
                            if t == 0:
                                pe.wait_ge(ahi_a, KD * 3 * li + k + 1)
                                pe.wait_ge(alo_v, LO_LAYER * li + k + 1)
                            at_ = slice(w * k + c0, w * k + c0 + P)
                            i = exact(bank("proj", li, t)[:, 0:T], parts_of_load(m, at_), (a_hi[:, k, :], a_lo[:, k, :]),
                                      k == 0, k == KD - 1)
                        i.then_inc(made_of("proj", li, t), 1)
                    if n == 3:
                        pe.wait_ge(params_in, 16 * (li + 1))
                        pe.wait_ge(*gone("proj", li, ALR))
                        pe.wait_ge(*room("gate", li))
                        for c in range(3):
                            i = mm(bank("gate", li)[:, P * c:P * c + P], pr[0:META, ALR, WIDE[c]], param('wgate')[0:META, :], True, True)
                        i.then_inc(made_of("gate", li), 1)
                        turn_values(li, AV, 0)
                    if n in (6, 7):
                        for j in (2 * n - 12, 2 * n - 11):
                            pe.wait_ge(*gone("proj", li, RQ + j))
                            pe.wait_ge(*room("swap", li, j))
                            mm(bank("swap", li, j)[:, 0:T], const("swap_ret"), pr[:, RQ + j, :], True, True)\
                                .then_inc(made_of("swap", li, j), 1)
                    if n == 7:
                        turn_values(li, RV, 1)
                    if n == 9:
                        pe.wait_ge(gla_v, 5 * li + 2)
                        pe.wait_ge(*room("cum", li))
                        for c in range(3):
                            a = (0, META, META + P)[c]
                            i = mm(bank("cum", li)[:, a:a + ROWS[c]], gx[0:ROWS[c], P * c:P * c + P],
                                   const("cum")[0:ROWS[c], 0:ROWS[c]], True, True)
                        i.then_inc(made_of("cum", li), 1)
                    if n == 10:
                        pe.wait_ge(c_a, 4 * li + 2)
                        pe.wait_ge(*room("cq", li))
                        mm(bank("cq", li)[:, 0:T], ones, rms[:, 0, :], True, False)
                        mm(bank("cq", li)[:, 0:T], ones[0:64, :], rms[0:64, 1, :], False, True).then_inc(made_of("cq", li), 1)
                        pe.wait_ge(*room("ckv", li))
                        mm(bank("ckv", li)[:, 0:T], ones[64:128, :], rms[64:128, 1, :], True, True).then_inc(made_of("ckv", li), 1)
                        pe.wait_ge(*gone("proj", li, KPE))
                        pe.wait_ge(*room("kswap", li))
                        mm(bank("kswap", li)[64:96, 0:T], const("swap_mla")[64:96, :], pr[64:96, KPE, :], True, True)\
                            .then_inc(made_of("kswap", li), 1)
                turn_values(li, DVT, 2)

                pe.wait_ge(c_v, 5 * li + 4)
                for h in range(H):
                    hs = slice(MLA_DK * h, MLA_DK * h + MLA_DK)
                    pe.wait_ge(*room("mq", li, h))
                    mm(bank("mq", li, h)[0:MLA_DK, 0:T], param('wuq0')[:, hs], pr[:, CQ, :], True, False)
                    mm(bank("mq", li, h)[0:MLA_DK, 0:T], param('wuq1')[0:64, hs], pr[0:64, CKV, :], False, True)\
                        .then_inc(made_of("mq", li, h), 1)
                pe.wait_ge(c_v, 5 * li + 5)
                for h in range(H):
                    pe.wait_ge(*room("mk", li, h))
                    mm(bank("mk", li, h)[0:NOPE, 0:T], param('wukv')[64:128, P * h:P * h + NOPE], pr[64:128, CKV, :], True, True)\
                        .then_inc(made_of("mk", li, h), 1)
                wv = param('wukv')[64:128, :].rearrange("p (h c) -> p h c", h=H)[:, :, NOPE:NOPE + DV]
                pe.wait_ge(*room("mvA", li))
                for c in range(2):
                    i = mm(bank("mvA", li)[:, 256 * c:256 * c + 256], pr[64:128, CKV, WIDE[c]], wv, True, True)
                i.then_inc(made_of("mvA", li), 1)
                pe.wait_ge(*room("mvB", li))
                mm(bank("mvB", li)[:, 0:256], pr[64:128, CKV, WIDE[2]], wv, True, True).then_inc(made_of("mvB", li), 1)

                pe.wait_ge(gla_v, 5 * li + 4)
                pe.wait_ge(*room("kd", li))
                for c, (a, q) in enumerate(((0, META), (META, P), (META + P, CHUNK))):
                    i = pe.transpose(bank("kd", li)[0:q, P * c:P * c + P], kdT[:, a:a + q], ident)
                i.then_inc(made_of("kd", li), 1)
                for h in range(H):
                    pe.wait_ge(*gone("mq", li, h))
                    pe.wait_ge(*room("qswap", li, h))
                    mm(bank("qswap", li, h)[64:96, 0:T], const("swap_mla")[64:96, :], qc[64:96, h, :], True, True)\
                        .then_inc(made_of("qswap", li, h), 1)
                pe.wait_ge(*gone("kd", li))
                pe.wait_ge(*gone("vA", li, 0))
                pe.wait_ge(*gone("vB", li, 0))
                for name, parts in (("upA", ((0, 0, META), (1, 0, CHUNK))), ("upB", ((1, CHUNK, CHUNK),)), ("upC", ((2, 0, CHUNK),))):
                    pe.wait_ge(*room(name, li))
                    for j, (c, p0, q) in enumerate(parts):
                        i = mm(bank(name, li)[:, 256 * j:256 * j + 256], kd_tok[p0:p0 + q, P * c:P * c + P],
                               va[p0:p0 + q, c, :], True, True)
                    i.then_inc(made_of(name, li), 1)
                pe.wait_ge(gla_v, 5 * li + 5)
                for h in range(H):
                    d = slice(GLA_DK * h, GLA_DK * h + GLA_DK)
                    pe.wait_ge(*room("gs", li, h))
                    for j, c in enumerate((1, 2, 0)):
                        i = mm(bank("gs", li, h)[:, P * j:P * j + P], pr[d, AK, WIDE[c]], pr[d, AQ, WIDE[c]], True, True,
                               tile_position=(GLA_DK * h, 0))
                    i.then_inc(made_of("gs", li, h), 1)
                oa, ol = bank("goA", li), bank("goB", li)
                pe.wait_ge(*room("goA", li))
                pe.wait_ge(*room("goB", li))
                for h in range(H):
                    hs, ho = slice(DV * h, DV * h + DV), slice(256 + DV * h, 256 + DV * h + DV)
                    mp = pt[:, h % 2, :]
                    pe.wait_ge(*gone("gs", li, h))
                    mm(oa[:, hs], mp[0:META, 256:384], va[0:META, 0, hs], h == 0, False, skip_group_check=True)
                    mm(oa[:, ho], mp[:, 0:128], va[:, 1, hs], False, False, skip_group_check=True)
                    mm(ol[:, hs], mp[:, 128:256], va[:, 2, hs], h == 0, False, skip_group_check=True).then_inc(map_used, 1)
                pe.wait_ge(st_v, 4 * li + 4)
                mm(oa[0:64, 256:512], pr[:, AQ, 16:80], state[0], False, False, skip_group_check=True)
                mm(oa[64:128, 256:512], pr[:, AQ, 80:144], state[1], False, True, skip_group_check=True)\
                    .then_inc(made_of("goA", li), 1)
                mm(ol[0:64, 0:256], pr[:, AQ, 144:208], state[2], False, False, skip_group_check=True)
                mm(ol[64:128, 0:256], pr[:, AQ, 208:272], state[3], False, True, skip_group_check=True)\
                    .then_inc(made_of("goB", li), 1)

                pe.wait_ge(rot_v, 8 * li + 8)
                for h in range(H):
                    d = slice(RET_DK * (h % 2), RET_DK * (h % 2) + RET_DK)
                    qt, kt = pr[d, RQ + h // 2, :], pr[d, RK + h // 2, :]
                    pe.wait_ge(*room("rsM", li, h))
                    mm(bank("rsM", li, h)[0:META, 0:T], kt[:, 0:META], qt, True, True).then_inc(made_of("rsM", li, h), 1)
                    pe.wait_ge(*room("rsX", li, h))
                    b = bank("rsX", li, h)
                    mm(b[:, 0:256], kt[:, WIDE[1]], qt[:, META:T], True, True)
                    mm(b[:, 256:384], kt[:, WIDE[2]], qt[:, WIDE[2]], True, True).then_inc(made_of("rsX", li, h), 1)
                oa, ol = bank("roA", li), bank("roB", li)
                pe.wait_ge(*gone("vA", li, 1))
                pe.wait_ge(*gone("vB", li, 1))
                pe.wait_ge(*room("roA", li))
                pe.wait_ge(*room("roB", li))
                for h in range(H):
                    hs, ho = slice(DV * h, DV * h + DV), slice(256 + DV * h, 256 + DV * h + DV)
                    mp = pt[:, h % 2, :]
                    mk = mp[0:META, 384:384 + T]
                    vmeta = vr[0:META, 0, hs]
                    pe.wait_ge(*gone("rsM", li, h))
                    pe.wait_ge(*gone("rsX", li, h))
                    mm(oa[:, hs], mk[:, WIDE[0]], vmeta, True, True, skip_group_check=True)
                    mm(oa[:, ho], mk[:, WIDE[1]], vmeta, True, False, skip_group_check=True)
                    i = mm(oa[:, ho], mp[:, 0:128], vr[:, 1, hs], False, True, skip_group_check=True)
                    if h == H - 1:
                        i.then_inc(made_of("roA", li), 1)
                    mm(ol[:, hs], mk[:, WIDE[2]], vmeta, True, False, skip_group_check=True)
                    mm(ol[:, hs], mp[:, 128:256], vr[:, 1, hs], False, False, skip_group_check=True)
                    i = mm(ol[:, hs], mp[:, 256:384], vr[:, 2, hs], False, True, skip_group_check=True)
                    i.then_inc(made_of("roB", li) if h == H - 1 else map_used, 1)

                def scores(m):
                    b = bank("sc", li, m)
                    if m < DIFF_MAPS:
                        d = slice(DIFF_DK * (m % 4), DIFF_DK * (m % 4) + DIFF_DK)
                        q, k = pr[d, DQ + m // 4, :], pr[d, DK + m // 4, :]
                        kw = {"tile_position": (DIFF_DK * (m % 4), 0)}
                    else:
                        q, k, kw = qc[0:MLA_DK, m - DIFF_MAPS, :], kc[0:MLA_DK, m - DIFF_MAPS, :], {}
                    if m == 0:
                        pe.wait_ge(*gone("proj", li, DK + 1))
                    if m == DIFF_MAPS:
                        pe.wait_ge(*gone("mk", li, H - 1))
                        pe.wait_ge(rk_v, 2 * li + 2)
                        pe.wait_ge(rq_v, 8 * li + 8)
                    pe.wait_ge(*room("sc", li, m))
                    mm(b[:, 0:T], q[:, WIDE[2]], k, True, True, **kw)
                    mm(b[:, T:T + 144], q[:, WIDE[1]], k[:, 0:144], True, True, **kw)
                    mm(b[:, T + 144:T + 160], q[:, WIDE[0]], k[:, 0:META], True, True, **kw).then_inc(made_of("sc", li, m), 1)

                def turn_map(m):
                    pb = probs[:, m % 3, :]
                    pe.wait_ge(exp_a, N_MAPS * li + m + 1)
                    pe.wait_ge(*room("ptX", li, m))
                    b = bank("ptX", li, m)
                    pe.transpose(b[:, 0:128], pb[:, T + META:T + 144], ident)
                    pe.transpose(b[:, 128:256], pb[:, WIDE[1]], ident)
                    pe.transpose(b[:, 256:384], pb[:, WIDE[2]], ident).then_inc(made_of("ptX", li, m), 1)
                    pe.wait_ge(*room("ptM", li, m))
                    b = bank("ptM", li, m)
                    pe.transpose(b[0:META, 0:128], pb[:, T:T + META], ident)
                    pe.transpose(b[0:META, 128:256], pb[:, 0:META], ident)
                    pe.transpose(b[0:META, 256:384], pb[:, T + 144:T + 160], ident).then_inc(made_of("ptM", li, m), 1)

                def output(m):
                    v, h = (vd, m // 2) if m < DIFF_MAPS else (vm, m - DIFF_MAPS)
                    hs = slice(DV * h, DV * h + DV)
                    mp, b = pt[:, m % 2, :], bank("o", li, m)
                    if m == 0:
                        pe.wait_ge(*gone("vA", li, 2))
                        pe.wait_ge(*gone("vB", li, 2))
                    if m == DIFF_MAPS:
                        pe.wait_ge(*gone("mvA", li))
                        pe.wait_ge(*gone("mvB", li))
                    pe.wait_ge(*gone("ptX", li, m))
                    pe.wait_ge(*gone("ptM", li, m))
                    pe.wait_ge(*room("o", li, m))
                    mm(b[:, 0:64], mp[0:META, 640:768], v[0:META, 0, hs], True, True)
                    mm(b[:, 64:128], mp[0:META, 384:512], v[0:META, 0, hs], True, False)
                    mm(b[:, 64:128], mp[:, 0:128], v[:, 1, hs], False, True)
                    mm(b[:, 128:192], mp[0:META, 512:640], v[0:META, 0, hs], True, False)
                    mm(b[:, 128:192], mp[:, 128:256], v[:, 1, hs], False, False)
                    mm(b[:, 128:192], mp[:, 256:384], v[:, 2, hs], False, True).then_inc(made_of("o", li, m), 1)

                for m in range(N_MAPS + 3):
                    if m < N_MAPS:
                        scores(m)
                    if 2 <= m < N_MAPS + 2:
                        turn_map(m - 2)
                    if m >= 3:
                        output(m - 3)
                    if m in TURNS:
                        pe.wait_ge(n_v, N_NORM * li + (3 if m == 3 else 9))
                        for k in TURNS[m]:
                            turn_output(li, k, ob if m == 3 else ob_r)
                pe.wait_ge(*gone("o", li, N_MAPS - 1))
                for k in (4, 5):
                    turn_output(li, k, om)
                pe.wait_ge(n_v, N_NORM * li + N_NORM)
                for k in (6, 7):
                    turn_output(li, k, o1)

                for k in range(KD):
                    m = load_out(li, k // 2)
                    for wait in ready(m):
                        pe.wait_ge(*wait)
                    pe.wait_ge(*room("wo", li, k))
                    for j in range(KD):
                        if k == 0:
                            pe.wait_ge(ahi_a, KD * (3 * li + 1) + j + 1)
                            if j in (4, 5):
                                pe.wait_ge(*gone("turn", li, j))
                            else:
                                pe.wait_ge(alo_v, LO_LAYER * li + KD + (j + 1 if j < 4 else j - 1))
                        at_ = slice(FW * j + P * (k % 2), FW * j + P * (k % 2) + P)
                        i = exact(bank("wo", li, k)[:, 0:T], parts_of_load(m, at_), (a_hi[:, j, :], a_lo[:, j, :]),
                                  j == 0, j == KD - 1)
                    i.then_inc(made_of("wo", li, k), 1)
                mean_squares(2 * li + 1)

                if li == 0:
                    for c in range(FF_GROUPS):
                        for name, m in (("fg", load_gate(c)), ("fu", load_up(c))):
                            for wait in ready(m):
                                pe.wait_ge(*wait)
                            for f in (2 * c, 2 * c + 1):
                                pe.wait_ge(*room(name, f))
                                for k in range(KD):
                                    if f == 0 and name == "fg":
                                        pe.wait_ge(ahi_a, KD * 2 + k + 1)
                                        pe.wait_ge(alo_v, 2 * KD - 2 + k + 1)
                                    at_ = slice(FW * k + P * (f % 2), FW * k + P * (f % 2) + P)
                                    i = exact(bank(name, f)[:, 0:T], parts_of_load(m, at_), (a_hi[:, k, :], a_lo[:, k, :]),
                                              k == 0, k == KD - 1)
                                i.then_inc(made_of(name, f), 1)
                    for pair in range(4):
                        for j, nt in enumerate(FF_ROWS):
                            m = load_down(pair, j)
                            for wait in ready(m):
                                pe.wait_ge(*wait)
                            for k in (2 * pair, 2 * pair + 1):
                                if j == 0:
                                    pe.wait_ge(*room("fd", k))
                                for ft in range(nt):
                                    f = 8 * j + ft
                                    if k == 0:
                                        pe.wait_ge(ff_a, f + 1)
                                        pe.wait_ge(ff_v, f + 1)
                                    at_ = slice(FW * ft + P * (k % 2), FW * ft + P * (k % 2) + P)
                                    i = exact(bank("fd", k)[:, 0:T], parts_of_load(m, at_), (f_hi[:, f, :], f_lo[:, f, :]),
                                              f == 0, f == FT - 1)
                                if j == len(FF_ROWS) - 1:
                                    i.then_inc(made_of("fd", k), 1)
                                elif k % 2:
                                    i.then_inc(part_used, 1)

            for j in range(4):
                c, k0 = 1 + j // 2, 4 * (j % 2)
                pe.wait_ge(*room("h_tok", j))
                for k in range(4):
                    i = pe.transpose(bank("h_tok", j)[:, P * k:P * k + P], hT[:, k0 + k, WIDE[c]], ident)
                i.then_inc(made_of("h_tok", j), 1)
            pe.wait_ge(hn_v, KD * 4)
            for j in range(4):
                c, k0 = 1 + j // 2, 4 * (j % 2)
                pe.wait_ge(*room("hn_tok", j))
                for k in range(4):
                    i = pe.transpose(bank("hn_tok", j)[:, P * k:P * k + P], hnT[:, k0 + k, WIDE[c]], ident)
                i.then_inc(made_of("hn_tok", j), 1)
            pe.wait_ge(*room("logits"))
            for c in range(2):
                for k in range(KD):
                    i = mm(bank("logits")[:, EXPERTS * c:EXPERTS * c + EXPERTS], hnT[:, k, WIDE[c + 1]], wrout[:, k, :],
                           k == 0, k == KD - 1)
            i.then_inc(made_of("logits"), 1)
            pe.wait_ge(r_v, R_MASK)
            m0, m1 = route[:, R["mask"]:R["mask"] + 8], route[:, R["mask"] + 8:R["mask"] + 16]
            b = bank("pos")
            pe.wait_ge(*room("pos"))
            mm(b[:, 0:8], const("upper"), m0, True, True)
            mm(b[:, 8:16], ones, m0, True, False)
            mm(b[:, 8:16], const("upper"), m1, False, True).then_inc(made_of("pos"), 1)
            pe.wait_ge(*room("count"))
            mm(bank("count")[:, 0:8], ones, m0, True, False)
            mm(bank("count")[:, 0:8], ones, m1, False, True).then_inc(made_of("count"), 1)
            for j in range(4):
                pe.wait_ge(*gone("hn_tok", j))

            def gather(i):
                pe.wait_ge(sel_v, 2 * i + 2)
                for j in range(4):
                    src = (hn_hi, hn_lo)[j // 2]
                    pe.wait_ge(*room_i(i, "xg", j))
                    for k in range(4):
                        for c in range(2):
                            f = P * (4 * (j % 2) + k)
                            m = mm(bank("xg", j)[:, P * k:P * k + P], src[:, c, f:f + P], sel[:, c, :], c == 0, c == 1)
                    m.then_inc(made_of("xg", j), 1)

            def back(i, js):
                pe.wait_ge(*gone_i(i, "selT", before=1))
                for j in js:
                    c, half = j // 2, j % 2
                    hs = slice(FC * half, FC * half + FC)
                    pe.wait_ge(*gone_i(i, "y", half, before=1))
                    pe.wait_ge(*room_i(i, "back", j, before=1))
                    mm(bank("back", j), selT[:, c, :], y_hi[:, hs], True, False)
                    mm(bank("back", j), selT[:, c, :], y_lo[:, hs], False, True).then_inc(made_of("back", j), 1)

            def item(i, first):
                def turn(c):
                    pe.wait_ge(*gone_i(i, "u", c))
                    pe.wait_ge(*room_i(i, "aT", c))
                    v = act_sb[:, c % 2, :].rearrange("p (j f r) -> p j r f", j=2, r=2)
                    for j in range(4):
                        m = pe.transpose(bank("aT", c)[:, P * j:P * j + P], v[:, j // 2, j % 2, :], ident)
                    m.then_inc(made_of("aT", c), 1)

                for n, (w, c, j) in enumerate(ITEM):
                    turned = turned_after(w, c, j)
                    if turned is not None:
                        turn(turned)
                        if turned == NFC - 1:
                            gather(i + 1)
                    if n in BACK and not first:
                        back(i, BACK[n])
                    if n == SEL_TURN:
                        pe.wait_ge(*room_i(i, "selT"))
                        for q in range(2):
                            m = pe.transpose(bank("selT")[:, P * q:P * q + P], sel[:, q, :].bitcast(F32), ident)
                        m.then_inc(made_of("selT"), 1)
                    for wait in ready_i(i, n):
                        pe.wait_ge(*wait)
                    if w == "d":
                        if j == 0:
                            pe.wait_ge(part_a, PA * i + c + 1)
                            pe.wait_ge(*gone_i(i, "aT", c))
                            if c == 0:
                                pe.wait_ge(*room_i(i, "y", 0))
                                pe.wait_ge(*room_i(i, "y", 1))
                        for r in range(2):
                            q = slice(P * (2 * j + r), P * (2 * j + r) + P)
                            for half in range(2):
                                at_ = slice(D * r + FC * half, D * r + FC * half + FC)
                                m = exact(bank("y", half), (act_hi[:, c % 2, q], act_lo[:, c % 2, q]),
                                          parts_of_load(MOE0 + n, at_), (c, j, r) == (0, 0, 0), (c, j, r) == (NFC - 1, 1, 1))
                                if (c, j, r) == (NFC - 1, 1, 1):
                                    m.then_inc(made_of("y", half), 1)
                                elif r == 1 and half == 1:
                                    m.then_inc(part_used, 1)
                        continue
                    if j == 0:
                        pe.wait_ge(*room_i(i, w, c))
                    for kk in range(4):
                        k = 4 * j + kk
                        if n < 2 and kk == 0:
                            pe.wait_ge(*gone_i(i, "xg", j))
                            pe.wait_ge(*gone_i(i, "xg", 2 + j))
                        q = slice(P * k, P * k + P)
                        m = exact(bank(w, c), (x_hi[:, q], x_lo[:, q]), parts_of_load(MOE0 + n, slice(FC * kk, FC * kk + FC)),
                                  k == 0, k == KD - 1)
                    if j:
                        m.then_inc(made_of(w, c), 1)
                    else:
                        m.then_inc(part_used, 1)

            gather(0)
            item(0, True)
            pe.wait_ge(r_v, N_ROUTE)
            n_items = pe.value_load(ctl[0:1, 0:1], min_val=EXPERTS, max_val=ITEMS)
            with pe.Fori(1, ITEMS) as i:
                with pe.If(i < n_items):
                    item(i, False)
            back(n_items, range(4))

        @block.scalar
        def _(act):
            def square(r, k):
                if r:
                    act.wait_ge(*gone(*stream(r, k)))
                if k == 0 and r in (1, 3):
                    act.wait_ge(*done("wo", r // 2, KD - 1))
                act.activation(hnT[:, k, :], hT[:, k, :], ACT.Square).then_inc(sq_a, 1)

            def first_parts(r):
                act.wait_ge(*gone("ms", r))
                act.activation(rms[:, 1, :], rms[:, 0, :], ACT.Sqrt).then_inc(rms_a, 1)
                if r < 3:
                    for k in range(KD):
                        act.wait_ge(hn_v, KD * r + k + 1)
                        act.activation(a_hi[:, k, :], hnT[:, k, :], ACT.Copy).then_inc(ahi_a, 1)

            act.wait_ge(x_in, 16)
            for k in range(KD):
                square(0, k)
            for n in range(SPLIT):
                split_hi(act, n)
            for li in range(LAYERS):
                first_parts(2 * li)

                def values(n, v):
                    act.wait_ge(*done("vA", li, n))
                    act.activation(v[:, 0:2, :], bank("vA", li, n)[:, :].rearrange("p (c v) -> p c v", c=2), ACT.Copy)\
                        .then_inc(taken_of("vA", li, n), 1)
                    act.wait_ge(*done("vB", li, n))
                    act.activation(v[:, 2, :], bank("vB", li, n)[:, 0:256], ACT.Copy).then_inc(taken_of("vB", li, n), 1)

                for n, (_, _, tiles) in enumerate(IN_LOADS):
                    for t, _ in tiles:
                        f = ACT.Silu if t in (AOG, AOG + 1, ROG, ROG + 1) else ACT.Copy
                        q = PART.get(t, slice(0, P))
                        act.wait_ge(*done("proj", li, t))
                        act.activation(pr[q, t, :], bank("proj", li, t)[q, 0:T], f).then_inc(taken_of("proj", li, t), 1)
                    split_hi(act, load_in(li, n) + SPLIT)
                    if n == 4:
                        values(0, va)
                    if n == 7:
                        act.wait_ge(gla_v, 5 * li + 1)
                        act.activation(gabs, gabs, ACT.Exp, scale=-1.0).then_inc(gate_a, 1)
                        act.wait_ge(lam_v, 3 * li + 2)
                        act.activation(lam[:, 2 * li:2 * li + 2], lam[:, 2 * li:2 * li + 2], ACT.Exp).then_inc(lam_a, 1)
                        act.wait_ge(gate_a, 2 * li + 1)
                        act.activation(gabs, gabs, ACT.Ln, bias=1.0).then_inc(gate_a, 1)
                    if n == 8:
                        values(1, vr)
                    if n == 9:
                        act.wait_ge(*gone("proj", li, CQ))
                        act.wait_ge(*gone("proj", li, CKV))
                        act.activation(rms[:, 0, :], pr[:, CQ, :], ACT.Square).then_inc(c_a, 1)
                        act.activation(rms[:, 1, :], pr[:, CKV, :], ACT.Square).then_inc(c_a, 1)
                    if n == 10:
                        act.wait_ge(*gone("cum", li))
                        act.activation(eq, cumT, ACT.Exp).then_inc(cum_a, 1)
                        act.activation(ek, cumT, ACT.Exp, scale=-1.0).then_inc(cum_a, 1)
                        for a, e in ((0, 16), (16, 80), (80, 144), (144, 208)):
                            act.activation(ekd[:, a:e], cumT[:, a:e], ACT.Exp, bias=cumT[:, e - 1:e], scale=-1.0)\
                                .then_inc(cum_a, 1)
                    if n == 11:
                        act.wait_ge(*gone("cq", li))
                        act.activation(rms[:, 0, :], rms[:, 0, :], ACT.Sqrt).then_inc(c_a, 1)
                        act.wait_ge(*gone("ckv", li))
                        act.activation(rms[64:128, 1, :], rms[64:128, 1, :], ACT.Sqrt).then_inc(c_a, 1)
                values(2, vd)
                for h in range(H):
                    act.wait_ge(*done("mq", li, h))
                    act.activation(qc[0:MLA_DK, h, :], bank("mq", li, h)[0:MLA_DK, 0:T], ACT.Copy).then_inc(taken_of("mq", li, h), 1)
                for h in range(H):
                    act.wait_ge(*done("mk", li, h))
                    act.activation(kc[0:NOPE, h, :], bank("mk", li, h)[0:NOPE, 0:T], ACT.Copy).then_inc(taken_of("mk", li, h), 1)
                act.wait_ge(*done("mvA", li))
                act.activation(vm[:, 0:2, :], bank("mvA", li)[:, :].rearrange("p (c v) -> p c v", c=2), ACT.Copy)\
                    .then_inc(taken_of("mvA", li), 1)
                act.wait_ge(*done("mvB", li))
                act.activation(vm[:, 2, :], bank("mvB", li)[:, 0:256], ACT.Copy).then_inc(taken_of("mvB", li), 1)
                for name, o in (("go", ob), ("ro", ob_r)):
                    act.wait_ge(*done(name + "A", li))
                    act.activation(o[:, 0:2, :], bank(name + "A", li)[:, :].rearrange("p (c v) -> p c v", c=2), ACT.Copy)\
                        .then_inc(taken_of(name + "A", li), 1)
                    act.wait_ge(*done(name + "B", li))
                    act.activation(o[:, 2, :], bank(name + "B", li)[:, 0:256], ACT.Copy).then_inc(taken_of(name + "B", li), 1)
                    if name == "go":
                        act.wait_ge(*gone("goB", li))
                        act.wait_ge(*gone("goA", li))
                        act.activation(sq[:, :, :], ob[:, :, :], ACT.Square).then_inc(n_a, 1)
                for m in range(N_MAPS + 2):
                    if m < N_MAPS:
                        act.wait_ge(*gone("sc", li, m))
                        pb = probs[:, m % 3, :]
                        for c, a, e in ((2, 0, T), (1, T, T + 144), (0, T + 144, T + 160)):
                            i = act.activation(pb[:, a:e], pb[:, a:e], ACT.Exp, bias=neg_max[:, m, c:c + 1], scale=-1.0,
                                               accum_out=den[:, m, c:c + 1])
                        i.then_inc(exp_a, 1)
                    if m >= 2:
                        act.wait_ge(*done("ptM", li, m - 2))
                        if m >= 4:
                            act.wait_ge(*done("o", li, m - 4))
                        act.activation(pt[0:META, m % 2, 384:768], bank("ptM", li, m - 2)[0:META, 0:384], ACT.Copy)\
                            .then_inc(taken_of("ptM", li, m - 2), 1)
                    if m in (6, 11):
                        for k in ((0, 1) if m == 6 else (2, 3)):
                            act.wait_ge(*gone("turn", li, k))
                            act.activation(a_hi[:, k, :], oT[:, k, :], ACT.Copy).then_inc(ahi_a, 1)
                    if m == 5:
                        act.wait_ge(n_v, N_NORM * li + 6)
                        act.activation(sq[:, :, :], ob_r, ACT.Square).then_inc(n_a, 1)
                    if m == 11:
                        act.wait_ge(n_v, N_NORM * li + 10)
                        act.activation(sq[:, :, :], o1[:, :, :], ACT.Square).then_inc(n_a, 1)
                for k in (4, 5, 6, 7):
                    act.wait_ge(*(done if k < 6 else gone)("turn", li, k))
                    act.activation(a_hi[:, k, :], bank("turn", li, k)[:, 0:T] if k < 6 else oT[:, k, :], ACT.Copy).then_inc(ahi_a, 1)
                for n in range(4):
                    split_hi(act, load_out(li, n) + SPLIT)
                for k in range(KD):
                    square(2 * li + 1, k)
                first_parts(2 * li + 1)
                if li == 0:
                    for c in range(FF_GROUPS):
                        for f in (2 * c, 2 * c + 1):
                            act.wait_ge(*done("fg", f))
                            if f >= 2:
                                act.wait_ge(*gone("fu", f - 2))
                            act.activation(ffs[:, f % 2, :], bank("fg", f)[:, 0:T], ACT.Silu).then_inc(taken_of("fg", f), 1)
                        split_hi(act, load_gate(c) + SPLIT)
                        for f in (2 * c, 2 * c + 1):
                            act.wait_ge(*gone("fu", f))
                            act.activation(f_hi[:, f, :], ffa[:, f % 3, :], ACT.Copy).then_inc(ff_a, 1)
                        split_hi(act, load_up(c) + SPLIT)
                    for pair in range(4):
                        for j in range(len(FF_ROWS)):
                            if j == len(FF_ROWS) - 1:
                                for k in (2 * pair, 2 * pair + 1):
                                    square(2, k)
                            split_hi(act, load_down(pair, j) + SPLIT)
            for j in range(4):
                act.wait_ge(*done("hn_tok", j))
                act.activation(hn_hi[:, j // 2, FC * (j % 2):FC * (j % 2) + FC], bank("hn_tok", j), ACT.Copy).then_inc(tok_a, 1)
            act.wait_ge(r_v, R_EXP)
            act.activation(route[:, R["e"]:R["e"] + 2], route[:, R["d"]:R["d"] + 2], ACT.Exp).then_inc(r_a, 1)

            def tokens(i):
                for j in range(2):
                    act.wait_ge(*done_i(i, "xg", j))
                    act.activation(x_hi[:, FC * j:FC * j + FC], bank("xg", j), ACT.Copy).then_inc(taken_of("xg", j), 1)

            def item(i, first):
                def first_part(dst, *name):
                    act.wait_ge(*done_i(i, *name))
                    act.activation(dst, bank(*name), ACT.Copy).then_inc(part_a, 1)

                if not first:
                    split_hi_i(act, i, SPLIT - 1)
                for n, (w, c, j) in enumerate(ITEM):
                    if (w, j) == ("g", 1):
                        act.wait_ge(*done_i(i, "g", c))
                        if c >= 2:
                            act.wait_ge(*gone_i(i, "u", c - 2))
                        act.activation(sg[:, c % 2, :], bank("g", c), ACT.Silu).then_inc(taken_of("g", c), 1)
                    turned = turned_after(w, c, j)
                    if turned is not None:
                        if turned >= 2:
                            act.wait_ge(*used_i(i, ITEM.index(("d", turned - 2, 1))))
                        first_part(act_hi[:, turned % 2, :], "aT", turned)
                        if turned == NFC - 1:
                            tokens(i + 1)
                    if n + SPLIT < PER_EXPERT:
                        split_hi_i(act, i, n + SPLIT)
                if first:
                    for n in range(SPLIT - 1):
                        split_hi_i(act, i, PER_EXPERT + n)
                else:
                    with act.If(i + 1 < n_items):
                        for n in range(SPLIT - 1):
                            split_hi_i(act, i, PER_EXPERT + n)
                for half in range(2):
                    first_part(y_hi[:, FC * half:FC * half + FC], "y", half)

            tokens(0)
            item(0, True)
            act.wait_ge(r_v, N_ROUTE)
            n_items = act.value_load(ctl[0:1, 0:1], min_val=EXPERTS, max_val=ITEMS)
            with act.Fori(1, ITEMS) as i:
                with act.If(i < n_items):
                    item(i, False)
            act.wait_ge(*gone_i(n_items, "back", 3, before=1))
            for c in range(2):
                act.activation(out_sb[:, c, :], h_tok[:, c, :], ACT.Square, accum_out=st1[:, c:c + 1]).then_inc(fin_a, 1)

        @block.vector
        def _(dve):
            def normalize(r):
                dve.wait_ge(*done("ms", r))
                dve.tensor_scalar(rms[:, 0, :], bank("ms", r)[:, 0:T], 1.0 / D, EPS, ALU.mult, ALU.add)\
                    .then_inc(taken_of("ms", r), 1)
                dve.wait_ge(rms_a, r + 1)
                dve.reciprocal(rms[:, 0, :], rms[:, 1, :]).then_inc(rstd_v, 1)
                dve.wait_ge(rstd_v, r + 1)

                def second_part(k):
                    dve.wait_ge(ahi_a, KD * (0, 2, 3)[r] + k + 1)
                    dve.tensor_tensor(a_lo[:, k, :], hnT[:, k, :], a_hi[:, k, :].bitcast(F32), ALU.subtract).then_inc(alo_v, 1)

                for k in range(KD):
                    dve.scalar_tensor_tensor(out=hnT[:, k, :], in0=hT[:, k, :], scalar=gain("ffn" if r % 2 else "attn", r // 2, k),
                                             in1=rms[:, 0, :], op0=ALU.mult, op1=ALU.mult).then_inc(hn_v, 1)
                    if k and r < 3:
                        second_part(k - 1)
                if r < 3:
                    second_part(KD - 1)

            def head_sums(o, n):
                dve.tensor_reduce(st1, o[:, :, :].rearrange("p c (h v) -> p (c h) v", h=H), AX.X, ALU.add).then_inc(n_v, 1)

            def head_mean_squares(li, step, n):
                dve.wait_ge(n_v, N_NORM * li + step)
                dve.tensor_scalar(st2, st1, 1.0 / DV, EPS, ALU.mult, ALU.add).then_inc(n_v, 1)

            def head_scale(li, o, n):
                dve.wait_ge(n_p, 3 * li + n)
                v = o[:, :, :].rearrange("p c (h v) -> p (c h) v", h=H)
                dve.tensor_tensor(v, v, st3.unsqueeze(2).to_broadcast([P, 12, DV]), ALU.mult).then_inc(n_v, 1)

            def out_part(li, k):
                dve.wait_ge(ahi_a, KD * (3 * li + 1) + k + 1)
                dve.tensor_tensor(a_lo[:, k, :], oT[:, k, :], a_hi[:, k, :].bitcast(F32), ALU.subtract).then_inc(alo_v, 1)

            for n in range(SPLIT):
                split_lo(dve, n)
            for li in range(LAYERS):
                if li == 0:
                    dve.wait_ge(tables_in, 16 * 3)
                normalize(2 * li)

                def rotate(j):
                    dve.wait_ge(*gone("proj", li, RQ + j))
                    if j:
                        dve.wait_ge(rot_v, 8 * li + 2 * j)
                    dve.tensor_tensor(t1, pr[:, RQ + j, :], const("cos_ret"), ALU.mult).then_inc(rot_v, 1)
                    dve.wait_ge(*done("swap", li, j))
                    dve.tensor_tensor(t2, bank("swap", li, j)[:, 0:T], const("sin_ret"), ALU.mult).then_inc(taken_of("swap", li, j), 1)
                    dve.wait_ge(rot_v, 8 * li + 2 * j + 1)
                    dve.wait_ge(*gone("swap", li, j))
                    dve.tensor_tensor(pr[:, RQ + j, :], t1, t2, ALU.add).then_inc(rot_v, 1)

                r4 = slice(64, 96)
                for n in range(len(IN_LOADS)):
                    split_lo(dve, load_in(li, n) + SPLIT)
                    if n == 4:
                        dve.wait_ge(*done("gate", li))
                        dve.tensor_tensor(gx.rearrange("p (c f) -> p c f", c=3), bank("gate", li)[:, 0:384].rearrange("p (c f) -> p c f", c=3),
                                          param("bgate").unsqueeze(1).to_broadcast([P, 3, P]), ALU.add).then_inc(taken_of("gate", li), 1)
                        dve.wait_ge(*gone("gate", li))
                        dve.scalar_tensor_tensor(out=gabs, in0=gx, scalar=-1.0, in1=gx, op0=ALU.mult, op1=ALU.max).then_inc(gla_v, 1)
                        lv = param("dlam").rearrange("p (n d) -> p n d", n=4)
                        for j in range(2):
                            dve.tensor_tensor_reduce(kdT[:, 32 * j:32 * j + 32], lv[:, 2 * j, :], lv[:, 2 * j + 1, :], 1.0, 0.0,
                                                     ALU.mult, ALU.add, lam[:, 2 * li + j:2 * li + j + 1]).then_inc(lam_v, 1)
                    if n in (6, 7):
                        rotate(2 * n - 12)
                        rotate(2 * n - 11)
                    if n == 8:
                        dve.wait_ge(gate_a, 2 * li + 2)
                        dve.scalar_tensor_tensor(out=gx, in0=gx, scalar=0.0, in1=gabs, op0=ALU.min, op1=ALU.subtract).then_inc(gla_v, 1)
                        dve.wait_ge(lam_a, li + 1)
                        dve.scalar_tensor_tensor(out=lam[:, 4 + li:5 + li], in0=lam[:, 2 * li + 1:2 * li + 2], scalar=-LAM_INIT[li],
                                                 in1=lam[:, 2 * li:2 * li + 1], op0=ALU.add, op1=ALU.subtract).then_inc(lam_v, 1)
                    if n == 9:
                        dve.wait_ge(*done("cum", li))
                        dve.tensor_copy(cumT, bank("cum", li)[:, 0:T]).then_inc(taken_of("cum", li), 1)
                    if n == 11:
                        dve.wait_ge(*done("cq", li))
                        dve.wait_ge(*done("ckv", li))
                        dve.tensor_scalar(rms[:, 0, :], bank("cq", li)[:, 0:T], 1.0 / Q_RANK, EPS, ALU.mult, ALU.add)\
                            .then_inc(taken_of("cq", li), 1)
                        dve.tensor_scalar(rms[64:128, 1, :], bank("ckv", li)[64:128, 0:T], 1.0 / 64, EPS, ALU.mult, ALU.add)\
                            .then_inc(taken_of("ckv", li), 1)
                        dve.wait_ge(rot_v, 8 * li + 8)
                        dve.tensor_tensor(t1[r4, :], pr[r4, KPE, :], const("cos_mla")[r4, :], ALU.mult).then_inc(rk_v, 1)
                        dve.wait_ge(*done("kswap", li))
                        dve.tensor_tensor(t2[r4, :], bank("kswap", li)[r4, 0:T], const("sin_mla")[r4, :], ALU.mult)\
                            .then_inc(taken_of("kswap", li), 1)
                        dve.wait_ge(rk_v, 2 * li + 1)
                        dve.wait_ge(*gone("kswap", li))
                        dve.tensor_tensor(kc[r4, :, :], t1[r4, :].unsqueeze(1).to_broadcast([32, H, T]),
                                          t2[r4, :].unsqueeze(1).to_broadcast([32, H, T]), ALU.add).then_inc(rk_v, 1)
                        dve.wait_ge(cum_a, 6 * li + 6)
                        dve.scalar_tensor_tensor(out=pr[:, AQ, :], in0=pr[:, AQ, :], scalar=GLA_DK**-0.5, in1=eq, op0=ALU.mult, op1=ALU.mult)\
                            .then_inc(gla_v, 1)
                        dve.tensor_tensor(kdT[:, 0:208], pr[:, AK, 0:208], ekd[:, 0:208], ALU.mult).then_inc(gla_v, 1)
                        dve.wait_ge(gla_v, 5 * li + 4)
                        dve.tensor_tensor(pr[:, AK, :], pr[:, AK, :], ek, ALU.mult).then_inc(gla_v, 1)
                    if n == 12:
                        dve.wait_ge(c_a, 4 * li + 4)
                        dve.reciprocal(rms[:, 0, :], rms[:, 0, :]).then_inc(c_v, 1)
                        dve.reciprocal(rms[64:128, 1, :], rms[64:128, 1, :]).then_inc(c_v, 1)
                        dve.wait_ge(c_v, 5 * li + 2)
                        dve.scalar_tensor_tensor(out=pr[:, CQ, :], in0=pr[:, CQ, :], scalar=gain("q", li), in1=rms[:, 0, :],
                                                 op0=ALU.mult, op1=ALU.mult).then_inc(c_v, 1)
                        dve.scalar_tensor_tensor(out=pr[0:64, CKV, :], in0=pr[0:64, CKV, :], scalar=gain("q_kv", li)[0:64, :],
                                                 in1=rms[0:64, 0, :], op0=ALU.mult, op1=ALU.mult).then_inc(c_v, 1)
                        dve.scalar_tensor_tensor(out=pr[64:128, CKV, :], in0=pr[64:128, CKV, :], scalar=gain("q_kv", li)[64:128, :],
                                                 in1=rms[64:128, 1, :], op0=ALU.mult, op1=ALU.mult).then_inc(c_v, 1)
                dve.wait_ge(*done("kd", li))
                dve.tensor_copy(kd_tok[0:META, 0:128], bank("kd", li)[0:META, 0:128])
                dve.tensor_copy(kd_tok[:, 128:256], bank("kd", li)[:, 128:256])
                dve.tensor_copy(kd_tok[0:64, 256:384], bank("kd", li)[0:64, 256:384]).then_inc(taken_of("kd", li), 1)
                for h in range(H):
                    dve.wait_ge(*gone("mq", li, h))
                    if h:
                        dve.wait_ge(rq_v, 8 * li + 2 * h)
                    else:
                        dve.wait_ge(rk_v, 2 * li + 2)
                    dve.tensor_tensor(t1[r4, :], qc[r4, h, :], const("cos_mla")[r4, :], ALU.mult).then_inc(rq_v, 1)
                    dve.wait_ge(*done("qswap", li, h))
                    dve.tensor_tensor(t2[r4, :], bank("qswap", li, h)[r4, 0:T], const("sin_mla")[r4, :], ALU.mult)\
                        .then_inc(taken_of("qswap", li, h), 1)
                    dve.wait_ge(rq_v, 8 * li + 2 * h + 1)
                    dve.wait_ge(*gone("qswap", li, h))
                    dve.tensor_tensor(qc[r4, h, :], t1[r4, :], t2[r4, :], ALU.add).then_inc(rq_v, 1)
                dve.wait_ge(*done("upA", li))
                dve.tensor_tensor(state[0], bank("upA", li)[:, 0:256], const("block"), ALU.mult).then_inc(st_v, 1)
                dve.tensor_tensor(state[1], bank("upA", li)[:, 256:512], const("block"), ALU.mult).then_inc(taken_of("upA", li), 1)
                dve.wait_ge(*done("upB", li))
                dve.tensor_tensor(state[2], bank("upB", li)[:, 0:256], const("block"), ALU.mult).then_inc(taken_of("upB", li), 1)
                dve.wait_ge(*done("upC", li))
                dve.tensor_tensor(state[3], bank("upC", li)[:, 0:256], const("block"), ALU.mult).then_inc(taken_of("upC", li), 1)
                for name in ("upA", "upB", "upC"):
                    dve.wait_ge(*gone(name, li))
                for j in range(3):
                    dve.wait_ge(st_v, 4 * li + 1 + j)
                    e = (80, 144, 208)[j]
                    dve.scalar_tensor_tensor(out=state[j + 1], in0=state[j], scalar=eq[:, e - 1:e], in1=state[j + 1],
                                             op0=ALU.mult, op1=ALU.add).then_inc(st_v, 1)
                for h in range(H):
                    dve.wait_ge(*done("gs", li, h))
                    if h >= 2:
                        dve.wait_ge(map_used, 7 * li + h - 1)
                    dve.tensor_tensor(pt[:, h % 2, 0:384].rearrange("p (c q) -> p c q", c=3),
                                      bank("gs", li, h)[:, 0:384].rearrange("p (c q) -> p c q", c=3),
                                      const("intra").unsqueeze(1).to_broadcast([P, 3, P]), ALU.mult).then_inc(taken_of("gs", li, h), 1)
                for h in range(H):
                    dve.wait_ge(map_used, 7 * li + 3 + h)
                    mp = pt[:, h % 2, :]
                    dve.wait_ge(*done("rsM", li, h))
                    dve.tensor_tensor(mp[0:META, 384:384 + T], bank("rsM", li, h)[0:META, 0:T], decay[0:META, h, :], ALU.mult)\
                        .then_inc(taken_of("rsM", li, h), 1)
                    dve.wait_ge(*done("rsX", li, h))
                    dve.tensor_tensor(mp[:, 0:256], bank("rsX", li, h)[:, 0:256], decay[:, h, 0:256], ALU.mult)
                    dve.tensor_tensor(mp[:, 256:384], bank("rsX", li, h)[:, 256:384], decay[:, h, 0:128], ALU.mult)\
                        .then_inc(taken_of("rsX", li, h), 1)
                sc = DIFF_DK**-0.5
                for m in range(N_MAPS + 3):
                    if m - 1 in TURNS:
                        kind = "gla" if m == 4 else "ret"
                        og = AOG if m == 4 else ROG
                        for j, k in enumerate(TURNS[m - 1]):
                            dve.wait_ge(*done("turn", li, k))
                            dve.scalar_tensor_tensor(out=oT[:, k, :], in0=bank("turn", li, k)[:, 0:T], scalar=gain(kind, li),
                                                     in1=pr[:, og + j, :], op0=ALU.mult, op1=ALU.mult).then_inc(taken_of("turn", li, k), 1)
                    if m < N_MAPS:
                        sc = DIFF_DK**-0.5 if m < DIFF_MAPS else MLA_DK**-0.5
                        dve.wait_ge(*done("sc", li, m))
                        b, pb = bank("sc", li, m), probs[:, m % 3, :]
                        if m >= 3:
                            dve.wait_ge(*done("ptM", li, m - 3))
                        for c, a, e, q in ((2, 0, T, 0), (1, T, T + 144, 128), (0, T + 144, T + 160, 144)):
                            i = dve.tensor_tensor_reduce(pb[:, a:e], b[:, a:e], mask[:, q:q + e - a], -sc, 3e38,
                                                         ALU.add, ALU.min, neg_max[:, m, c:c + 1])
                        i.then_inc(taken_of("sc", li, m), 1)
                        if m:
                            dve.wait_ge(exp_a, N_MAPS * li + m)
                            dve.reciprocal(rden[:, m - 1, :], den[:, m - 1, :]).then_inc(rd_v, 1)
                    if m == N_MAPS:
                        dve.wait_ge(exp_a, N_MAPS * li + m)
                        dve.reciprocal(rden[:, m - 1, :], den[:, m - 1, :]).then_inc(rd_v, 1)
                    if 2 <= m < N_MAPS + 2:
                        dve.wait_ge(*done("ptX", li, m - 2))
                        if m >= 4:
                            dve.wait_ge(*done("o", li, m - 4))
                        dve.tensor_copy(pt[:, m % 2, 0:384], bank("ptX", li, m - 2)[:, 0:384]).then_inc(taken_of("ptX", li, m - 2), 1)
                    if m >= 3:
                        n = m - 3
                        o, h = (((o1, o2)[n % 2], n // 2) if n < DIFF_MAPS else (om, n - DIFF_MAPS))
                        dve.wait_ge(*done("o", li, n))
                        dve.wait_ge(rd_v, N_MAPS * li + n + 1)
                        dve.tensor_tensor(o[:, :, DV * h:DV * h + DV], bank("o", li, n)[:, 0:192].rearrange("p (c v) -> p c v", c=3),
                                          rden[:, n, :].unsqueeze(2).to_broadcast([P, 3, DV]), ALU.mult).then_inc(taken_of("o", li, n), 1)
                    if m in (7, 12):
                        for k in ((0, 1) if m == 7 else (2, 3)):
                            out_part(li, k)
                    if m == 0:
                        dve.wait_ge(n_a, 3 * li + 1)
                        head_sums(sq, 0)
                    if m == 1:
                        head_mean_squares(li, 1, 0)
                    if m == 2:
                        head_scale(li, ob, 1)
                    if m == 3:
                        dve.wait_ge(*gone("roA", li))
                        dve.wait_ge(*gone("roB", li))
                        dve.wait_ge(n_v, N_NORM * li + 3)
                        head_sums(ob_r, 0)
                    if m == 4:
                        dve.wait_ge(n_v, N_NORM * li + 4)
                        dve.tensor_scalar(st4, st1, -1.0 / DV, None, ALU.mult).then_inc(n_v, 1)
                    if m == 5:
                        dve.wait_ge(n_v, N_NORM * li + 5)
                        v = ob_r.rearrange("p c (h v) -> p c h v", h=H)
                        dve.tensor_tensor(v, v, st4.rearrange("p (c h) -> p c h", c=3).unsqueeze(3).to_broadcast([P, 3, H, DV]),
                                          ALU.add).then_inc(n_v, 1)
                    if m == 6:
                        dve.wait_ge(n_a, 3 * li + 2)
                        head_sums(sq, 0)
                    if m == 7:
                        head_mean_squares(li, 7, 0)
                    if m == 8:
                        head_scale(li, ob_r, 2)
                    if m == 10:
                        dve.wait_ge(lam_v, 3 * (li + 1))
                        for n in (6, 7):
                            dve.wait_ge(*gone("o", li, n))
                        dve.scalar_tensor_tensor(out=flat(o1[:, :, :]), in0=flat(o2[:, :, :]), scalar=lam[:, 4 + li:5 + li],
                                                 in1=flat(o1[:, :, :]), op0=ALU.mult, op1=ALU.add).then_inc(n_v, 1)
                    if m == 12:
                        dve.wait_ge(n_a, 3 * li + 3)
                        head_sums(sq, 0)
                    if m == 13:
                        head_mean_squares(li, 11, 0)
                    if m == 14:
                        head_scale(li, o1, 3)
                for k in (4, 5):
                    dve.wait_ge(ahi_a, KD * (3 * li + 1) + k + 1)
                    dve.tensor_tensor(a_lo[:, k, :], bank("turn", li, k)[:, 0:T], a_hi[:, k, :].bitcast(F32), ALU.subtract)\
                        .then_inc(taken_of("turn", li, k), 1)
                for k in (6, 7):
                    dve.wait_ge(*done("turn", li, k))
                    dve.tensor_scalar(oT[:, k, :], bank("turn", li, k)[:, 0:T], gain("diff", li), 1.0 - LAM_INIT[li],
                                      ALU.mult, ALU.mult).then_inc(taken_of("turn", li, k), 1)
                for k in (6, 7):
                    out_part(li, k)

                def add(name, k):
                    dve.wait_ge(*done(*name, k))
                    dve.tensor_tensor(hT[:, k, :], hT[:, k, :], bank(*name, k)[:, 0:T], ALU.add).then_inc(taken_of(*name, k), 1)

                for n in range(4):
                    add(("wo", li), 2 * n)
                    add(("wo", li), 2 * n + 1)
                    split_lo(dve, load_out(li, n) + SPLIT)
                normalize(2 * li + 1)
                if li == 0:
                    for c in range(FF_GROUPS):
                        split_lo(dve, load_gate(c) + SPLIT)
                        for f in (2 * c, 2 * c + 1):
                            dve.wait_ge(*done("fu", f))
                            dve.wait_ge(*gone("fg", f))
                            if f >= 3:
                                dve.wait_ge(ff_v, f - 2)
                            dve.tensor_tensor(ffa[:, f % 3, :], ffs[:, f % 2, :], bank("fu", f)[:, 0:T], ALU.mult).then_inc(taken_of("fu", f), 1)
                        for f in (2 * c, 2 * c + 1):
                            dve.wait_ge(ff_a, f + 1)
                            dve.tensor_tensor(f_lo[:, f, :], ffa[:, f % 3, :], f_hi[:, f, :].bitcast(F32), ALU.subtract).then_inc(ff_v, 1)
                        split_lo(dve, load_up(c) + SPLIT)
                    for pair in range(4):
                        for j in range(len(FF_ROWS)):
                            if j == len(FF_ROWS) - 1:
                                add(("fd",), 2 * pair)
                                add(("fd",), 2 * pair + 1)
                            split_lo(dve, load_down(pair, j) + SPLIT)

            for j in range(4):
                dve.wait_ge(*done("h_tok", j))
                dve.tensor_copy(h_tok[:, j // 2, FC * (j % 2):FC * (j % 2) + FC], bank("h_tok", j)).then_inc(taken_of("h_tok", j), 1)
            for j in range(4):
                a = slice(FC * (j % 2), FC * (j % 2) + FC)
                dve.wait_ge(tok_a, j + 1)
                dve.tensor_tensor(hn_lo[:, j // 2, a], bank("hn_tok", j), hn_hi[:, j // 2, a].bitcast(F32), ALU.subtract)\
                    .then_inc(taken_of("hn_tok", j), 1)

            step = [0]

            def next_step(ins):
                step[0] += 1
                ins.then_inc(r_v, 1)
                dve.wait_ge(r_v, step[0])

            def rt(name, n): return route[:, R[name]:R[name] + n]
            def by(name, n=EXPERTS): return rt(name, 2 * n).rearrange("p (c e) -> p c e", c=2)
            def wide(a): return a.unsqueeze(2).to_broadcast([P, 2, EXPERTS])

            index = const("index").rearrange("p (c e) -> p c e", c=2)
            dve.wait_ge(*done("logits"))
            dve.tensor_copy(rt("logits", 16), bank("logits")[:, 0:16]).then_inc(taken_of("logits"), 1)
            dve.wait_ge(*gone("logits"))
            for n, src in enumerate(("logits", "rest")):
                next_step(dve.tensor_reduce(rt(f"max{n}", 2), by(src), AX.X, ALU.max))
                next_step(dve.tensor_tensor(by("tmp"), by(src), wide(rt(f"max{n}", 2)), ALU.is_equal))
                next_step(dve.scalar_tensor_tensor(out=rt("tmp", 16), in0=rt("tmp", 16), scalar=-float(EXPERTS), in1=const("index"),
                                                   op0=ALU.mult, op1=ALU.add))
                next_step(dve.tensor_reduce(rt("first", 2), by("tmp"), AX.X, ALU.min))
                next_step(dve.tensor_scalar(rt("first", 2), rt("first", 2), float(EXPERTS), None, ALU.add))
                next_step(dve.tensor_tensor(by(f"hot{n}"), index, wide(rt("first", 2)), ALU.is_equal))
                if n == 0:
                    next_step(dve.scalar_tensor_tensor(out=rt("rest", 16), in0=rt("hot0", 16), scalar=-3e38, in1=rt("logits", 16),
                                                       op0=ALU.mult, op1=ALU.add))
            next_step(dve.tensor_tensor(rt("d", 2), rt("max1", 2), rt("max0", 2), ALU.subtract))
            assert step[0] == R_EXP
            next_step(dve.tensor_tensor(rt("mask", 16), rt("hot0", 16), rt("hot1", 16), ALU.add))
            assert step[0] == R_MASK
            dve.wait_ge(r_a, 1)
            next_step(dve.tensor_scalar(rt("w0", 2), rt("e", 2), 1.0, None, ALU.add))
            next_step(dve.reciprocal(rt("w0", 2), rt("w0", 2)))
            next_step(dve.tensor_tensor(rt("w1", 2), rt("e", 2), rt("w0", 2), ALU.mult))
            next_step(dve.tensor_tensor(by("hot0"), by("hot0"), wide(rt("w0", 2)), ALU.mult))
            next_step(dve.tensor_tensor(by("hot1"), by("hot1"), wide(rt("w1", 2)), ALU.mult))
            gates, places = by("gates", ITEMS), by("places", ITEMS + 1)
            next_step(dve.memset(places[:, :, ITEMS:ITEMS + 1], -1.0))
            next_step(dve.tensor_tensor(gates[:, :, 0:EXPERTS], by("hot0"), by("hot1"), ALU.add))
            dve.wait_ge(*done("pos"))
            dve.tensor_tensor(rt("tmp", 16), bank("pos")[:, 0:16], rt("mask", 16), ALU.mult).then_inc(taken_of("pos"), 1)
            dve.wait_ge(*gone("pos"))
            next_step(dve.tensor_scalar(places[:, :, 0:EXPERTS], by("tmp"), -1.0, None, ALU.add))
            dve.wait_ge(*done("count"))
            dve.tensor_scalar(rt("over", 8), bank("count")[:, 0:8], P + 0.5, None, ALU.is_gt).then_inc(taken_of("count"), 1)
            dve.wait_ge(*gone("count"))
            next_step(dve.tensor_tensor(rt("tmp64", 64).rearrange("p (a b) -> p a b", a=8), const("before").rearrange("p (a b) -> p a b", a=8),
                                        rt("over", 8).unsqueeze(1).to_broadcast([P, 8, 8]), ALU.mult))
            next_step(dve.tensor_reduce(rt("rank", 8), rt("tmp64", 64).rearrange("p (a b) -> p a b", a=8), AX.X, ALU.add))
            for n in range(OVER):
                pick = rt("pick", 8)
                next_step(dve.scalar_tensor_tensor(out=pick, in0=rt("rank", 8), scalar=float(n), in1=rt("over", 8),
                                                   op0=ALU.is_equal, op1=ALU.mult))
                for c in range(2):
                    next_step(dve.tensor_tensor_reduce(rt("tmp64", 8), gates[:, c, 0:EXPERTS], pick, 1.0, 0.0, ALU.mult, ALU.add,
                                                       gates[:, c, EXPERTS + n:EXPERTS + n + 1]))
                    next_step(dve.tensor_tensor_reduce(rt("tmp64", 8), places[:, c, 0:EXPERTS], pick, 1.0, 0.0, ALU.mult, ALU.add,
                                                       places[:, c, EXPERTS + n:EXPERTS + n + 1]))
                next_step(dve.tensor_tensor_reduce(rt("tmp64", 8), const("index")[:, 0:8], pick, 1.0, 0.0, ALU.mult, ALU.add,
                                                   rt("ctl", 4)[:, 1 + n:2 + n]))
            next_step(dve.tensor_scalar(places[:, :, EXPERTS:ITEMS], places[:, :, EXPERTS:ITEMS], -float(P), None, ALU.add))
            next_step(dve.tensor_reduce(rt("ctl", 1), rt("over", 8), AX.X, ALU.add))
            next_step(dve.tensor_scalar(rt("ctl", 1), rt("ctl", 1), float(EXPERTS), None, ALU.add))
            next_step(dve.tensor_copy(ctl[:, :], rt("ctl", 4)[0:1, :]))
            assert step[0] == N_ROUTE, step[0]

            def choose(i):
                for c in range(2):
                    dve.tensor_scalar(sel[:, c, :], const("iota"), places[:, c, bass.ds(i, 1)], None, ALU.is_equal).then_inc(sel_v, 1)

            def tokens(i):
                for j in range(2):
                    dve.wait_ge(*done_i(i, "xg", 2 + j))
                    dve.tensor_copy(x_lo[:, FC * j:FC * j + FC], bank("xg", 2 + j)).then_inc(taken_of("xg", 2 + j), 1)

            def back(i, js):
                for j in js:
                    c, half = j // 2, j % 2
                    hs = h_tok[:, c, FC * half:FC * half + FC]
                    dve.wait_ge(*done_i(i, "back", j, before=1))
                    dve.scalar_tensor_tensor(out=hs, in0=bank("back", j), scalar=gates[:, c, bass.ds(i - 1, 1)], in1=hs,
                                             op0=ALU.mult, op1=ALU.add).then_inc(taken_of("back", j), 1)

            def item(i, first):
                def second_part(dst, src, step, *name):
                    dve.wait_ge(part_a, PA * i + step)
                    dve.tensor_tensor(dst, bank(*name), src.bitcast(F32), ALU.subtract).then_inc(taken_of(*name), 1)

                if not first:
                    split_lo_i(dve, i, SPLIT - 1)
                for n, (w, c, j) in enumerate(ITEM):
                    if n in BACK and not first:
                        back(i, BACK[n])
                    if n == SEL_TURN:
                        dve.wait_ge(*done_i(i, "selT"))
                        dve.tensor_copy(flat(selT), bank("selT")[:, 0:256]).then_inc(taken_of("selT"), 1)
                    if (w, j) == ("u", 1):
                        dve.wait_ge(*done_i(i, "u", c))
                        dve.wait_ge(*gone_i(i, "g", c))
                        if c >= 2:
                            dve.wait_ge(*done_i(i, "aT", c - 2))
                        dve.tensor_tensor(act_sb[:, c % 2, :], sg[:, c % 2, :], bank("u", c), ALU.mult).then_inc(taken_of("u", c), 1)
                        if c == NFC - 1:
                            choose(i + 1)
                    turned = turned_after(w, c, j)
                    if turned is not None:
                        second_part(act_lo[:, turned % 2, :], act_hi[:, turned % 2, :], turned + 1, "aT", turned)
                        if turned == NFC - 1:
                            tokens(i + 1)
                    if n + SPLIT < PER_EXPERT:
                        split_lo_i(dve, i, n + SPLIT)
                if first:
                    for n in range(SPLIT - 1):
                        split_lo_i(dve, i, PER_EXPERT + n)
                else:
                    with dve.If(i + 1 < n_items):
                        for n in range(SPLIT - 1):
                            split_lo_i(dve, i, PER_EXPERT + n)
                for half in range(2):
                    hs = slice(FC * half, FC * half + FC)
                    second_part(y_lo[:, hs], y_hi[:, hs], PA_Y + half + 1, "y", half)

            choose(0)
            tokens(0)
            item(0, True)
            n_items = dve.value_load(ctl[0:1, 0:1], min_val=EXPERTS, max_val=ITEMS)
            with dve.Fori(1, ITEMS) as i:
                with dve.If(i < n_items):
                    item(i, False)
            back(n_items, range(4))
            dve.wait_ge(fin_a, 2)
            dve.tensor_scalar(st2[:, 0:2], st1[:, 0:2], 1.0 / D, EPS, ALU.mult, ALU.add).then_inc(fin_v, 1)
            dve.wait_ge(fin_p, 1)
            dve.wait_ge(gain_in, 16)
            for c in range(2):
                dve.scalar_tensor_tensor(out=out_sb[:, c, :], in0=h_tok[:, c, :], scalar=st3[:, c:c + 1], in1=fgain,
                                         op0=ALU.mult, op1=ALU.mult).then_inc(fin_v, 1)

        @block.gpsimd
        def _(pool):
            pool.memset(half_neg[:, :], -0.5).then_inc(filled, 1)
            pool.wait_ge(filled, 1)
            for li in range(LAYERS):
                for n, s in enumerate((2, 8, 12)):
                    pool.wait_ge(n_v, N_NORM * li + s)
                    pool.tensor_tensor(st3, st2, half_neg[:, :], ALU.pow).then_inc(n_p, 1)
            pool.wait_ge(fin_v, 1)
            pool.tensor_tensor(st3[:, 0:2], st2[:, 0:2], half_neg[:, 0:2], ALU.pow).then_inc(fin_p, 1)


N_NORM = 13
PARAMS, _at = {}, 0
for _name, _n in (("wuq0", H * MLA_DK), ("wuq1", H * MLA_DK), ("wukv", H * 2 * DV), ("wgate", P), ("bgate", P), ("dlam", 4 * DIFF_DK)):
    PARAMS[_name] = (_at, _n)
    _at += _n
N_PARAMS = _at
LAM_INIT = [0.8 - 0.6 * float(np.exp(-0.3 * li)) for li in range(LAYERS)]
R_EXP, R_MASK, N_ROUTE = 14, 15, 47
R, _at = {}, 0
for _name, _n in (("logits", 16), ("rest", 16), ("tmp", 16), ("max0", 2), ("max1", 2), ("first", 2), ("hot0", 16), ("hot1", 16),
                  ("d", 2), ("e", 2), ("w0", 2), ("w1", 2), ("mask", 16), ("gates", 2 * ITEMS), ("places", 2 * ITEMS + 2),
                  ("over", 8), ("rank", 8), ("pick", 8), ("tmp64", 64), ("ctl", 4)):
    R[_name] = _at
    _at += _n


def kernel(x, meta_tokens, attn_norm, w_in, gla_w_gate, gla_b_gate, gla_norm, ret_norm, mla_q_norm, mla_w_uq, mla_kv_norm,
           mla_w_ukv, diff_lambda, diff_norm, w_out, ffn_norm, ffn_w_gate, ffn_w_up, ffn_w_down, moe_router, moe_w_gate,
           moe_w_up, moe_w_down, final_norm):
    import concourse.bacc as _bacc
    from concourse.bass_utils import run_bass_kernel_spmd as _run

    x, meta_tokens, moe_router = np.asarray(x), np.asarray(meta_tokens), np.asarray(moe_router)
    stream = np.concatenate([meta_tokens, x[0]], axis=0)
    x_t = stream.T.reshape(KD, P, T).transpose(1, 0, 2)
    cols_t = np.zeros((P, 48), np.float32)
    for a, at in ((attn_norm, 0), (ffn_norm, 16)):
        cols_t[:, at:at + LAYERS * KD] = np.asarray(a).reshape(LAYERS * KD, P).T
    q_norm = np.asarray(mla_q_norm)
    cols_t[:, 32:34] = q_norm[:, 0:P].T
    cols_t[:, 34:36] = np.concatenate([q_norm[:, P:Q_RANK], np.asarray(mla_kv_norm)], axis=1).T
    for a, at in ((gla_norm, 36), (ret_norm, 38), (diff_norm, 40)):
        cols_t[:, at:at + LAYERS] = np.tile(np.asarray(a), (1, 2)).T
    params_t = np.zeros((LAYERS, P, N_PARAMS), np.float32)
    w_uq = np.asarray(mla_w_uq)
    for name, rows, a in (("wuq0", slice(0, P), w_uq[:, 0:P]), ("wuq1", slice(0, Q_RANK - P), w_uq[:, P:Q_RANK]),
                          ("wukv", slice(P - 64, P), np.asarray(mla_w_ukv)), ("wgate", slice(0, 16), np.asarray(gla_w_gate)),
                          ("bgate", slice(0, P), np.asarray(gla_b_gate)[:, None, :]),
                          ("dlam", slice(0, P), np.asarray(diff_lambda).reshape(LAYERS, 1, -1))):
        at, n = PARAMS[name]
        params_t[:, rows, at:at + n] = a
    router_t = moe_router[0].reshape(KD, P, EXPERTS).transpose(1, 0, 2)

    nc = _bacc.Bacc("TRN2", target_bir_lowering=False, num_devices=1, dynamic_dma_scratch_size=1024)
    table, const_at = constants()
    arrays, args = {}, []
    for name, a in (("w_in", w_in), ("w_out", w_out), ("ffn_w_gate", ffn_w_gate), ("ffn_w_up", ffn_w_up),
                    ("ffn_w_down", ffn_w_down), ("moe_w_gate", moe_w_gate), ("moe_w_up", moe_w_up),
                    ("moe_w_down", moe_w_down), ("final_norm", final_norm), ("x_t", x_t), ("cols_t", cols_t),
                    ("params_t", params_t), ("router_t", router_t), ("consts", table)):
        a = np.ascontiguousarray(a)
        arrays[f"in_{name}_dram"] = a
        args.append(nc.dram_tensor(f"in_{name}_dram", a.shape, mybir.dt.from_np(a.dtype), kind="ExternalInput").ap())
    args.append(nc.dram_tensor("out_0_dram", (1, SEQ, D), F32, kind="ExternalOutput").ap())
    hybrid_trunk(nc, *args, const_at)
    r = _run(nc, [arrays], core_ids=[0])
    return r.results[0]["out_0_dram"]
```

```python
from contextlib import ExitStack

import numpy as np
import concourse.bass as bass
from concourse import mybir

F32 = mybir.dt.float32
F32R = mybir.dt.float32r
I32 = mybir.dt.int32
ALU = mybir.AluOpType
ACT = mybir.ActivationFunctionType
AX = mybir.AxisListType

P = 128
MAP_X = 3 * P
D = 1024
KD = D // P
META = 16
SEQ = 256
T = META + SEQ
LAYERS = 2
EPS = 1e-6
NEG = -1e30
H = 4
DV = 64
GLA_DK = 32
GLA_TAU = 16.0
RET_DK = 64
NOPE, ROPE = 64, 32
MLA_DK = NOPE + ROPE
Q_RANK = 192
DIFF_DK = 32
CHUNK = 64
D_FF = 2816
F_EXP = 3584
EXPERTS = 8
FC = 512
LOAD = 2048
RING = 6
SPLIT = 3
OVER = (2 * SEQ) // (P + 1)
ITEMS = EXPERTS + OVER

WIDE = [slice(0, 128), slice(16, 144), slice(144, 272)]
ROWS = [META, P, P]

IN_LOADS = [
    (512, 144, [(4, 0), (5, 16)]),
    (256, 256, [(2, 0), (3, 128)]),
    (0, 256, [(0, 0), (1, 128)]),
    (1808, 128, [(15, 0)]),
    (1936, 192, [(16, 0), (17, 64)]),
    (784, 256, [(7, 0), (8, 128)]),
    (1040, 256, [(9, 0), (10, 128)]),
    (1296, 256, [(11, 0), (12, 128)]),
    (656, 128, [(6, 0)]),
    (1552, 256, [(13, 0), (14, 128)]),
    (2096, 256, [(18, 0), (19, 128)]),
    (2352, 256, [(20, 0), (21, 128)]),
    (2608, 256, [(22, 0), (23, 128)]),
]
TILE_ORDER = [t for _, _, tiles in IN_LOADS for t, _ in tiles]
PART = {4: slice(0, 16), 17: slice(64, 96)}
AQ, AK, AV, ALR, AOG, RQ, RK, RV, ROG, CQ, CKV, KPE, DQ, DK, DVT = 0, 1, 2, 4, 5, 7, 9, 11, 13, 15, 16, 17, 18, 20, 22
TILES = 24
FW = 256
FF_GROUPS = D_FF // FW
FT = D_FF // P
FF_ROWS = [8, 8, 6]
LAST_DOWN = (3, 2)
N_MAPS = 12
MLA_MAPS = H
UNITS = 8

MIXER = [
    ("load", 0), ("first", 0), ("second", 0),
    ("load", 1), ("gate",), ("first", 1), ("gsig",), ("second", 1),
    ("load", 2), ("gfin",), ("turn", 0), ("first", 2), ("second", 2),
    ("load", 3), ("cum",), ("first", 3), ("dec",), ("second", 3),
    ("load", 4), ("csq",), ("first", 4), ("second", 4),
    ("load", 5), ("kd",), ("cvar",), ("swap", 0), ("first", 5), ("second", 5),
    ("load", 6), ("up",), ("swap", 1), ("cbc",), ("first", 6), ("second", 6),
    ("load", 7), ("gs", 0), ("gs", 1), ("swap", 2), ("mq", 0), ("mq", 1), ("first", 7), ("second", 7),
    ("load", 8), ("swap", 3), ("turn", 1), ("mq", 2), ("mq", 3), ("go", 0), ("mk", 0), ("mk", 1), ("first", 8),
    ("load", 9), ("second", 8), ("sq", "gla", 0), ("gs", 2), ("gs", 3), ("mk", 2), ("mk", 3), ("qswap", 0), ("first", 9), ("second", 9),
    ("load", 10), ("go", 1), ("qswap", 1), ("mv",), ("sq", "gla", 1), ("rs", 0), ("rs", 1), ("qswap", 2), ("first", 10),
    ("load", 11), ("ro", 0), ("var", "gla"), ("qswap", 3), ("rcopy", 0), ("sc", 0), ("rs", 2), ("rs", 3), ("rc", 0), ("sq", "ret", 0), ("second", 10), ("first", 11), ("second", 11),
    ("load", 12), ("r", 0), ("ro", 1), ("sc", 1), ("rcopy", 1), ("bc", "gla", 0), ("bc", "gla", 1), ("turn", 2),
    ("pt", 0), ("r", 1), ("sc", 2), ("rc", 1), ("sq", "ret", 1), ("lo", "gla"),
    ("pt", 1), ("r", 2), ("sc", 3), ("o", 0), ("var", "ret"),
    ("pt", 2), ("r", 3), ("sc", 4), ("sc", 5), ("o", 1), ("bc", "ret", 0), ("bc", "ret", 1), ("mo", 0),
    ("pt", 3), ("r", 4), ("sc", 6), ("w", 4), ("sc", 7), ("o", 2), ("lo", "ret"),
    ("pt", 4), ("r", 5), ("sc", 8), ("w", 5), ("sc", 9), ("o", 3), ("mo", 1),
    ("pt", 5), ("r", 6), ("sc", 10), ("w", 6), ("sc", 11), ("o", 4),
    ("pt", 6), ("r", 7), ("o", 5), ("w", 7), ("sq", "diff", 0), ("out", 0), ("out", 1), ("pt", 7), ("o", 6), ("o", 7), ("sq", "diff", 1), ("out", 2),
    ("var", "diff"), ("first", 12), ("out", 3), ("bc", "diff", 0), ("bc", "diff", 1), ("lo", "diff"), ("second", 12),
]
NORMED = {"gla": (0, 1), "ret": (2, 3), "diff": (6, 7)}
NORMS = [a[1] for a in MIXER if a[0] == "var"]
SQUARED = [a[1:] for a in MIXER if a[0] == "sq"]
OUT_ORDER = [NORMED[a[1]][a[2]] if a[0] == "bc" else a[1] + 4 for a in MIXER if a[0] in ("bc", "mo")]
EARLY = sum(a[0] == "out" for a in MIXER)
LO_ORDER = [k for a in MIXER if a[0] == "lo" for k in NORMED[a[1]]]


def constants():
    parts, at = [], {}

    def put(name, a):
        full = np.zeros((P, a.shape[1]), np.float32)
        full[: a.shape[0]] = a
        at[name] = (sum(x.shape[1] for x in parts), a.shape[1])
        parts.append(full)

    p = np.arange(P)
    put("ident", np.eye(P))
    put("ones", np.ones((P, P)))
    half = RET_DK // 2
    swap = np.zeros((P, P))
    for m in range(P):
        if m % RET_DK < half:
            swap[m + half, m] = -1.0
        else:
            swap[m - half, m] = 1.0
    put("swap_ret", swap)
    half = ROPE // 2
    swap = np.zeros((P, ROPE))
    for m in range(ROPE):
        if m < half:
            swap[NOPE + m + half, m] = -1.0
        else:
            swap[NOPE + m - half, m] = 1.0
    put("swap_mla", swap)
    same = (p[:, None] // CHUNK == p[None, :] // CHUNK) & (p[:, None] <= p[None, :])
    put("cum", same / GLA_TAU)
    put("intra", same * 1.0)
    put("block", (p[:, None] // GLA_DK == np.arange(H * DV)[None, :] // DV) * 1.0)
    lg = np.log(1.0 - 2.0 ** (-5.0 - np.arange(H)))
    rel = np.arange(T)[None, :] - p[:, None]
    decay = [np.where(rel >= 0, np.exp(np.maximum(rel, 0) * lg[h]), 0.0) * RET_DK**-0.5 for h in range(H)]
    put("decay", np.concatenate(decay, axis=1))
    put("mask", np.where(np.arange(T)[None, :] <= META + P + p[:, None], 0.0, NEG))
    inv = 10000.0 ** (-(p % (RET_DK // 2)) / (RET_DK // 2))
    ang = np.arange(T)[None, :] * inv[:, None]
    put("cos_ret", np.cos(ang))
    put("sin_ret", np.sin(ang))
    inv = 10000.0 ** (-(p % (ROPE // 2)) / (ROPE // 2))
    ang = np.arange(T)[None, :] * inv[:, None]
    put("cos_mla", np.cos(ang))
    put("sin_mla", np.sin(ang))
    put("center", np.eye(P) - (p[:, None] // DV == p[None, :] // DV) / DV)
    put("heads", (p[:, None] // DV == np.array([[0, 1, -1, -1, -1, -1, 0, 1]])) * 1.0)
    put("iota", np.broadcast_to(p[None, :], (P, P)))
    put("upper", (p[:, None] <= p[None, :]) * 1.0)
    e = np.arange(EXPERTS)
    put("index", np.broadcast_to(np.tile(e, 2)[None, :], (P, 2 * EXPERTS)))
    put("before", np.broadcast_to((e[None, :] < e[:, None]).reshape(1, -1), (P, EXPERTS**2)))
    return np.concatenate(parts, axis=1).astype(np.float32), at


class Results:

    def __init__(self):
        self.at, self.n = {}, [0] * 8

    def add(self, bank, *name):
        assert name not in self.at
        self.at[name] = (bank, self.n[bank])
        self.n[bank] += 1


def plan_results():
    r = Results()
    for li in range(LAYERS):
        r.add(7, "ms", 2 * li)
        shared, pool = 0, (3, 4, 5, 6)
        for step, *of in MIXER:
            if step == "load":
                for t, _ in IN_LOADS[of[0]][2]:
                    r.add(TILE_ORDER.index(t) % 3, "proj", li, t)
            elif step == "sc":
                r.add(of[0] % 2, "sc", li, *of)
            elif step == "pt":
                pool = (5, 6)
                r.add(2, "ptX", li, *of)
                r.add(3, "ptM", li, *of)
            elif step == "o":
                if of[0] % 2 == 0:
                    r.add(4, "o", li, of[0] // 2)
            elif step == "out":
                r.add(*of, "wo", li, *of)
            elif step in ("go", "ro", "rc"):
                r.add(7, step, li, *of)
            elif step not in ("gsig", "gfin", "dec", "csq", "first", "second", "r", "w", "rcopy", "sq", "mo", "lo"):
                several = {"mv": ("mvA", "mvB"), "up": ("upA", "upB", "upC"), "rs": ("rsM", "rsX"), "turn": ("vA", "vB"),
                           "cvar": ("cvar", "kswap"), "cbc": ("cq", "ckv")}
                for name in several.get(step, (step,)):
                    r.add(pool[shared % len(pool)], name, li, *of)
                    shared += 1
        for k in range(EARLY, KD):
            r.add(k, "wo", li, k)
        r.add(7, "ms", 2 * li + 1)
        if li == 0:
            for f in range(FT):
                r.add(2 * (f % 3), "fg", f)
                r.add(2 * (f % 3) + 1, "fu", f)
            for k in range(KD):
                r.add((6, 7, 4, 5)[k % 4], "fd", k)
    r.add(0, "logitsT")
    r.add(0, "logits")
    for j in range(4):
        r.add(4 + j, "hn_tok", j)
    r.add(1, "pos")
    r.add(2, "count")
    for j in range(4):
        r.add(4 + j, "h_tok", j)
    base = list(r.n)
    for j in range(4):
        r.add(j, "xg", j)
    r.add(5, "selT")
    for c in range(F_EXP // FC):
        r.add(c % 2, "g", c)
        r.add(2 + c % 2, "u", c)
        r.add(4 + c % 2, "aT", c)
    r.add(6, "y", 0)
    r.add(7, "y", 1)
    for j in range(4):
        r.add(6 + j % 2, "back", j)
    return r, [n - b for n, b in zip(r.n, base)]


def hybrid_trunk(nc, w_in, w_out, ffn_w_gate, ffn_w_up, ffn_w_down, moe_w_gate, moe_w_up, moe_w_down, final_norm,
                 x_t, cols_t, params_t, router_t, consts, out, const_at):
    plan, PER_ITEM = plan_results()
    NFC = F_EXP // FC

    with ExitStack() as ctx:
        def sem(name):
            return ctx.enter_context(nc.semaphore(name))

        top = [nc.sbuf_base + (-nc.sbuf_base) % 32]

        def at(offset, name, *shape, dt=F32):
            return nc.alloc_sbuf_tensor_at(name, list(shape), dt, offset=offset)

        def new(name, *shape, dt=F32):
            offset = top[0]
            size = 4 * int(np.prod(shape[1:]))
            top[0] += size + (-size) % 32
            return at(offset, name, *shape, dt=dt)

        ring = new("ring", P, RING, LOAD)
        w_hi, w_lo = new("w_hi", P, SPLIT, LOAD, dt=F32R), new("w_lo", P, SPLIT, LOAD, dt=F32R)
        hT = new("hT", P, KD, T)
        hnT = new("hnT", P, KD, T)
        a_hi, a_lo = new("a_hi", P, KD, T, dt=F32R), new("a_lo", P, KD, T, dt=F32R)
        work = top[0]
        pr = new("pr", P, TILES, T)
        oT = new("oT", P, KD, T)
        va, vr, vd, vm = (new(n, P, 3, H * DV) for n in ("va", "vr", "vd", "vm"))
        gm = new("gm", P, 2, MAP_X + T)
        pt = new("pt", P, 2, MAP_X + T)
        probs = new("probs", P, 4, 432)
        sq = new("sq", P, 4, T)
        work_end = top[0]
        cst = new("cst", P, consts.shape[1])
        cols = new("cols", P, 48)
        params = new("params", P, params_t.shape[2])
        small = new("small", P, 210)
        lam = new("lam", P, 8)
        half_neg = new("half_neg", P, 13)
        rms = new("rms", P, 2, T)
        wrout = new("wrout", P, KD, EXPERTS)
        ctl = new("ctl", 1, 4, dt=I32)
        assert top[0] <= nc.sbuf_usable_end, (top[0], nc.sbuf_usable_end)

        def over(name, *shape, dt=F32):
            offset = place[0]
            size = 4 * int(np.prod(shape[1:]))
            place[0] += size + (-size) % 32
            assert place[0] <= work_end
            return at(offset, name, *shape, dt=dt)

        place = [work]
        f_hi, f_lo = over("f_hi", P, FT, T, dt=F32R), over("f_lo", P, FT, T, dt=F32R)
        ffs, ffa = over("ffs", P, 2, T), over("ffa", P, 3, T)
        place = [work]
        hn_hi, hn_lo = over("hn_hi", P, 2, D, dt=F32R), over("hn_lo", P, 2, D, dt=F32R)
        h_tok = over("h_tok", P, 2, D)
        x_hi, x_lo = over("x_hi", P, D, dt=F32R), over("x_lo", P, D, dt=F32R)
        act_sb = over("act_sb", P, 2, FC)
        act_hi, act_lo = over("act_hi", P, 2, FC, dt=F32R), over("act_lo", P, 2, FC, dt=F32R)
        y_hi, y_lo = over("y_hi", P, D, dt=F32R), over("y_lo", P, D, dt=F32R)
        sg = over("sg", P, 2, FC)
        sel, selT = over("sel", P, 2, P, dt=F32R), over("selT", P, 2, P, dt=F32R)
        banks = [ctx.enter_context(nc.psum_tensor(f"bank{b}", [P, FC], F32))[:, :] for b in range(8)]

        def const(name):
            a, n = const_at[name]
            return cst[:, a:a + n]

        ident, ones = const("ident"), const("ones")
        decay = const("decay").rearrange("p (h t) -> p h t", h=H)
        mask = const("mask")

        def gain(kind, li, k=0):
            j = {"attn": KD * li + k, "ffn": 16 + KD * li + k, "q": 32 + li, "q_kv": 34 + li,
                 "gla": 36 + li, "ret": 38 + li, "diff": 40 + li}[kind]
            return cols[:, j:j + 1]

        def param(name):
            a, n = PARAMS[name]
            return params[:, a:a + n]

        def flat(a): return a.rearrange("p a b -> p (a b)")
        cumT, eq, ek, ekd, t1, t2, kdT = (oT[:, j, :] for j in range(7))
        gx, gabs = gm[:, 0, 0:384], gm[:, 1, 0:384]
        kd_tok = gm[:, 0, 0:384]
        s01, s23 = flat(pr[:, 2:4, :]), pt[:, 1, :]
        state = [s01[:, 0:256], s01[:, 256:512], s23[:, 0:256], s23[:, 256:512]]
        ob = [pr[:, ALR, :], pr[:, KPE, :]]
        qc, kc = hnT[:, 0:4, :], hnT[:, 4:8, :]
        neg_max, den, rden = (small[:, 36 * j:36 * j + 36].rearrange("p (m c) -> p m c", c=3) for j in range(3))
        rden_l = small[:, 108:120].rearrange("p (u c) -> p u c", c=3)
        st2, st3 = (small[:, 120 + 36 * j:156 + 36 * j].rearrange("p (n s) -> p n s", n=3) for j in range(2))
        c2, c3 = small[:, 192:198], small[:, 198:204]
        unread = small[:, 204:205]
        hnf = flat(hnT[:, :, :])
        fgain = hnf[:, 1024:2048]
        route = flat(rms)
        logitsT = pr[0:EXPERTS, KPE, 0:SEQ]
        out_sb = flat(hT[:, :, :])[:, 0:2048].rearrange("p (c d) -> p c d", c=2)

        made = [sem(f"made{b}") for b in range(8)]
        taken = [sem(f"taken{b}") for b in range(8)]
        landed = [sem(f"landed{s}") for s in range(RING)]
        x_in = sem("x_in")
        cols_in = sem("cols_in")
        ones_in = sem("ones_in")
        tables_in = sem("tables_in")
        params_in = sem("params_in")
        gain_in = sem("gain_in")
        filled = sem("filled")
        hi_a = sem("hi_a")
        lo_v = sem("lo_v")
        part_used = sem("part_used")
        sq_a = sem("sq_a")
        rms_a = sem("rms_a")
        rstd_v = sem("rstd_v")
        table_a = sem("table_a")
        hn_v = sem("hn_v")
        ahi_a = sem("ahi_a")
        alo_v = sem("alo_v")
        ff_a, ff_v = sem("ff_a"), sem("ff_v")
        lam_v, lam_a = sem("lam_v"), sem("lam_a")
        gate_a = sem("gate_a")
        gla_v = sem("gla_v")
        cum_a = sem("cum_a")
        rot_v = sem("rot_v")
        c_a, c_p = sem("c_a"), sem("c_p")
        rk_v, rq_v = sem("rk_v"), sem("rq_v")
        st_v = sem("st_v")
        o_used = sem("o_used")
        exp_a = sem("exp_a")
        rd_v = sem("rd_v")
        nl_v = sem("nl_v")
        scaled_a = sem("scaled_a")
        w_v = sem("w_v")
        sq_n, root_p = sem("sq_n"), sem("root_p")
        r_v, r_a = sem("r_v"), sem("r_a")
        tok_a = sem("tok_a")
        sel_v = sem("sel_v")
        part_a = sem("part_a")
        fin_v, fin_a, fin_p = sem("fin_v"), sem("fin_a"), sem("fin_p")
        stored = sem("stored")

        def bank(*name):
            return banks[plan.at[name][0]]

        def room(*name):
            b, n = plan.at[name]
            return taken[b], n

        def done(*name):
            b, n = plan.at[name]
            return made[b], n + 1

        def gone(*name):
            b, n = plan.at[name]
            return taken[b], n + 1

        def made_of(*name):
            return made[plan.at[name][0]]

        def taken_of(*name):
            return taken[plan.at[name][0]]

        def room_i(i, *name, before=0):
            b, n = plan.at[name]
            return taken[b], i * PER_ITEM[b] + (n - before * PER_ITEM[b])

        def done_i(i, *name, before=0):
            b, n = plan.at[name]
            return made[b], i * PER_ITEM[b] + (n + 1 - before * PER_ITEM[b])

        def gone_i(i, *name, before=0):
            b, n = plan.at[name]
            return taken[b], i * PER_ITEM[b] + (n + 1 - before * PER_ITEM[b])

        LO_LAYER = 3 * KD - 2

        def first_map(u):
            return u if u < MLA_MAPS else 2 * u - MLA_MAPS

        def unit(m):
            return m if m < MLA_MAPS else (m + MLA_MAPS) // 2

        def unit_out(li, u):
            return done("o", li, u // 2) if u % 2 else (o_used, 4 * li + u // 2 + 1)

        def normed(kind, li, t):
            return {"gla": "go", "ret": "rc", "diff": "o"}[kind], li, t + (2 if kind == "diff" else 0)

        def stream(v, k):
            return [None, ("wo", 0, k), ("fd", k), ("wo", 1, k)][v]

        PER_LAYER = len(IN_LOADS) + 4
        N_FF = 2 * FF_GROUPS + 4 * len(FF_ROWS)
        MOE0 = 2 * PER_LAYER + N_FF
        PER_EXPERT = 6 * NFC
        assert PER_EXPERT % RING == 0 and PER_EXPERT % SPLIT == 0

        def load_in(li, n): return li * (PER_LAYER + N_FF) + n
        def load_out(li, n): return load_in(li, len(IN_LOADS) + n)
        def load_gate(c): return PER_LAYER + 2 * c
        def load_up(c): return PER_LAYER + 2 * c + 1
        def load_down(pair, j): return PER_LAYER + 2 * FF_GROUPS + len(FF_ROWS) * pair + j

        ITEM = []
        for c in range(NFC):
            ITEM += [(w, c, j) for w in ("g", "u") for j in range(2)]
            ITEM += [("d", c - 1, j) for j in range(2)] if c else []
        ITEM += [("d", NFC - 1, j) for j in range(2)]

        def ends_i(n):
            w, c, j = ITEM[n]
            if w == "d":
                return ("y", 1) if (c, j) == (NFC - 1, 1) else None
            return (w, c) if j else None

        PA_Y, PA = NFC, NFC + 2

        def turned_after(w, c, j):
            if w == "u" and j == 0 and c:
                return c - 1
            return NFC - 1 if (w, c, j) == ("d", NFC - 2, 1) else None

        BACK, SEL_TURN = {2: (0, 1), 4: (2, 3)}, 5

        PARTS_I = sum(ends_i(n) is None for n in range(PER_EXPERT))

        def ends(n):
            for li in range(LAYERS):
                if load_in(li, 0) <= n < load_out(li, 0):
                    return ("proj", li, IN_LOADS[n - load_in(li, 0)][2][-1][0])
                if load_out(li, 0) <= n < load_out(li, 4):
                    return ("wo", li, 2 * (n - load_out(li, 0)) + 1)
            if n < load_down(0, 0):
                return ("fu" if (n - PER_LAYER) % 2 else "fg", 2 * ((n - PER_LAYER) // 2) + 1)
            pair, j = divmod(n - load_down(0, 0), len(FF_ROWS))
            return ("fd", 2 * pair + 1) if j == len(FF_ROWS) - 1 else None

        PARTS = sum(ends(n) is None for n in range(MOE0))

        def ready(n):
            return (hi_a, n + 1), (lo_v, n + 1)

        def ready_i(i, n):
            return (hi_a, i * PER_EXPERT + (MOE0 + n + 1)), (lo_v, i * PER_EXPERT + (MOE0 + n + 1))

        def used(n):
            if ends(n) is None:
                return part_used, sum(ends(m) is None for m in range(n + 1))
            return done(*ends(n))

        def used_i(i, n, before=0):
            if ends_i(n) is None:
                return part_used, i * PARTS_I + (PARTS + sum(ends_i(m) is None for m in range(n + 1)) - before * PARTS_I)
            return done_i(i, *ends_i(n), before=before)

        def width(n):
            for li in range(LAYERS):
                if load_in(li, 0) <= n < load_out(li, 0):
                    return KD * IN_LOADS[n - load_in(li, 0)][1]
            if load_down(0, 0) <= n < load_down(4, 0):
                return FW * FF_ROWS[(n - load_down(0, 0)) % len(FF_ROWS)]
            return LOAD

        def split_hi(act, n):
            a = slice(0, width(n))
            act.wait_ge(landed[n % RING], 16 * (n // RING + 1))
            if n >= SPLIT:
                act.wait_ge(*used(n - SPLIT))
            act.activation(w_hi[:, n % SPLIT, a], ring[:, n % RING, a], ACT.Copy).then_inc(hi_a, 1)

        def split_lo(dve, n):
            a = slice(0, width(n))
            dve.wait_ge(hi_a, n + 1)
            dve.tensor_tensor(w_lo[:, n % SPLIT, a], ring[:, n % RING, a], w_hi[:, n % SPLIT, a].bitcast(F32), ALU.subtract)\
                .then_inc(lo_v, 1)

        def split_hi_i(act, i, n):
            m = MOE0 + n
            act.wait_ge(landed[m % RING], i * (16 * PER_EXPERT // RING) + 16 * (m // RING + 1))
            act.wait_ge(*(used_i(i, n - SPLIT) if n >= SPLIT else used_i(i, n - SPLIT + PER_EXPERT, before=1)))
            act.activation(w_hi[:, m % SPLIT, :], ring[:, m % RING, :], ACT.Copy).then_inc(hi_a, 1)

        def split_lo_i(dve, i, n):
            m = MOE0 + n
            dve.wait_ge(hi_a, i * PER_EXPERT + (m + 1))
            dve.tensor_tensor(w_lo[:, m % SPLIT, :], ring[:, m % RING, :], w_hi[:, m % SPLIT, :].bitcast(F32), ALU.subtract)\
                .then_inc(lo_v, 1)

        block = ctx.enter_context(nc.Block())

        @block.sync
        def _(sp):
            sp.dma_start(hT[:, :, :], x_t).then_inc(x_in, 16)
            sp.dma_start(cols[:, :], cols_t).then_inc(cols_in, 16)
            sp.dma_start(cst[:, 0:2 * P], consts[:, 0:2 * P]).then_inc(ones_in, 16)

            def load(n, k, f, src):
                if n >= RING:
                    sp.wait_ge(lo_v, n - RING + 1)
                sp.dma_start(ring[:, n % RING, 0:k * f].rearrange("p (k f) -> p k f", k=k),
                             src.rearrange("(k p) f -> p k f", p=P)).then_inc(landed[n % RING], 16)

            for li in range(LAYERS):
                for n, (c0, w, _) in enumerate(IN_LOADS):
                    load(load_in(li, n), KD, w, w_in[li, :, c0:c0 + w])
                    if li == 0 and n == 1:
                        sp.dma_start(cst[:, 2 * P:], consts[:, 2 * P:]).then_inc(tables_in, 16)
                        sp.dma_start(wrout[:, :, :], router_t).then_inc(tables_in, 16)
                        sp.dma_start(params[:, :], params_t[0]).then_inc(params_in, 16)
                for n in range(4):
                    load(load_out(li, n), KD, FW, w_out[li, :, FW * n:FW * n + FW])
                if li == 0:
                    for name in (("mq", 0, H - 1), ("mk", 0, H - 1), ("mvB", 0)):
                        sp.wait_ge(*done(*name))
                    sp.dma_start(params[:, :], params_t[1]).then_inc(params_in, 16)
                    for c in range(FF_GROUPS):
                        load(load_gate(c), KD, FW, ffn_w_gate[0, :, FW * c:FW * c + FW])
                        load(load_up(c), KD, FW, ffn_w_up[0, :, FW * c:FW * c + FW])
                    for pair in range(4):
                        for j, nt in enumerate(FF_ROWS):
                            load(load_down(pair, j), nt, FW,
                                 ffn_w_down[0, 8 * P * j:8 * P * j + P * nt, FW * pair:FW * pair + FW])

            views = {
                "g": moe_w_gate[0].rearrange("e (j k p) f -> e j p k f", j=2, p=P),
                "u": moe_w_up[0].rearrange("e (j k p) f -> e j p k f", j=2, p=P),
                "d": moe_w_down[0].rearrange("e (c j p r) d -> e (c j) p (r d)", j=2, p=P, r=2),
            }

            def item(i, e, first):
                for n, (w, c, j) in enumerate(ITEM):
                    m = MOE0 + n
                    if first:
                        sp.wait_ge(lo_v, m - RING + 1)
                    else:
                        sp.wait_ge(lo_v, i * PER_EXPERT + (m - RING + 1))
                    if w == "d":
                        src = views[w][bass.ds(e, 1), 2 * c + j, :, :].rearrange("e p x -> (e p) x")
                        dst = ring[:, m % RING, :]
                    else:
                        src = views[w][bass.ds(e, 1), j, :, :, FC * c:FC * c + FC].rearrange("e p k f -> (e p) k f")
                        dst = ring[:, m % RING, :].rearrange("p (k f) -> p k f", k=4)
                    sp.dma_start(dst, src).then_inc(landed[m % RING], 16)

            item(0, 0, True)
            sp.wait_ge(*done("hn_tok", 3))
            sp.dma_start(fgain, final_norm.partition_broadcast(P)).then_inc(gain_in, 16)
            with sp.Fori(1, EXPERTS) as e:
                item(e, e, False)
            sp.wait_ge(r_v, N_ROUTE)
            n_items = sp.value_load(ctl[0:1, 0:1], min_val=EXPERTS, max_val=ITEMS)
            with sp.Fori(EXPERTS, ITEMS) as i:
                with sp.If(i < n_items):
                    e = sp.value_load(ctl[0:1, bass.ds(i - (EXPERTS - 1), 1)], min_val=0, max_val=EXPERTS - 1)
                    item(i, e, False)
            for c in range(2):
                sp.wait_ge(fin_v, c + 2)
                sp.dma_start(out[0, P * c:P * c + P, :], out_sb[:, c, :]).then_inc(stored, 16)
            sp.wait_ge(stored, 16 * 2)

        @block.tensor
        def _(pe):
            def mm(o, lhsT, rhs, first, end, **kw):
                return pe.matmul(o, lhsT, rhs, start=first, stop=end, **kw)

            def exact(o, a, b, first, end, **kw):
                (a_h, a_l), (b_h, b_l) = a, b
                pe.matmul(o, a_h, b_h, start=first, stop=False, **kw)
                pe.matmul(o, a_h, b_l, start=False, stop=False, **kw)
                return pe.matmul(o, a_l, b_h, start=False, stop=end, **kw)

            def parts_of_load(n, at):
                return w_hi[:, n % SPLIT, at], w_lo[:, n % SPLIT, at]

            pe.wait_ge(ones_in, 16)

            def mean_squares(r):
                pe.wait_ge(*room("ms", r))
                for k in range(KD):
                    pe.wait_ge(sq_a, KD * r + k + 1)
                    i = mm(bank("ms", r)[:, 0:T], ones, hnT[:, k, :], k == 0, k == KD - 1)
                i.then_inc(made_of("ms", r), 1)

            def turn_values(li, tile, n):
                pe.wait_ge(*gone("proj", li, tile))
                pe.wait_ge(*gone("proj", li, tile + 1))
                pe.wait_ge(*room("vA", li, n))
                for c in range(2):
                    for j in range(2):
                        i = pe.transpose(bank("vA", li, n)[:, 256 * c + 128 * j:256 * c + 128 * j + 128],
                                         pr[:, tile + j, WIDE[c]], ident)
                i.then_inc(made_of("vA", li, n), 1)
                pe.wait_ge(*room("vB", li, n))
                for j in range(2):
                    i = pe.transpose(bank("vB", li, n)[:, 128 * j:128 * j + 128], pr[:, tile + j, WIDE[2]], ident)
                i.then_inc(made_of("vB", li, n), 1)

            for li in range(LAYERS):
                mean_squares(2 * li)
                wv = param('wukv')[64:128, :].rearrange("p (h c) -> p h c", h=H)[:, :, NOPE:NOPE + DV]

                def map_output(o, v, hs, mp, end=True):
                    mm(o[:, 0:T], v[0:META, 0, hs], mp[0:META, MAP_X:MAP_X + T], True, False)
                    mm(o[:, META:T], v[:, 1, hs], mp[:, 0:2 * P], False, False)
                    return mm(o[:, META + P:T], v[:, 2, hs], mp[:, 2 * P:3 * P], False, end)

                def head(h):
                    return slice(DV * h, DV * h + DV), slice(DV * (h % 2), DV * (h % 2) + DV)

                def project_out(k, tiles):
                    m = load_out(li, k // 2)
                    if tiles[0] == OUT_ORDER[0]:
                        for wait in ready(m):
                            pe.wait_ge(*wait)
                        pe.wait_ge(*room("wo", li, k))
                    for j in tiles:
                        if k == 0:
                            pe.wait_ge(ahi_a, KD * (3 * li + 1) + OUT_ORDER.index(j) + 1)
                            if j in (4, 5):
                                pe.wait_ge(*gone("o", li, j - 4))
                            else:
                                pe.wait_ge(alo_v, LO_LAYER * li + KD + LO_ORDER.index(j) + 1)
                        at_ = slice(FW * j + P * (k % 2), FW * j + P * (k % 2) + P)
                        i = exact(bank("wo", li, k)[:, 0:T], parts_of_load(m, at_), (a_hi[:, j, :], a_lo[:, j, :]),
                                  j == OUT_ORDER[0], j == OUT_ORDER[-1])
                    if tiles[-1] == OUT_ORDER[-1]:
                        i.then_inc(made_of("wo", li, k), 1)

                for step, *of in MIXER:
                    if step == "out":
                        project_out(of[0], OUT_ORDER[:6])
                    if step == "load":
                        n, = of
                        _, w, tiles = IN_LOADS[n]
                        m = load_in(li, n)
                        for wait in ready(m):
                            pe.wait_ge(*wait)
                        for t, c0 in tiles:
                            pe.wait_ge(*room("proj", li, t))
                            for k in range(KD):
                                if t == TILE_ORDER[0]:
                                    pe.wait_ge(ahi_a, KD * 3 * li + k + 1)
                                    pe.wait_ge(alo_v, LO_LAYER * li + k + 1)
                                at_ = slice(w * k + c0, w * k + c0 + P)
                                i = exact(bank("proj", li, t)[:, 0:T], parts_of_load(m, at_), (a_hi[:, k, :], a_lo[:, k, :]),
                                          k == 0, k == KD - 1)
                            i.then_inc(made_of("proj", li, t), 1)
                    if step == "gate":
                        pe.wait_ge(tables_in, 16 * 2)
                        pe.wait_ge(params_in, 16 * (li + 1))
                        pe.wait_ge(*gone("proj", li, ALR))
                        pe.wait_ge(*room("gate", li))
                        for c in range(3):
                            i = mm(bank("gate", li)[:, P * c:P * c + P], pr[0:META, ALR, WIDE[c]], param('wgate')[0:META, :], True, True)
                        i.then_inc(made_of("gate", li), 1)
                    if step == "turn":
                        turn_values(li, (AV, RV, DVT)[of[0]], of[0])
                    if step == "swap":
                        j, = of
                        pe.wait_ge(*gone("proj", li, RQ + j))
                        pe.wait_ge(*room("swap", li, j))
                        mm(bank("swap", li, j)[:, 0:T], const("swap_ret"), pr[:, RQ + j, :], True, True)\
                            .then_inc(made_of("swap", li, j), 1)
                    if step == "cum":
                        pe.wait_ge(gla_v, 5 * li + 2)
                        pe.wait_ge(*room("cum", li))
                        for c in range(3):
                            a = (0, META, META + P)[c]
                            i = mm(bank("cum", li)[:, a:a + ROWS[c]], gx[0:ROWS[c], P * c:P * c + P],
                                   const("cum")[0:ROWS[c], 0:ROWS[c]], True, True)
                        i.then_inc(made_of("cum", li), 1)
                    if step == "cvar":
                        b = bank("cvar", li)
                        pe.wait_ge(c_a, 2 * li + 2)
                        pe.wait_ge(*room("cvar", li))
                        for c in range(3):
                            mm(b[:, 2 * c:2 * c + 1], rms[:, 0, WIDE[c]], ones[:, 0:1], True, False)
                            mm(b[:, 2 * c:2 * c + 1], rms[:, 1, WIDE[c]], const("heads")[:, 0:1], False, True)
                            i = mm(b[:, 2 * c + 1:2 * c + 2], rms[:, 1, WIDE[c]], const("heads")[:, 1:2], True, True)
                        i.then_inc(made_of("cvar", li), 1)
                        pe.wait_ge(*gone("proj", li, KPE))
                        pe.wait_ge(*room("kswap", li))
                        mm(bank("kswap", li)[64:96, 0:T], const("swap_mla")[64:96, :], pr[64:96, KPE, :], True, True)\
                            .then_inc(made_of("kswap", li), 1)
                    if step == "cbc":
                        pe.wait_ge(c_p, li + 1)
                        for name, parts in (("cq", ((slice(0, P), 0),)), ("ckv", ((slice(0, 64), 0), (slice(64, P), 1)))):
                            pe.wait_ge(*room(name, li))
                            for rows, j in parts:
                                for c, q in enumerate(ROWS):
                                    a = (0, META, META + P)[c]
                                    r = c3[0:q, 2 * c + j:2 * c + j + 1].to_broadcast([q, rows.stop - rows.start])
                                    i = mm(bank(name, li)[rows, a:a + q], r, ident[0:q, 0:q], True, True)
                            i.then_inc(made_of(name, li), 1)
                    if step == "mq":
                        h, = of
                        hs = slice(MLA_DK * h, MLA_DK * h + MLA_DK)
                        pe.wait_ge(*gone("cq", li))
                        pe.wait_ge(*gone("ckv", li))
                        pe.wait_ge(*room("mq", li, h))
                        mm(bank("mq", li, h)[0:MLA_DK, 0:T], param('wuq0')[:, hs], pr[:, CQ, :], True, False)
                        mm(bank("mq", li, h)[0:MLA_DK, 0:T], param('wuq1')[0:64, hs], pr[0:64, CKV, :], False, True)\
                            .then_inc(made_of("mq", li, h), 1)
                    if step == "mk":
                        h, = of
                        pe.wait_ge(*gone("ckv", li))
                        pe.wait_ge(*room("mk", li, h))
                        mm(bank("mk", li, h)[0:NOPE, 0:T], param('wukv')[64:128, P * h:P * h + NOPE], pr[64:128, CKV, :], True, True)\
                            .then_inc(made_of("mk", li, h), 1)
                    if step == "mv":
                        pe.wait_ge(*room("mvA", li))
                        for c in range(2):
                            i = mm(bank("mvA", li)[:, 256 * c:256 * c + 256], pr[64:128, CKV, WIDE[c]], wv, True, True)
                        i.then_inc(made_of("mvA", li), 1)
                        pe.wait_ge(*room("mvB", li))
                        mm(bank("mvB", li)[:, 0:256], pr[64:128, CKV, WIDE[2]], wv, True, True).then_inc(made_of("mvB", li), 1)
                    if step == "qswap":
                        h, = of
                        pe.wait_ge(*gone("mq", li, h))
                        pe.wait_ge(*room("qswap", li, h))
                        mm(bank("qswap", li, h)[64:96, 0:T], const("swap_mla")[64:96, :], qc[64:96, h, :], True, True)\
                            .then_inc(made_of("qswap", li, h), 1)
                    if step == "kd":
                        pe.wait_ge(gla_v, 5 * li + 4)
                        pe.wait_ge(*room("kd", li))
                        for c, (a, q) in enumerate(((0, META), (META, P), (META + P, CHUNK))):
                            i = pe.transpose(bank("kd", li)[0:q, P * c:P * c + P], kdT[:, a:a + q], ident)
                        i.then_inc(made_of("kd", li), 1)
                    if step == "up":
                        pe.wait_ge(*gone("kd", li))
                        pe.wait_ge(*gone("vA", li, 0))
                        pe.wait_ge(*gone("vB", li, 0))
                        for name, parts in (("upA", ((0, 0, META), (1, 0, CHUNK))), ("upB", ((1, CHUNK, CHUNK),)), ("upC", ((2, 0, CHUNK),))):
                            pe.wait_ge(*room(name, li))
                            for j, (c, p0, q) in enumerate(parts):
                                i = mm(bank(name, li)[:, 256 * j:256 * j + 256], kd_tok[p0:p0 + q, P * c:P * c + P],
                                       va[p0:p0 + q, c, :], True, True)
                            i.then_inc(made_of(name, li), 1)
                    if step == "gs":
                        h, = of
                        d = slice(GLA_DK * h, GLA_DK * h + GLA_DK)
                        pe.wait_ge(gla_v, 5 * li + 5)
                        pe.wait_ge(*room("gs", li, h))
                        for j, c in enumerate((1, 2, 0)):
                            i = mm(bank("gs", li, h)[:, P * j:P * j + P], pr[d, AK, WIDE[c]], pr[d, AQ, WIDE[c]], True, True,
                                   tile_position=(GLA_DK * h, 0))
                        i.then_inc(made_of("gs", li, h), 1)
                    if step == "go":
                        t, = of
                        b = bank("go", li, t)
                        pe.wait_ge(*room("go", li, t))
                        for h in (2 * t, 2 * t + 1):
                            hs, rows = head(h)
                            mp = gm[:, h % 2, :]
                            pe.wait_ge(*gone("gs", li, h))
                            mm(b[rows, WIDE[1]], va[:, 1, hs], mp[:, 0:128], True, False, skip_group_check=True)
                            mm(b[rows, WIDE[2]], va[:, 2, hs], mp[:, 128:256], False, False, skip_group_check=True)
                            mm(b[rows, 0:META], va[0:META, 0, hs], mp[0:META, 256:256 + META], False, False, skip_group_check=True)
                        pe.wait_ge(st_v, 4 * li + 4)
                        for n in range(4):
                            a = META + CHUNK * n
                            i = mm(b[:, a:a + CHUNK], state[n][:, P * t:P * t + P], pr[:, AQ, a:a + CHUNK], False, n == 3,
                                   skip_group_check=True)
                        i.then_inc(made_of("go", li, t), 1)
                    if step == "rs":
                        h, = of
                        d = slice(RET_DK * (h % 2), RET_DK * (h % 2) + RET_DK)
                        qt, kt = pr[d, RQ + h // 2, :], pr[d, RK + h // 2, :]
                        pe.wait_ge(rot_v, 8 * li + 8)
                        pe.wait_ge(*room("rsM", li, h))
                        mm(bank("rsM", li, h)[0:META, 0:T], kt[:, 0:META], qt, True, True).then_inc(made_of("rsM", li, h), 1)
                        pe.wait_ge(*room("rsX", li, h))
                        b = bank("rsX", li, h)
                        mm(b[:, 0:256], kt[:, WIDE[1]], qt[:, META:T], True, True)
                        mm(b[:, 256:384], kt[:, WIDE[2]], qt[:, WIDE[2]], True, True).then_inc(made_of("rsX", li, h), 1)
                    if step == "ro":
                        t, = of
                        pe.wait_ge(*gone("vA", li, 1))
                        pe.wait_ge(*gone("vB", li, 1))
                        pe.wait_ge(*room("ro", li, t))
                        for h in (2 * t, 2 * t + 1):
                            hs, rows = head(h)
                            pe.wait_ge(*gone("rsM", li, h))
                            pe.wait_ge(*gone("rsX", li, h))
                            i = map_output(bank("ro", li, t)[rows, :], vr, hs, gm[:, h % 2, :])
                        i.then_inc(made_of("ro", li, t), 1)
                    if step == "rc":
                        t, = of
                        pe.wait_ge(*gone("ro", li, t))
                        pe.wait_ge(*room("rc", li, t))
                        mm(bank("rc", li, t)[:, 0:T], const("center"), ob[t], True, True).then_inc(made_of("rc", li, t), 1)
                    if step == "sc":
                        m, = of
                        b = bank("sc", li, m)
                        if m >= MLA_MAPS:
                            n = m - MLA_MAPS
                            d = slice(DIFF_DK * (n % 4), DIFF_DK * (n % 4) + DIFF_DK)
                            q, k = pr[d, DQ + n // 4, :], pr[d, DK + n // 4, :]
                            kw = {"tile_position": (DIFF_DK * (n % 4), 0)}
                            pe.wait_ge(*gone("proj", li, DK + n // 4))
                        else:
                            q, k, kw = qc[0:MLA_DK, m, :], kc[0:MLA_DK, m, :], {}
                            pe.wait_ge(*gone("mk", li, m))
                            pe.wait_ge(rk_v, 2 * li + 2)
                            pe.wait_ge(rq_v, 8 * li + 2 * m + 2)
                        pe.wait_ge(*room("sc", li, m))
                        mm(b[:, 0:T], q[:, WIDE[2]], k, True, True, **kw)
                        mm(b[:, T:T + 144], q[:, WIDE[1]], k[:, 0:144], True, True, **kw)
                        mm(b[:, T + 144:T + 160], q[:, WIDE[0]], k[:, 0:META], True, True, **kw).then_inc(made_of("sc", li, m), 1)
                    if step == "pt":
                        u, = of
                        pb = probs[:, first_map(u) % 4, :]
                        if u >= MLA_MAPS:
                            pe.wait_ge(w_v, 4 * li + u - MLA_MAPS + 1)
                        else:
                            pe.wait_ge(scaled_a, UNITS * li + u + 1)
                        pe.wait_ge(*room("ptM", li, u))
                        b = bank("ptM", li, u)
                        pe.transpose(b[0:META, 0:META], pb[0:META, T + 144:T + 160], ident[0:META, 0:META])
                        pe.transpose(b[0:META, WIDE[1]], pb[:, T:T + META], ident)
                        pe.transpose(b[0:META, WIDE[2]], pb[:, 0:META], ident).then_inc(made_of("ptM", li, u), 1)
                        pe.wait_ge(*room("ptX", li, u))
                        b = bank("ptX", li, u)
                        pe.transpose(b[:, 0:128], pb[:, T + META:T + 144], ident)
                        pe.transpose(b[:, 128:256], pb[:, WIDE[1]], ident)
                        pe.transpose(b[:, 256:384], pb[:, WIDE[2]], ident).then_inc(made_of("ptX", li, u), 1)
                    if step == "o":
                        u, = of
                        v, h = (vm, u) if u < MLA_MAPS else (vd, u - MLA_MAPS)
                        hs, rows = head(h)
                        for name in ((("mvA", li), ("mvB", li)) if u < MLA_MAPS else (("vA", li, 2), ("vB", li, 2))):
                            pe.wait_ge(*gone(*name))
                        pe.wait_ge(*gone("ptX", li, u))
                        pe.wait_ge(*gone("ptM", li, u))
                        if u % 2 == 0:
                            pe.wait_ge(*room("o", li, u // 2))
                        map_output(bank("o", li, u // 2)[rows, :], v, hs, pt[:, u % 2, :])\
                            .then_inc(made_of("o", li, u // 2) if u % 2 else o_used, 1)
                    if step == "var":
                        kind, = of
                        b = bank("var", li, kind)
                        pe.wait_ge(sq_n, 6 * li + max(SQUARED.index((kind, t)) for t in range(2)) + 1)
                        pe.wait_ge(*room("var", li, kind))
                        for c in range(3):
                            for t in range(2):
                                i = mm(b[:, H * c:H * c + H], sq[:, 2 * (NORMS.index(kind) % 2) + t, WIDE[c]], const("heads")[:, H * t:H * t + H], t == 0, t == 1)
                        i.then_inc(made_of("var", li, kind), 1)
                    if step == "bc":
                        kind, t = of
                        b = bank("bc", li, kind, t)
                        roots = st3[:, NORMS.index(kind), :]
                        pe.wait_ge(root_p, 3 * li + NORMS.index(kind) + 1)
                        pe.wait_ge(*room("bc", li, kind, t))
                        for c, q in enumerate(ROWS):
                            a = (0, META, META + P)[c]
                            for h in (2 * t, 2 * t + 1):
                                r = roots[0:q, H * c + h:H * c + h + 1].to_broadcast([q, DV])
                                i = mm(b[head(h)[1], a:a + q], r, ident[0:q, 0:q], True, True)
                        i.then_inc(made_of("bc", li, kind, t), 1)

                for k in range(EARLY):
                    project_out(k, OUT_ORDER[6:])
                for k in range(EARLY, KD):
                    project_out(k, OUT_ORDER)
                mean_squares(2 * li + 1)

                if li == 0:
                    for c in range(FF_GROUPS):
                        for name, m in (("fg", load_gate(c)), ("fu", load_up(c))):
                            for wait in ready(m):
                                pe.wait_ge(*wait)
                            for f in (2 * c, 2 * c + 1):
                                pe.wait_ge(*room(name, f))
                                for k in range(KD):
                                    if f == 0 and name == "fg":
                                        pe.wait_ge(ahi_a, KD * 2 + k + 1)
                                        pe.wait_ge(alo_v, 2 * KD - 2 + k + 1)
                                    at_ = slice(FW * k + P * (f % 2), FW * k + P * (f % 2) + P)
                                    i = exact(bank(name, f)[:, 0:T], parts_of_load(m, at_), (a_hi[:, k, :], a_lo[:, k, :]),
                                              k == 0, k == KD - 1)
                                i.then_inc(made_of(name, f), 1)
                    for pair in range(4):
                        for j, nt in enumerate(FF_ROWS):
                            m = load_down(pair, j)
                            for wait in ready(m):
                                pe.wait_ge(*wait)
                            for k in (2 * pair, 2 * pair + 1):
                                if j == 0:
                                    pe.wait_ge(*room("fd", k))
                                for ft in range(nt):
                                    f = 8 * j + ft
                                    if k == 0:
                                        pe.wait_ge(ff_a, f + 1)
                                        pe.wait_ge(ff_v, f + 1)
                                    at_ = slice(FW * ft + P * (k % 2), FW * ft + P * (k % 2) + P)
                                    i = exact(bank("fd", k)[:, 0:T], parts_of_load(m, at_), (f_hi[:, f, :], f_lo[:, f, :]),
                                              f == 0, f == FT - 1)
                                if j == len(FF_ROWS) - 1:
                                    i.then_inc(made_of("fd", k), 1)
                                elif k % 2:
                                    i.then_inc(part_used, 1)

            pe.wait_ge(*room("logitsT"))
            for k in range(KD):
                pe.wait_ge(hn_v, 3 * KD + k + 1)
                i = mm(bank("logitsT")[0:EXPERTS, 0:SEQ], wrout[:, k, :], hnT[:, k, META:T], k == 0, k == KD - 1)
            i.then_inc(made_of("logitsT"), 1)
            for j in range(4):
                c, k0 = 1 + j // 2, 4 * (j % 2)
                pe.wait_ge(*room("hn_tok", j))
                for k in range(4):
                    i = pe.transpose(bank("hn_tok", j)[:, P * k:P * k + P], hnT[:, k0 + k, WIDE[c]], ident)
                i.then_inc(made_of("hn_tok", j), 1)
            pe.wait_ge(*room("logits"))
            for c in range(2):
                i = pe.transpose(bank("logits")[:, EXPERTS * c:EXPERTS * c + EXPERTS], logitsT[:, P * c:P * c + P],
                                 ident[0:EXPERTS, 0:EXPERTS])
            i.then_inc(made_of("logits"), 1)
            pe.wait_ge(r_v, R_MASK)
            m0, m1 = route[:, R["mask"]:R["mask"] + 8], route[:, R["mask"] + 8:R["mask"] + 16]
            b = bank("pos")
            pe.wait_ge(*room("pos"))
            mm(b[:, 0:8], const("upper"), m0, True, True)
            mm(b[:, 8:16], ones, m0, True, False)
            mm(b[:, 8:16], const("upper"), m1, False, True).then_inc(made_of("pos"), 1)
            pe.wait_ge(*room("count"))
            mm(bank("count")[:, 0:8], ones, m0, True, False)
            mm(bank("count")[:, 0:8], ones, m1, False, True).then_inc(made_of("count"), 1)
            for j in range(4):
                pe.wait_ge(*gone("hn_tok", j))

            def gather(i):
                pe.wait_ge(sel_v, 2 * i + 2)
                for j in range(4):
                    src = (hn_hi, hn_lo)[j // 2]
                    pe.wait_ge(*room_i(i, "xg", j))
                    for k in range(4):
                        for c in range(2):
                            f = P * (4 * (j % 2) + k)
                            m = mm(bank("xg", j)[:, P * k:P * k + P], src[:, c, f:f + P], sel[:, c, :], c == 0, c == 1)
                    m.then_inc(made_of("xg", j), 1)

            def back(i, js):
                pe.wait_ge(*gone_i(i, "selT", before=1))
                for j in js:
                    c, half = j // 2, j % 2
                    hs = slice(FC * half, FC * half + FC)
                    pe.wait_ge(*gone_i(i, "y", half, before=1))
                    pe.wait_ge(*room_i(i, "back", j, before=1))
                    mm(bank("back", j), selT[:, c, :], y_hi[:, hs], True, False)
                    mm(bank("back", j), selT[:, c, :], y_lo[:, hs], False, True).then_inc(made_of("back", j), 1)

            def item(i, first):
                def turn(c):
                    pe.wait_ge(*gone_i(i, "u", c))
                    pe.wait_ge(*room_i(i, "aT", c))
                    v = act_sb[:, c % 2, :].rearrange("p (j f r) -> p j r f", j=2, r=2)
                    for j in range(4):
                        m = pe.transpose(bank("aT", c)[:, P * j:P * j + P], v[:, j // 2, j % 2, :], ident)
                    m.then_inc(made_of("aT", c), 1)

                for n, (w, c, j) in enumerate(ITEM):
                    turned = turned_after(w, c, j)
                    if turned is not None:
                        turn(turned)
                        if turned == NFC - 1:
                            gather(i + 1)
                    if n in BACK and not first:
                        back(i, BACK[n])
                    if n == SEL_TURN:
                        pe.wait_ge(*room_i(i, "selT"))
                        for q in range(2):
                            m = pe.transpose(bank("selT")[:, P * q:P * q + P], sel[:, q, :].bitcast(F32), ident)
                        m.then_inc(made_of("selT"), 1)
                    for wait in ready_i(i, n):
                        pe.wait_ge(*wait)
                    if w == "d":
                        if j == 0:
                            pe.wait_ge(part_a, PA * i + c + 1)
                            pe.wait_ge(*gone_i(i, "aT", c))
                            if c == 0:
                                pe.wait_ge(*room_i(i, "y", 0))
                                pe.wait_ge(*room_i(i, "y", 1))
                        for r in range(2):
                            q = slice(P * (2 * j + r), P * (2 * j + r) + P)
                            for half in range(2):
                                at_ = slice(D * r + FC * half, D * r + FC * half + FC)
                                m = exact(bank("y", half), (act_hi[:, c % 2, q], act_lo[:, c % 2, q]),
                                          parts_of_load(MOE0 + n, at_), (c, j, r) == (0, 0, 0), (c, j, r) == (NFC - 1, 1, 1))
                                if (c, j, r) == (NFC - 1, 1, 1):
                                    m.then_inc(made_of("y", half), 1)
                                elif r == 1 and half == 1:
                                    m.then_inc(part_used, 1)
                        continue
                    if j == 0:
                        pe.wait_ge(*room_i(i, w, c))
                    for kk in range(4):
                        k = 4 * j + kk
                        if n < 2 and kk == 0:
                            pe.wait_ge(*gone_i(i, "xg", j))
                            pe.wait_ge(*gone_i(i, "xg", 2 + j))
                        q = slice(P * k, P * k + P)
                        m = exact(bank(w, c), (x_hi[:, q], x_lo[:, q]), parts_of_load(MOE0 + n, slice(FC * kk, FC * kk + FC)),
                                  k == 0, k == KD - 1)
                    if j:
                        m.then_inc(made_of(w, c), 1)
                    else:
                        m.then_inc(part_used, 1)

            gather(0)
            for j in range(4):
                c, k0 = 1 + j // 2, 4 * (j % 2)
                pe.wait_ge(*room("h_tok", j))
                for k in range(4):
                    i = pe.transpose(bank("h_tok", j)[:, P * k:P * k + P], hT[:, k0 + k, WIDE[c]], ident)
                i.then_inc(made_of("h_tok", j), 1)
            item(0, True)
            pe.wait_ge(r_v, N_ROUTE)
            n_items = pe.value_load(ctl[0:1, 0:1], min_val=EXPERTS, max_val=ITEMS)
            with pe.Fori(1, ITEMS) as i:
                with pe.If(i < n_items):
                    item(i, False)
            back(n_items, range(4))

        @block.scalar
        def _(act):
            def square(r, k):
                if k == 0:
                    if r == 0:
                        act.wait_ge(filled, 2)
                    else:
                        act.wait_ge(table_a, r)
                    act.activation(unread, half_neg[:, 12:13], ACT.Sqrt).then_inc(table_a, 1)
                if r:
                    act.wait_ge(*gone(*stream(r, k)))
                else:
                    act.wait_ge(x_in, 16)
                act.activation(hnT[:, k, :], hT[:, k, :], ACT.Square).then_inc(sq_a, 1)

            def first_parts(r):
                act.wait_ge(*gone("ms", r))
                act.activation(rms[:, 1, :], rms[:, 0, :], ACT.Sqrt).then_inc(rms_a, 1)
                if r < 3:
                    for k in range(KD):
                        act.wait_ge(hn_v, KD * r + k + 1)
                        act.activation(a_hi[:, k, :], hnT[:, k, :], ACT.Copy).then_inc(ahi_a, 1)

            for k in range(KD):
                square(0, k)
            split_hi(act, 0)
            for li in range(LAYERS):
                first_parts(2 * li)
                if li == 0:
                    for n in range(1, SPLIT):
                        split_hi(act, n)
                else:
                    split_hi(act, load_down(*LAST_DOWN) + SPLIT)

                def values(n, v):
                    act.wait_ge(*done("vA", li, n))
                    act.activation(v[:, 0:2, :], bank("vA", li, n)[:, :].rearrange("p (c v) -> p c v", c=2), ACT.Copy)\
                        .then_inc(taken_of("vA", li, n), 1)
                    act.wait_ge(*done("vB", li, n))
                    act.activation(v[:, 2, :], bank("vB", li, n)[:, 0:256], ACT.Copy).then_inc(taken_of("vB", li, n), 1)

                for step, *of in MIXER:
                    if step == "load":
                        n, = of
                        for t, _ in IN_LOADS[n][2]:
                            f = ACT.Silu if t in (AOG, AOG + 1, ROG, ROG + 1) else ACT.Copy
                            q = PART.get(t, slice(0, P))
                            act.wait_ge(*done("proj", li, t))
                            act.activation(pr[q, t, :], bank("proj", li, t)[q, 0:T], f).then_inc(taken_of("proj", li, t), 1)
                    if step == "first":
                        split_hi(act, load_in(li, of[0]) + SPLIT)
                    if step == "turn":
                        values(of[0], (va, vr, vd)[of[0]])
                    if step == "gsig":
                        act.wait_ge(gla_v, 5 * li + 1)
                        act.activation(gabs, gabs, ACT.Exp, scale=-1.0).then_inc(gate_a, 1)
                        act.wait_ge(lam_v, 3 * li + 2)
                        act.activation(lam[:, 2 * li:2 * li + 2], lam[:, 2 * li:2 * li + 2], ACT.Exp).then_inc(lam_a, 1)
                        act.wait_ge(gate_a, 2 * li + 1)
                        act.activation(gabs, gabs, ACT.Ln, bias=1.0).then_inc(gate_a, 1)
                    if step == "csq":
                        act.wait_ge(*gone("proj", li, CQ))
                        act.wait_ge(*gone("proj", li, CKV))
                        act.activation(rms[:, 0, :], pr[:, CQ, :], ACT.Square).then_inc(c_a, 1)
                        act.activation(rms[:, 1, :], pr[:, CKV, :], ACT.Square).then_inc(c_a, 1)
                    if step == "dec":
                        act.wait_ge(*gone("cum", li))
                        act.activation(eq, cumT, ACT.Exp).then_inc(cum_a, 1)
                        act.activation(ek, cumT, ACT.Exp, scale=-1.0).then_inc(cum_a, 1)
                        for a, e in ((0, 16), (16, 80), (80, 144), (144, 208)):
                            act.activation(ekd[:, a:e], cumT[:, a:e], ACT.Exp, bias=cumT[:, e - 1:e], scale=-1.0)\
                                .then_inc(cum_a, 1)
                    if step == "mq":
                        h, = of
                        act.wait_ge(*done("mq", li, h))
                        act.activation(qc[0:MLA_DK, h, :], bank("mq", li, h)[0:MLA_DK, 0:T], ACT.Copy).then_inc(taken_of("mq", li, h), 1)
                    if step == "mk":
                        h, = of
                        act.wait_ge(*done("mk", li, h))
                        act.activation(kc[0:NOPE, h, :], bank("mk", li, h)[0:NOPE, 0:T], ACT.Copy).then_inc(taken_of("mk", li, h), 1)
                    if step == "mv":
                        act.wait_ge(*done("mvA", li))
                        act.activation(vm[:, 0:2, :], bank("mvA", li)[:, :].rearrange("p (c v) -> p c v", c=2), ACT.Copy)\
                            .then_inc(taken_of("mvA", li), 1)
                        act.wait_ge(*done("mvB", li))
                        act.activation(vm[:, 2, :], bank("mvB", li)[:, 0:256], ACT.Copy).then_inc(taken_of("mvB", li), 1)
                    if step == "rcopy":
                        t, = of
                        act.wait_ge(*done("ro", li, t))
                        act.activation(ob[t], bank("ro", li, t)[:, 0:T], ACT.Copy).then_inc(taken_of("ro", li, t), 1)
                    if step == "sc":
                        m, = of
                        act.wait_ge(*gone("sc", li, m))
                        pb = probs[:, m % 4, :]
                        for c, a, e in ((2, 0, T), (1, T, T + 144), (0, T + 144, T + 160)):
                            i = act.activation(pb[:, a:e], pb[:, a:e], ACT.Exp, bias=neg_max[:, m, c:c + 1], scale=-1.0,
                                               accum_out=den[:, m, c:c + 1])
                        i.then_inc(exp_a, 1)
                    if step == "r":
                        u, = of
                        m = first_map(u)
                        pb = probs[:, m % 4, :]
                        act.wait_ge(rd_v, UNITS * li + u + 1)
                        for c, a, e in ((2, 0, T), (1, T, T + 144), (0, T + 144, T + 160)):
                            i = act.activation(pb[:, a:e], pb[:, a:e], ACT.Copy, scale=rden[:, m, c:c + 1])
                        i.then_inc(scaled_a, 1)
                    if step == "pt":
                        u, = of
                        act.wait_ge(*done("ptM", li, u))
                        if u >= 2:
                            act.wait_ge(*unit_out(li, u - 2))
                        act.activation(pt[0:META, u % 2, MAP_X:MAP_X + T], bank("ptM", li, u)[0:META, 0:T], ACT.Copy)\
                            .then_inc(taken_of("ptM", li, u), 1)
                    if step == "sq":
                        kind, t = of
                        if NORMS.index(kind) >= 2:
                            act.wait_ge(*done("var", li, NORMS[NORMS.index(kind) - 2]))
                        act.wait_ge(*done(*normed(kind, li, t)))
                        act.activation(sq[:, 2 * (NORMS.index(kind) % 2) + t, :], bank(*normed(kind, li, t))[:, 0:T], ACT.Square).then_inc(sq_n, 1)
                    if step == "bc":
                        kind, t = of
                        k = NORMED[kind][t]
                        act.wait_ge(*gone("bc", li, kind, t))
                        act.activation(a_hi[:, k, :], oT[:, k, :], ACT.Copy).then_inc(ahi_a, 1)
                    if step == "mo":
                        t, = of
                        act.wait_ge(*done("o", li, t))
                        act.activation(a_hi[:, t + 4, :], bank("o", li, t)[:, 0:T], ACT.Copy).then_inc(ahi_a, 1)
                for n in range(4):
                    if n < 3:
                        split_hi(act, load_out(li, n) + SPLIT)
                    square(2 * li + 1, 2 * n)
                    square(2 * li + 1, 2 * n + 1)
                first_parts(2 * li + 1)
                split_hi(act, load_out(li, 3) + SPLIT)
                if li == 0:
                    for c in range(FF_GROUPS):
                        for f in (2 * c, 2 * c + 1):
                            act.wait_ge(*done("fg", f))
                            if f >= 2:
                                act.wait_ge(*gone("fu", f - 2))
                            act.activation(ffs[:, f % 2, :], bank("fg", f)[:, 0:T], ACT.Silu).then_inc(taken_of("fg", f), 1)
                        split_hi(act, load_gate(c) + SPLIT)
                        for f in (2 * c, 2 * c + 1):
                            act.wait_ge(*gone("fu", f))
                            act.activation(f_hi[:, f, :], ffa[:, f % 3, :], ACT.Copy).then_inc(ff_a, 1)
                        split_hi(act, load_up(c) + SPLIT)
                    for pair in range(4):
                        for j in range(len(FF_ROWS)):
                            if j == len(FF_ROWS) - 1:
                                for k in (2 * pair, 2 * pair + 1):
                                    square(2, k)
                            if (pair, j) != LAST_DOWN:
                                split_hi(act, load_down(pair, j) + SPLIT)
            act.wait_ge(*done("logitsT"))
            act.activation(logitsT, bank("logitsT")[0:EXPERTS, 0:SEQ], ACT.Copy).then_inc(taken_of("logitsT"), 1)
            for j in range(4):
                act.wait_ge(*done("hn_tok", j))
                act.activation(hn_hi[:, j // 2, FC * (j % 2):FC * (j % 2) + FC], bank("hn_tok", j), ACT.Copy).then_inc(tok_a, 1)
            act.wait_ge(r_v, R_EXP)
            act.activation(route[:, R["e"]:R["e"] + 2], route[:, R["d"]:R["d"] + 2], ACT.Exp).then_inc(r_a, 1)

            def tokens(i):
                for j in range(2):
                    act.wait_ge(*done_i(i, "xg", j))
                    act.activation(x_hi[:, FC * j:FC * j + FC], bank("xg", j), ACT.Copy).then_inc(taken_of("xg", j), 1)

            def item(i, first):
                def first_part(dst, *name):
                    act.wait_ge(*done_i(i, *name))
                    act.activation(dst, bank(*name), ACT.Copy).then_inc(part_a, 1)

                if not first:
                    split_hi_i(act, i, SPLIT - 1)
                for n, (w, c, j) in enumerate(ITEM):
                    if (w, j) == ("g", 1):
                        act.wait_ge(*done_i(i, "g", c))
                        if c >= 2:
                            act.wait_ge(*gone_i(i, "u", c - 2))
                        act.activation(sg[:, c % 2, :], bank("g", c), ACT.Silu).then_inc(taken_of("g", c), 1)
                    turned = turned_after(w, c, j)
                    if turned is not None:
                        if turned >= 2:
                            act.wait_ge(*used_i(i, ITEM.index(("d", turned - 2, 1))))
                        first_part(act_hi[:, turned % 2, :], "aT", turned)
                        if turned == NFC - 1:
                            tokens(i + 1)
                    if n + SPLIT < PER_EXPERT:
                        split_hi_i(act, i, n + SPLIT)
                if first:
                    for n in range(SPLIT - 1):
                        split_hi_i(act, i, PER_EXPERT + n)
                else:
                    with act.If(i + 1 < n_items):
                        for n in range(SPLIT - 1):
                            split_hi_i(act, i, PER_EXPERT + n)
                for half in range(2):
                    first_part(y_hi[:, FC * half:FC * half + FC], "y", half)

            tokens(0)
            for j in range(4):
                act.wait_ge(*done("h_tok", j))
                act.activation(h_tok[:, j // 2, FC * (j % 2):FC * (j % 2) + FC], bank("h_tok", j), ACT.Copy)\
                    .then_inc(taken_of("h_tok", j), 1)
            item(0, True)
            act.wait_ge(r_v, N_ROUTE)
            n_items = act.value_load(ctl[0:1, 0:1], min_val=EXPERTS, max_val=ITEMS)
            with act.Fori(1, ITEMS) as i:
                with act.If(i < n_items):
                    item(i, False)
            act.wait_ge(*gone_i(n_items, "back", 3, before=1))
            for c in range(2):
                act.activation(out_sb[:, c, :], h_tok[:, c, :], ACT.Square, accum_out=den[:, 0, c:c + 1]).then_inc(fin_a, 1)

        @block.vector
        def _(dve):
            def normalize(r):
                dve.wait_ge(*done("ms", r))
                dve.tensor_scalar(rms[:, 0, :], bank("ms", r)[:, 0:T], 1.0 / D, EPS, ALU.mult, ALU.add)\
                    .then_inc(taken_of("ms", r), 1)
                dve.wait_ge(rms_a, r + 1)
                dve.reciprocal(rms[:, 0, :], rms[:, 1, :]).then_inc(rstd_v, 1)
                dve.wait_ge(rstd_v, r + 1)
                if r == 0:
                    dve.wait_ge(cols_in, 16)

                def second_part(k):
                    dve.wait_ge(ahi_a, KD * (0, 2, 3)[r] + k + 1)
                    dve.tensor_tensor(a_lo[:, k, :], hnT[:, k, :], a_hi[:, k, :].bitcast(F32), ALU.subtract).then_inc(alo_v, 1)

                for k in range(KD):
                    dve.scalar_tensor_tensor(out=hnT[:, k, :], in0=hT[:, k, :], scalar=gain("ffn" if r % 2 else "attn", r // 2, k),
                                             in1=rms[:, 0, :], op0=ALU.mult, op1=ALU.mult).then_inc(hn_v, 1)
                    if k and r < 3:
                        second_part(k - 1)
                if r < 3:
                    second_part(KD - 1)

            def out_part(li, k):
                dve.wait_ge(ahi_a, KD * (3 * li + 1) + OUT_ORDER.index(k) + 1)
                dve.tensor_tensor(a_lo[:, k, :], oT[:, k, :], a_hi[:, k, :].bitcast(F32), ALU.subtract).then_inc(alo_v, 1)

            for li in range(LAYERS):
                if li == 0:
                    split_lo(dve, 0)
                normalize(2 * li)
                if li == 0:
                    for n in range(1, SPLIT):
                        split_lo(dve, n)
                else:
                    split_lo(dve, load_down(*LAST_DOWN) + SPLIT)

                def rotate(j):
                    dve.wait_ge(*gone("proj", li, RQ + j))
                    dve.wait_ge(*((rot_v, 8 * li + 2 * j) if j else (rk_v, 2 * li + 2)))
                    dve.tensor_tensor(t1, pr[:, RQ + j, :], const("cos_ret"), ALU.mult).then_inc(rot_v, 1)
                    dve.wait_ge(*done("swap", li, j))
                    dve.tensor_tensor(t2, bank("swap", li, j)[:, 0:T], const("sin_ret"), ALU.mult).then_inc(taken_of("swap", li, j), 1)
                    dve.wait_ge(rot_v, 8 * li + 2 * j + 1)
                    dve.wait_ge(*gone("swap", li, j))
                    dve.tensor_tensor(pr[:, RQ + j, :], t1, t2, ALU.add).then_inc(rot_v, 1)

                r4 = slice(64, 96)
                for step, *of in MIXER:
                    if step == "second":
                        split_lo(dve, load_in(li, of[0]) + SPLIT)
                    if step == "gate":
                        dve.wait_ge(*done("gate", li))
                        dve.tensor_tensor(gx.rearrange("p (c f) -> p c f", c=3), bank("gate", li)[:, 0:384].rearrange("p (c f) -> p c f", c=3),
                                          param("bgate").unsqueeze(1).to_broadcast([P, 3, P]), ALU.add).then_inc(taken_of("gate", li), 1)
                        dve.wait_ge(*gone("gate", li))
                        dve.scalar_tensor_tensor(out=gabs, in0=gx, scalar=-1.0, in1=gx, op0=ALU.mult, op1=ALU.max).then_inc(gla_v, 1)
                        lv = param("dlam").rearrange("p (n d) -> p n d", n=4)
                        for j in range(2):
                            dve.tensor_tensor_reduce(kdT[:, 32 * j:32 * j + 32], lv[:, 2 * j, :], lv[:, 2 * j + 1, :], 1.0, 0.0,
                                                     ALU.mult, ALU.add, lam[:, 2 * li + j:2 * li + j + 1]).then_inc(lam_v, 1)
                    if step == "swap":
                        rotate(of[0])
                    if step == "gfin":
                        dve.wait_ge(gate_a, 2 * li + 2)
                        dve.scalar_tensor_tensor(out=gx, in0=gx, scalar=0.0, in1=gabs, op0=ALU.min, op1=ALU.subtract).then_inc(gla_v, 1)
                        dve.wait_ge(lam_a, li + 1)
                        dve.scalar_tensor_tensor(out=lam[:, 4 + li:5 + li], in0=lam[:, 2 * li + 1:2 * li + 2], scalar=-LAM_INIT[li],
                                                 in1=lam[:, 2 * li:2 * li + 1], op0=ALU.add, op1=ALU.subtract).then_inc(lam_v, 1)
                    if step == "cum":
                        dve.wait_ge(*done("cum", li))
                        dve.tensor_copy(cumT, bank("cum", li)[:, 0:T]).then_inc(taken_of("cum", li), 1)
                    if step == "dec":
                        dve.wait_ge(*gone("proj", li, AK))
                        dve.wait_ge(cum_a, 6 * li + 6)
                        dve.scalar_tensor_tensor(out=pr[:, AQ, :], in0=pr[:, AQ, :], scalar=GLA_DK**-0.5, in1=eq, op0=ALU.mult, op1=ALU.mult)\
                            .then_inc(gla_v, 1)
                        dve.tensor_tensor(kdT[:, 0:208], pr[:, AK, 0:208], ekd[:, 0:208], ALU.mult).then_inc(gla_v, 1)
                        dve.wait_ge(gla_v, 5 * li + 4)
                        dve.tensor_tensor(pr[:, AK, :], pr[:, AK, :], ek, ALU.mult).then_inc(gla_v, 1)
                    if step == "cvar":
                        dve.wait_ge(*done("cvar", li))
                        by_kind = [a.rearrange("p (c n) -> p n c", c=3) for a in (c2, bank("cvar", li)[:, 0:6])]
                        dve.tensor_scalar(by_kind[0][:, 0, :], by_kind[1][:, 0, :], 1.0 / Q_RANK, EPS, ALU.mult, ALU.add)
                        dve.tensor_scalar(by_kind[0][:, 1, :], by_kind[1][:, 1, :], 1.0 / 64, EPS, ALU.mult, ALU.add)\
                            .then_inc(taken_of("cvar", li), 1)
                        dve.tensor_tensor(t1[r4, :], pr[r4, KPE, :], const("cos_mla")[r4, :], ALU.mult).then_inc(rk_v, 1)
                        dve.wait_ge(*done("kswap", li))
                        dve.tensor_tensor(t2[r4, :], bank("kswap", li)[r4, 0:T], const("sin_mla")[r4, :], ALU.mult)\
                            .then_inc(taken_of("kswap", li), 1)
                        dve.wait_ge(rk_v, 2 * li + 1)
                        dve.wait_ge(*gone("kswap", li))
                        dve.tensor_tensor(kc[r4, :, :], t1[r4, :].unsqueeze(1).to_broadcast([32, H, T]),
                                          t2[r4, :].unsqueeze(1).to_broadcast([32, H, T]), ALU.add).then_inc(rk_v, 1)
                    if step == "cbc":
                        dve.wait_ge(*done("cq", li))
                        dve.scalar_tensor_tensor(out=pr[:, CQ, :], in0=pr[:, CQ, :], scalar=gain("q", li), in1=bank("cq", li)[:, 0:T],
                                                 op0=ALU.mult, op1=ALU.mult).then_inc(taken_of("cq", li), 1)
                        dve.wait_ge(*done("ckv", li))
                        dve.scalar_tensor_tensor(out=pr[:, CKV, :], in0=pr[:, CKV, :], scalar=gain("q_kv", li), in1=bank("ckv", li)[:, 0:T],
                                                 op0=ALU.mult, op1=ALU.mult).then_inc(taken_of("ckv", li), 1)
                    if step == "kd":
                        dve.wait_ge(*done("kd", li))
                        dve.tensor_copy(kd_tok[0:META, 0:128], bank("kd", li)[0:META, 0:128])
                        dve.tensor_copy(kd_tok[:, 128:256], bank("kd", li)[:, 128:256])
                        dve.tensor_copy(kd_tok[0:64, 256:384], bank("kd", li)[0:64, 256:384]).then_inc(taken_of("kd", li), 1)
                    if step == "qswap":
                        h, = of
                        dve.wait_ge(*gone("mq", li, h))
                        dve.wait_ge(*((rq_v, 8 * li + 2 * h) if h else (rot_v, 8 * li + 8)))
                        dve.tensor_tensor(t1[r4, :], qc[r4, h, :], const("cos_mla")[r4, :], ALU.mult).then_inc(rq_v, 1)
                        dve.wait_ge(*done("qswap", li, h))
                        dve.tensor_tensor(t2[r4, :], bank("qswap", li, h)[r4, 0:T], const("sin_mla")[r4, :], ALU.mult)\
                            .then_inc(taken_of("qswap", li, h), 1)
                        dve.wait_ge(rq_v, 8 * li + 2 * h + 1)
                        dve.wait_ge(*gone("qswap", li, h))
                        dve.tensor_tensor(qc[r4, h, :], t1[r4, :], t2[r4, :], ALU.add).then_inc(rq_v, 1)
                    if step == "up":
                        dve.wait_ge(*done("upA", li))
                        dve.tensor_tensor(state[0], bank("upA", li)[:, 0:256], const("block"), ALU.mult).then_inc(st_v, 1)
                        dve.tensor_tensor(state[1], bank("upA", li)[:, 256:512], const("block"), ALU.mult).then_inc(taken_of("upA", li), 1)
                        dve.wait_ge(*done("upB", li))
                        dve.tensor_tensor(state[2], bank("upB", li)[:, 0:256], const("block"), ALU.mult).then_inc(taken_of("upB", li), 1)
                        dve.wait_ge(*done("upC", li))
                        dve.tensor_tensor(state[3], bank("upC", li)[:, 0:256], const("block"), ALU.mult).then_inc(taken_of("upC", li), 1)
                        for name in ("upA", "upB", "upC"):
                            dve.wait_ge(*gone(name, li))
                        for j in range(3):
                            dve.wait_ge(st_v, 4 * li + 1 + j)
                            e = (80, 144, 208)[j]
                            dve.scalar_tensor_tensor(out=state[j + 1], in0=state[j], scalar=eq[:, e - 1:e], in1=state[j + 1],
                                                     op0=ALU.mult, op1=ALU.add).then_inc(st_v, 1)
                    if step == "gs":
                        h, = of
                        dve.wait_ge(*done("gs", li, h))
                        if h >= 2:
                            dve.wait_ge(*done("go", li, 0))
                        dve.tensor_tensor(gm[:, h % 2, 0:384].rearrange("p (c q) -> p c q", c=3),
                                          bank("gs", li, h)[:, 0:384].rearrange("p (c q) -> p c q", c=3),
                                          const("intra").unsqueeze(1).to_broadcast([P, 3, P]), ALU.mult).then_inc(taken_of("gs", li, h), 1)
                    if step == "rs":
                        h, = of
                        dve.wait_ge(*(done("ro", li, 0) if h >= 2 else done("go", li, 1)))
                        mp = gm[:, h % 2, :]
                        dve.wait_ge(*done("rsM", li, h))
                        dve.tensor_tensor(mp[0:META, MAP_X:MAP_X + T], bank("rsM", li, h)[0:META, 0:T], decay[0:META, h, :], ALU.mult)\
                            .then_inc(taken_of("rsM", li, h), 1)
                        dve.wait_ge(*done("rsX", li, h))
                        dve.tensor_tensor(mp[:, 0:256], bank("rsX", li, h)[:, 0:256], decay[:, h, 0:256], ALU.mult)
                        dve.tensor_tensor(mp[:, 256:384], bank("rsX", li, h)[:, 256:384], decay[:, h, 0:128], ALU.mult)\
                            .then_inc(taken_of("rsX", li, h), 1)
                    if step == "sc":
                        m, = of
                        scale = DIFF_DK**-0.5 if m >= MLA_MAPS else MLA_DK**-0.5
                        b, pb = bank("sc", li, m), probs[:, m % 4, :]
                        dve.wait_ge(*done("sc", li, m))
                        if m >= 4:
                            dve.wait_ge(*done("ptX", li, unit(m - 4)))
                        for c, a, e, q in ((2, 0, T, 0), (1, T, T + 144, 128), (0, T + 144, T + 160, 144)):
                            i = dve.tensor_tensor_reduce(pb[:, a:e], b[:, a:e], mask[:, q:q + e - a], -scale, 3e38,
                                                         ALU.add, ALU.min, neg_max[:, m, c:c + 1])
                        i.then_inc(taken_of("sc", li, m), 1)
                    if step == "r":
                        u, = of
                        m, e = first_map(u), first_map(u) + (2 if u >= MLA_MAPS else 1)
                        dve.wait_ge(exp_a, N_MAPS * li + e)
                        dve.reciprocal(rden[:, m:e, :], den[:, m:e, :]).then_inc(rd_v, 1)
                        if u >= MLA_MAPS:
                            dve.wait_ge(rd_v, UNITS * li + u + 1)
                            dve.wait_ge(lam_v, 3 * (li + 1))
                            dve.tensor_scalar(rden_l[:, u - MLA_MAPS, :], rden[:, m + 1, :], lam[:, 4 + li:5 + li], None, ALU.mult).then_inc(nl_v, 1)
                    if step == "w":
                        u, = of
                        p1, p2 = (probs[:, (first_map(u) + j) % 4, :] for j in range(2))
                        dve.wait_ge(scaled_a, UNITS * li + u + 1)
                        dve.wait_ge(nl_v, 4 * li + u - MLA_MAPS + 1)
                        for c, a, e in ((2, 0, T), (1, T, T + 144), (0, T + 144, T + 160)):
                            i = dve.scalar_tensor_tensor(out=p1[:, a:e], in0=p2[:, a:e], scalar=rden_l[:, u - MLA_MAPS, c:c + 1], in1=p1[:, a:e],
                                                         op0=ALU.mult, op1=ALU.add)
                        i.then_inc(w_v, 1)
                    if step == "pt":
                        u, = of
                        dve.wait_ge(*done("ptX", li, u))
                        if u >= 2:
                            dve.wait_ge(*unit_out(li, u - 2))
                        dve.tensor_copy(pt[:, u % 2, 0:MAP_X], bank("ptX", li, u)[:, 0:MAP_X]).then_inc(taken_of("ptX", li, u), 1)
                    if step == "sq":
                        kind, t = of
                        k, name = NORMED[kind][t], normed(kind, li, t)
                        dve.wait_ge(*done(*name))
                        dve.wait_ge(sq_n, 6 * li + SQUARED.index((kind, t)) + 1)
                        if kind == "diff":
                            dve.tensor_scalar(oT[:, k, :], bank(*name)[:, 0:T], gain("diff", li), 1.0 - LAM_INIT[li],
                                              ALU.mult, ALU.mult).then_inc(taken_of(*name), 1)
                        else:
                            gate = {"gla": AOG, "ret": ROG}[kind] + t
                            og = pr[:, gate, :]
                            dve.wait_ge(*gone("proj", li, gate))
                            dve.scalar_tensor_tensor(out=oT[:, k, :], in0=bank(*name)[:, 0:T], scalar=gain(kind, li),
                                                     in1=og, op0=ALU.mult, op1=ALU.mult).then_inc(taken_of(*name), 1)
                    if step == "var":
                        kind, = of
                        dve.wait_ge(*done("var", li, kind))
                        dve.tensor_scalar(st2[:, NORMS.index(kind), :], bank("var", li, kind)[:, 0:3 * H], 1.0 / DV, EPS, ALU.mult, ALU.add)\
                            .then_inc(taken_of("var", li, kind), 1)
                    if step == "bc":
                        kind, t = of
                        k = NORMED[kind][t]
                        dve.wait_ge(*done("bc", li, kind, t))
                        dve.wait_ge(*gone(*normed(kind, li, t)))
                        dve.tensor_tensor(oT[:, k, :], oT[:, k, :], bank("bc", li, kind, t)[:, 0:T], ALU.mult)\
                            .then_inc(taken_of("bc", li, kind, t), 1)
                    if step == "lo":
                        for k in NORMED[of[0]]:
                            out_part(li, k)
                    if step == "mo":
                        t, = of
                        dve.wait_ge(ahi_a, KD * (3 * li + 1) + OUT_ORDER.index(t + 4) + 1)
                        dve.tensor_tensor(a_lo[:, t + 4, :], bank("o", li, t)[:, 0:T], a_hi[:, t + 4, :].bitcast(F32), ALU.subtract)\
                            .then_inc(taken_of("o", li, t), 1)

                def add(name, k):
                    dve.wait_ge(*done(*name, k))
                    dve.tensor_tensor(hT[:, k, :], hT[:, k, :], bank(*name, k)[:, 0:T], ALU.add).then_inc(taken_of(*name, k), 1)

                for n in range(4):
                    add(("wo", li), 2 * n)
                    add(("wo", li), 2 * n + 1)
                    if n < 3:
                        split_lo(dve, load_out(li, n) + SPLIT)
                normalize(2 * li + 1)
                split_lo(dve, load_out(li, 3) + SPLIT)
                if li == 0:
                    for c in range(FF_GROUPS):
                        split_lo(dve, load_gate(c) + SPLIT)
                        for f in (2 * c, 2 * c + 1):
                            dve.wait_ge(*done("fu", f))
                            dve.wait_ge(*gone("fg", f))
                            if f >= 3:
                                dve.wait_ge(ff_v, f - 2)
                            dve.tensor_tensor(ffa[:, f % 3, :], ffs[:, f % 2, :], bank("fu", f)[:, 0:T], ALU.mult).then_inc(taken_of("fu", f), 1)
                        for f in (2 * c, 2 * c + 1):
                            dve.wait_ge(ff_a, f + 1)
                            dve.tensor_tensor(f_lo[:, f, :], ffa[:, f % 3, :], f_hi[:, f, :].bitcast(F32), ALU.subtract).then_inc(ff_v, 1)
                        split_lo(dve, load_up(c) + SPLIT)
                    for pair in range(4):
                        for j in range(len(FF_ROWS)):
                            if j == len(FF_ROWS) - 1:
                                add(("fd",), 2 * pair)
                                add(("fd",), 2 * pair + 1)
                            if (pair, j) != LAST_DOWN:
                                split_lo(dve, load_down(pair, j) + SPLIT)

            step = [0]

            def next_step(ins):
                step[0] += 1
                ins.then_inc(r_v, 1)
                dve.wait_ge(r_v, step[0])

            def rt(name, n): return route[:, R[name]:R[name] + n]
            def by(name, n=EXPERTS): return rt(name, 2 * n).rearrange("p (c e) -> p c e", c=2)
            def wide(a): return a.unsqueeze(2).to_broadcast([P, 2, EXPERTS])

            index = const("index").rearrange("p (c e) -> p c e", c=2)
            dve.wait_ge(*done("logits"))
            dve.tensor_copy(rt("logits", 16), bank("logits")[:, 0:16]).then_inc(taken_of("logits"), 1)
            dve.wait_ge(*gone("logits"))
            for n, src in enumerate(("logits", "rest")):
                next_step(dve.tensor_reduce(rt(f"max{n}", 2), by(src), AX.X, ALU.max))
                next_step(dve.tensor_tensor(by("tmp"), by(src), wide(rt(f"max{n}", 2)), ALU.is_equal))
                next_step(dve.scalar_tensor_tensor(out=rt("tmp", 16), in0=rt("tmp", 16), scalar=-float(EXPERTS), in1=const("index"),
                                                   op0=ALU.mult, op1=ALU.add))
                next_step(dve.tensor_reduce(rt("first", 2), by("tmp"), AX.X, ALU.min))
                next_step(dve.tensor_scalar(rt("first", 2), rt("first", 2), float(EXPERTS), None, ALU.add))
                next_step(dve.tensor_tensor(by(f"hot{n}"), index, wide(rt("first", 2)), ALU.is_equal))
                if n == 0:
                    next_step(dve.scalar_tensor_tensor(out=rt("rest", 16), in0=rt("hot0", 16), scalar=-3e38, in1=rt("logits", 16),
                                                       op0=ALU.mult, op1=ALU.add))
            next_step(dve.tensor_tensor(rt("d", 2), rt("max1", 2), rt("max0", 2), ALU.subtract))
            assert step[0] == R_EXP
            next_step(dve.tensor_tensor(rt("mask", 16), rt("hot0", 16), rt("hot1", 16), ALU.add))
            assert step[0] == R_MASK
            for j in range(4):
                a = slice(FC * (j % 2), FC * (j % 2) + FC)
                dve.wait_ge(tok_a, j + 1)
                dve.tensor_tensor(hn_lo[:, j // 2, a], bank("hn_tok", j), hn_hi[:, j // 2, a].bitcast(F32), ALU.subtract)\
                    .then_inc(taken_of("hn_tok", j), 1)
            dve.wait_ge(r_a, 1)
            next_step(dve.tensor_scalar(rt("w0", 2), rt("e", 2), 1.0, None, ALU.add))
            next_step(dve.reciprocal(rt("w0", 2), rt("w0", 2)))
            next_step(dve.tensor_tensor(rt("w1", 2), rt("e", 2), rt("w0", 2), ALU.mult))
            next_step(dve.tensor_tensor(by("hot0"), by("hot0"), wide(rt("w0", 2)), ALU.mult))
            next_step(dve.tensor_tensor(by("hot1"), by("hot1"), wide(rt("w1", 2)), ALU.mult))
            gates, places = by("gates", ITEMS), by("places", ITEMS + 1)
            next_step(dve.memset(places[:, :, ITEMS:ITEMS + 1], -1.0))
            next_step(dve.tensor_tensor(gates[:, :, 0:EXPERTS], by("hot0"), by("hot1"), ALU.add))
            dve.wait_ge(*done("pos"))
            dve.tensor_tensor(rt("tmp", 16), bank("pos")[:, 0:16], rt("mask", 16), ALU.mult).then_inc(taken_of("pos"), 1)
            dve.wait_ge(*gone("pos"))
            next_step(dve.tensor_scalar(places[:, :, 0:EXPERTS], by("tmp"), -1.0, None, ALU.add))
            def choose(i):
                for c in range(2):
                    dve.tensor_scalar(sel[:, c, :], const("iota"), places[:, c, bass.ds(i, 1)], None, ALU.is_equal).then_inc(sel_v, 1)

            def tokens(i):
                for j in range(2):
                    dve.wait_ge(*done_i(i, "xg", 2 + j))
                    dve.tensor_copy(x_lo[:, FC * j:FC * j + FC], bank("xg", 2 + j)).then_inc(taken_of("xg", 2 + j), 1)

            def back(i, js):
                for j in js:
                    c, half = j // 2, j % 2
                    hs = h_tok[:, c, FC * half:FC * half + FC]
                    dve.wait_ge(*done_i(i, "back", j, before=1))
                    dve.scalar_tensor_tensor(out=hs, in0=bank("back", j), scalar=gates[:, c, bass.ds(i - 1, 1)], in1=hs,
                                             op0=ALU.mult, op1=ALU.add).then_inc(taken_of("back", j), 1)

            def item(i, first):
                def second_part(dst, src, step, *name):
                    dve.wait_ge(part_a, PA * i + step)
                    dve.tensor_tensor(dst, bank(*name), src.bitcast(F32), ALU.subtract).then_inc(taken_of(*name), 1)

                if not first:
                    split_lo_i(dve, i, SPLIT - 1)
                for n, (w, c, j) in enumerate(ITEM):
                    if n in BACK and not first:
                        back(i, BACK[n])
                    if n == SEL_TURN:
                        dve.wait_ge(*done_i(i, "selT"))
                        dve.tensor_copy(flat(selT), bank("selT")[:, 0:256]).then_inc(taken_of("selT"), 1)
                    if (w, j) == ("u", 1):
                        dve.wait_ge(*done_i(i, "u", c))
                        dve.wait_ge(*gone_i(i, "g", c))
                        if c >= 2:
                            dve.wait_ge(*done_i(i, "aT", c - 2))
                        dve.tensor_tensor(act_sb[:, c % 2, :], sg[:, c % 2, :], bank("u", c), ALU.mult).then_inc(taken_of("u", c), 1)
                        if c == NFC - 1:
                            choose(i + 1)
                    turned = turned_after(w, c, j)
                    if turned is not None:
                        second_part(act_lo[:, turned % 2, :], act_hi[:, turned % 2, :], turned + 1, "aT", turned)
                        if turned == NFC - 1:
                            tokens(i + 1)
                    if n + SPLIT < PER_EXPERT:
                        split_lo_i(dve, i, n + SPLIT)
                if first:
                    for n in range(SPLIT - 1):
                        split_lo_i(dve, i, PER_EXPERT + n)
                else:
                    with dve.If(i + 1 < n_items):
                        for n in range(SPLIT - 1):
                            split_lo_i(dve, i, PER_EXPERT + n)
                for half in range(2):
                    hs = slice(FC * half, FC * half + FC)
                    second_part(y_lo[:, hs], y_hi[:, hs], PA_Y + half + 1, "y", half)

            choose(0)
            dve.wait_ge(*done("count"))
            dve.tensor_scalar(rt("over", 8), bank("count")[:, 0:8], P + 0.5, None, ALU.is_gt).then_inc(taken_of("count"), 1)
            dve.wait_ge(*gone("count"))
            next_step(dve.tensor_tensor(rt("tmp64", 64).rearrange("p (a b) -> p a b", a=8), const("before").rearrange("p (a b) -> p a b", a=8),
                                        rt("over", 8).unsqueeze(1).to_broadcast([P, 8, 8]), ALU.mult))
            next_step(dve.tensor_reduce(rt("rank", 8), rt("tmp64", 64).rearrange("p (a b) -> p a b", a=8), AX.X, ALU.add))
            for n in range(OVER):
                pick = rt("pick", 8)
                next_step(dve.scalar_tensor_tensor(out=pick, in0=rt("rank", 8), scalar=float(n), in1=rt("over", 8),
                                                   op0=ALU.is_equal, op1=ALU.mult))
                for c in range(2):
                    next_step(dve.tensor_tensor_reduce(rt("tmp64", 8), gates[:, c, 0:EXPERTS], pick, 1.0, 0.0, ALU.mult, ALU.add,
                                                       gates[:, c, EXPERTS + n:EXPERTS + n + 1]))
                    next_step(dve.tensor_tensor_reduce(rt("tmp64", 8), places[:, c, 0:EXPERTS], pick, 1.0, 0.0, ALU.mult, ALU.add,
                                                       places[:, c, EXPERTS + n:EXPERTS + n + 1]))
                next_step(dve.tensor_tensor_reduce(rt("tmp64", 8), const("index")[:, 0:8], pick, 1.0, 0.0, ALU.mult, ALU.add,
                                                   rt("ctl", 4)[:, 1 + n:2 + n]))
            next_step(dve.tensor_scalar(places[:, :, EXPERTS:ITEMS], places[:, :, EXPERTS:ITEMS], -float(P), None, ALU.add))
            next_step(dve.tensor_reduce(rt("ctl", 1), rt("over", 8), AX.X, ALU.add))
            next_step(dve.tensor_scalar(rt("ctl", 1), rt("ctl", 1), float(EXPERTS), None, ALU.add))
            next_step(dve.tensor_copy(ctl[:, :], rt("ctl", 4)[0:1, :]))
            assert step[0] == N_ROUTE, step[0]

            tokens(0)
            item(0, True)
            n_items = dve.value_load(ctl[0:1, 0:1], min_val=EXPERTS, max_val=ITEMS)
            with dve.Fori(1, ITEMS) as i:
                with dve.If(i < n_items):
                    item(i, False)
            back(n_items, range(4))
            dve.wait_ge(fin_a, 2)
            dve.tensor_scalar(st2[:, 0, 0:2], den[:, 0, 0:2], 1.0 / D, EPS, ALU.mult, ALU.add).then_inc(fin_v, 1)
            dve.wait_ge(fin_p, 1)
            dve.wait_ge(gain_in, 16)
            for c in range(2):
                dve.scalar_tensor_tensor(out=out_sb[:, c, :], in0=h_tok[:, c, :], scalar=st3[:, 0, c:c + 1], in1=fgain,
                                         op0=ALU.mult, op1=ALU.mult).then_inc(fin_v, 1)

        @block.gpsimd
        def _(pool):
            pool.memset(half_neg[:, 0:12], -0.5).then_inc(filled, 1)
            pool.memset(half_neg[:, 12:13], 1.0).then_inc(filled, 1)
            pool.wait_ge(filled, 2)
            for li in range(LAYERS):
                pool.wait_ge(*gone("cvar", li))
                pool.tensor_tensor(c3, c2, half_neg[:, 0:6], ALU.pow).then_inc(c_p, 1)
                for n, kind in enumerate(NORMS):
                    pool.wait_ge(*gone("var", li, kind))
                    pool.tensor_tensor(st3[:, n, :], st2[:, n, :], half_neg[:, 0:12], ALU.pow).then_inc(root_p, 1)
            pool.wait_ge(fin_v, 1)
            pool.tensor_tensor(st3[:, 0, 0:2], st2[:, 0, 0:2], half_neg[:, 0:2], ALU.pow).then_inc(fin_p, 1)


PARAMS, _at = {}, 0
for _name, _n in (("wuq0", H * MLA_DK), ("wuq1", H * MLA_DK), ("wukv", H * 2 * DV), ("wgate", P), ("bgate", P), ("dlam", 4 * DIFF_DK)):
    PARAMS[_name] = (_at, _n)
    _at += _n
N_PARAMS = _at
LAM_INIT = [0.8 - 0.6 * float(np.exp(-0.3 * li)) for li in range(LAYERS)]
R_EXP, R_MASK, N_ROUTE = 14, 15, 47
R, _at = {}, 0
for _name, _n in (("logits", 16), ("rest", 16), ("tmp", 16), ("max0", 2), ("max1", 2), ("first", 2), ("hot0", 16), ("hot1", 16),
                  ("d", 2), ("e", 2), ("w0", 2), ("w1", 2), ("mask", 16), ("gates", 2 * ITEMS), ("places", 2 * ITEMS + 2),
                  ("over", 8), ("rank", 8), ("pick", 8), ("tmp64", 64), ("ctl", 4)):
    R[_name] = _at
    _at += _n


def kernel(x, meta_tokens, attn_norm, w_in, gla_w_gate, gla_b_gate, gla_norm, ret_norm, mla_q_norm, mla_w_uq, mla_kv_norm,
           mla_w_ukv, diff_lambda, diff_norm, w_out, ffn_norm, ffn_w_gate, ffn_w_up, ffn_w_down, moe_router, moe_w_gate,
           moe_w_up, moe_w_down, final_norm):
    import concourse.bacc as _bacc
    from concourse.bass_utils import run_bass_kernel_spmd as _run

    x, meta_tokens, moe_router = np.asarray(x), np.asarray(meta_tokens), np.asarray(moe_router)
    stream = np.concatenate([meta_tokens, x[0]], axis=0)
    x_t = stream.T.reshape(KD, P, T).transpose(1, 0, 2)
    cols_t = np.zeros((P, 48), np.float32)
    for a, at in ((attn_norm, 0), (ffn_norm, 16)):
        cols_t[:, at:at + LAYERS * KD] = np.asarray(a).reshape(LAYERS * KD, P).T
    q_norm = np.asarray(mla_q_norm)
    cols_t[:, 32:34] = q_norm[:, 0:P].T
    cols_t[:, 34:36] = np.concatenate([q_norm[:, P:Q_RANK], np.asarray(mla_kv_norm)], axis=1).T
    for a, at in ((gla_norm, 36), (ret_norm, 38), (diff_norm, 40)):
        cols_t[:, at:at + LAYERS] = np.tile(np.asarray(a), (1, 2)).T
    params_t = np.zeros((LAYERS, P, N_PARAMS), np.float32)
    w_uq = np.asarray(mla_w_uq)
    for name, rows, a in (("wuq0", slice(0, P), w_uq[:, 0:P]), ("wuq1", slice(0, Q_RANK - P), w_uq[:, P:Q_RANK]),
                          ("wukv", slice(P - 64, P), np.asarray(mla_w_ukv)), ("wgate", slice(0, 16), np.asarray(gla_w_gate)),
                          ("bgate", slice(0, P), np.asarray(gla_b_gate)[:, None, :]),
                          ("dlam", slice(0, P), np.asarray(diff_lambda).reshape(LAYERS, 1, -1))):
        at, n = PARAMS[name]
        params_t[:, rows, at:at + n] = a
    router_t = moe_router[0].reshape(KD, P, EXPERTS).transpose(1, 0, 2)

    nc = _bacc.Bacc("TRN2", target_bir_lowering=False, num_devices=1, dynamic_dma_scratch_size=1024)
    table, const_at = constants()
    arrays, args = {}, []
    for name, a in (("w_in", w_in), ("w_out", w_out), ("ffn_w_gate", ffn_w_gate), ("ffn_w_up", ffn_w_up),
                    ("ffn_w_down", ffn_w_down), ("moe_w_gate", moe_w_gate), ("moe_w_up", moe_w_up),
                    ("moe_w_down", moe_w_down), ("final_norm", final_norm), ("x_t", x_t), ("cols_t", cols_t),
                    ("params_t", params_t), ("router_t", router_t), ("consts", table)):
        a = np.ascontiguousarray(a)
        arrays[f"in_{name}_dram"] = a
        args.append(nc.dram_tensor(f"in_{name}_dram", a.shape, mybir.dt.from_np(a.dtype), kind="ExternalInput").ap())
    args.append(nc.dram_tensor("out_0_dram", (1, SEQ, D), F32, kind="ExternalOutput").ap())
    hybrid_trunk(nc, *args, const_at)
    r = _run(nc, [arrays], core_ids=[0])
    return r.results[0]["out_0_dram"]
```
